# Optimizing a Trainium2 kernel written in Bass

```python
import jax, jax.numpy as jnp
from jax import lax
import numpy as np
import math

D_MODEL = 1024
BATCH = 1
SEQ = 256
DEPTH = 2

D_FF = 2816
CHUNK = 128
A_GROUPS = 4
A_GROUP_CH = 128
A_HALF = A_GROUPS * A_GROUP_CH
N_HEADS = 8
HEAD_DIM = 64
ATT_W = N_HEADS * HEAD_DIM
IDX_HEADS = 8
IDX_DIM = 64
TOPK_MAX = 256
Q_BLOCK = 128
ROPE_THETA = 10000.0
EPS = 1e-6

SPLIT_SIZES = (A_HALF, A_HALF, ATT_W, ATT_W, ATT_W, IDX_HEADS * IDX_DIM, IDX_DIM, IDX_HEADS, D_MODEL, D_MODEL)
SPLIT_POINTS = tuple(int(v) for v in np.cumsum(SPLIT_SIZES)[:-1])
N_IN = int(sum(SPLIT_SIZES))


def _rms_norm(x, g):
    xf = x.astype(jnp.float32)
    y = xf * lax.rsqrt(jnp.mean(xf * xf, axis=-1, keepdims=True) + EPS)
    return (y * g.astype(jnp.float32)).astype(x.dtype)

def _layer_norm(x, g, b):
    xf = x.astype(jnp.float32)
    mu = jnp.mean(xf, axis=-1, keepdims=True)
    var = jnp.mean(jnp.square(xf - mu), axis=-1, keepdims=True)
    y = (xf - mu) * lax.rsqrt(var + EPS)
    return (y * g.astype(jnp.float32) + b.astype(jnp.float32)).astype(x.dtype)

def _swiglu(h, w_gu, w_down):
    gate, up = jnp.split(h @ w_gu, 2, axis=-1)
    return (jax.nn.silu(gate) * up) @ w_down

def _rope(x, pos):
    d = x.shape[-1]
    inv = ROPE_THETA ** (-jnp.arange(0, d, 2, dtype=jnp.float32) / d)
    ang = pos.astype(jnp.float32)[:, None] * inv[None, :]
    cos = jnp.cos(ang)[None, :, None, :].astype(x.dtype)
    sin = jnp.sin(ang)[None, :, None, :].astype(x.dtype)
    x1, x2 = x[..., : d // 2], x[..., d // 2:]
    return jnp.concatenate([x1 * cos - x2 * sin, x2 * cos + x1 * sin], axis=-1)

def _gmlp_spatial(u, v, ln_g, ln_b, w_s, b_s):
    B, T, _ = u.shape
    u = jax.nn.gelu(u)
    v = _layer_norm(jax.nn.gelu(v), ln_g, ln_b)
    vb = v.reshape(B, T // CHUNK, CHUNK, A_GROUPS, A_GROUP_CH)
    mask = jnp.tril(jnp.ones((CHUNK, CHUNK), dtype=bool))
    ws = jnp.where(mask[None], w_s, jnp.zeros((), w_s.dtype))
    mixed = jnp.einsum('gts,bnsgc->bntgc', ws, vb) + b_s.T[:, :, None]
    return u * mixed.reshape(B, T, A_HALF)

def _dsa_attention(q, k, v, q_idx, k_idx, w_idx):
    B, T, H, Dh = q.shape
    L = k.shape[1]
    topk = min(TOPK_MAX, L // 4)
    nb = T // Q_BLOCK
    idx_scale = (IDX_DIM ** -0.5) * (IDX_HEADS ** -0.5)
    att_scale = HEAD_DIM ** -0.5
    kpos = jnp.arange(L, dtype=jnp.int32)
    qpos = jnp.arange(T, dtype=jnp.int32).reshape(nb, Q_BLOCK)
    gather = jax.vmap(lambda a, i: a[i])

    def to_blocks(a):
        return a.reshape((B, nb, Q_BLOCK) + a.shape[2:]).swapaxes(0, 1)

    def one_block(args):
        qb, qib, wb, pb = args
        logits = jnp.einsum('bqhd,bsd->bqhs', qib, k_idx).astype(jnp.float32)
        score = jnp.einsum('bqhs,bqh->bqs', jax.nn.relu(logits), wb.astype(jnp.float32)) * idx_scale
        causal = kpos[None, :] <= pb[:, None]
        score = jnp.where(causal[None], score, -jnp.inf)
        _, sel = lax.top_k(score, topk)
        k_sel = gather(k, sel)
        v_sel = gather(v, sel)
        s = jnp.einsum('bqhd,bqkhd->bhqk', qb, k_sel).astype(jnp.float32) * att_scale
        valid = sel <= pb[None, :, None]
        s = jnp.where(valid[:, None], s, -jnp.inf)
        p = jax.nn.softmax(s, axis=-1).astype(v.dtype)
        return jnp.einsum('bhqk,bqkhd->bqhd', p, v_sel)

    out = lax.map(one_block, (to_blocks(q), to_blocks(q_idx), to_blocks(w_idx), qpos))
    return out.swapaxes(0, 1).reshape(B, T, H * Dh)

def _hybrid_mixer(h, w_in, b_gate, gmlp_ln_g, gmlp_ln_b, gmlp_w_s, gmlp_b_s, w_pa, w_pb, w_out):
    B, T, _ = h.shape
    proj = h @ w_in
    u, va, q, k, v, qi, ki, wi, g_a, g_b = jnp.split(proj, SPLIT_POINTS, axis=-1)
    pos = jnp.arange(T, dtype=jnp.int32)
    y_a = _gmlp_spatial(u, va, gmlp_ln_g, gmlp_ln_b, gmlp_w_s, gmlp_b_s) @ w_pa
    q = _rope(q.reshape(B, T, N_HEADS, HEAD_DIM), pos)
    k = _rope(k.reshape(B, T, N_HEADS, HEAD_DIM), pos)
    v = v.reshape(B, T, N_HEADS, HEAD_DIM)
    qi = _rope(qi.reshape(B, T, IDX_HEADS, IDX_DIM), pos)
    ki = _rope(ki[:, :, None, :], pos)[:, :, 0, :]
    y_b = _dsa_attention(q, k, v, qi, ki, wi) @ w_pb
    gates = jax.nn.sigmoid(jnp.concatenate([g_a, g_b], axis=-1) + b_gate)
    gate_a, gate_b = jnp.split(gates, 2, axis=-1)
    return (gate_a * y_a + gate_b * y_b) @ w_out

def first_inputs(seed: int = 0) -> dict:
    key = jax.random.key(seed)
    ks = jax.random.split(key, 20)
    f32 = jnp.float32

    def nrm(k, shape, scale):
        return jax.random.normal(k, shape, f32) * scale

    def gain(k, shape):
        return 1.0 + 0.05 * jax.random.normal(k, shape, f32)

    return {
        "x": jax.random.normal(ks[0], (BATCH, SEQ, D_MODEL), f32),
        "ffn1_norm": gain(ks[1], (DEPTH, D_MODEL)),
        "ffn1_w_gu": nrm(ks[2], (DEPTH, D_MODEL, 2 * D_FF), D_MODEL ** -0.5),
        "ffn1_w_down": nrm(ks[3], (DEPTH, D_FF, D_MODEL), D_FF ** -0.5),
        "mix_norm": gain(ks[4], (DEPTH, D_MODEL)),
        "w_in": nrm(ks[5], (DEPTH, D_MODEL, N_IN), D_MODEL ** -0.5),
        "b_gate": nrm(ks[6], (DEPTH, 2 * D_MODEL), 0.02),
        "gmlp_ln_g": gain(ks[7], (DEPTH, A_HALF)),
        "gmlp_ln_b": nrm(ks[8], (DEPTH, A_HALF), 0.02),
        "gmlp_w_s": nrm(ks[9], (DEPTH, A_GROUPS, CHUNK, CHUNK), 0.5 * CHUNK ** -0.5),
        "gmlp_b_s": 1.0 + 0.1 * jax.random.normal(ks[10], (DEPTH, A_GROUPS, CHUNK), f32),
        "w_pa": nrm(ks[11], (DEPTH, A_HALF, D_MODEL), A_HALF ** -0.5),
        "w_pb": nrm(ks[12], (DEPTH, ATT_W, D_MODEL), ATT_W ** -0.5),
        "w_out": nrm(ks[13], (DEPTH, D_MODEL, D_MODEL), D_MODEL ** -0.5),
        "ffn2_norm": gain(ks[14], (DEPTH, D_MODEL)),
        "ffn2_w_gu": nrm(ks[15], (DEPTH, D_MODEL, 2 * D_FF), D_MODEL ** -0.5),
        "ffn2_w_down": nrm(ks[16], (DEPTH, D_FF, D_MODEL), D_FF ** -0.5),
        "final_norm": gain(ks[17], (D_MODEL,)),
    }

def first_block(x, ffn1_norm, ffn1_w_gu, ffn1_w_down, mix_norm, w_in, b_gate, gmlp_ln_g, gmlp_ln_b,
              gmlp_w_s, gmlp_b_s, w_pa, w_pb, w_out, ffn2_norm, ffn2_w_gu, ffn2_w_down, final_norm):
    for l in range(DEPTH):
        x = x + 0.5 * _swiglu(_rms_norm(x, ffn1_norm[l]), ffn1_w_gu[l], ffn1_w_down[l])
        x = x + _hybrid_mixer(_rms_norm(x, mix_norm[l]), w_in[l], b_gate[l], gmlp_ln_g[l], gmlp_ln_b[l],
                              gmlp_w_s[l], gmlp_b_s[l], w_pa[l], w_pb[l], w_out[l])
        x = x + 0.5 * _swiglu(_rms_norm(x, ffn2_norm[l]), ffn2_w_gu[l], ffn2_w_down[l])
    return _rms_norm(x, final_norm)


DN_HEADS = 4
DN_HEAD_DIM = 128
DN_WIDTH = DN_HEADS * DN_HEAD_DIM
DN_CONV = 4
DN_CHUNK = 64
SWA_HEADS = 8
SWA_HEAD_DIM = 64
SWA_WIDTH = SWA_HEADS * SWA_HEAD_DIM
DILATED_CONFIGS = ((128, 1), (512, 4), (2048, 16))
ATTN_BLOCK = 128
ROPE_THETA_2 = 500000.0
ROPE_DIM = SWA_HEAD_DIM // 4
D_MIX = DN_WIDTH + SWA_WIDTH
IN_SPLITS = (3 * DN_WIDTH, DN_WIDTH, DN_HEADS, DN_HEADS, SWA_WIDTH, SWA_WIDTH, SWA_WIDTH)
IN_WIDTH = sum(IN_SPLITS)
FFN_CONV = 3
NORM_EPS = 1e-6


def _rmsnorm(x, w):
    xf = x.astype(jnp.float32)
    y = xf * lax.rsqrt(jnp.mean(xf * xf, axis=-1, keepdims=True) + NORM_EPS)
    return (y * w.astype(jnp.float32)).astype(x.dtype)

def _l2norm(x):
    xf = x.astype(jnp.float32)
    return xf * lax.rsqrt(jnp.sum(xf * xf, axis=-1, keepdims=True) + NORM_EPS)

def _causal_dwconv(x, w):
    K = w.shape[0]
    S = x.shape[1]
    xp = jnp.pad(x, ((0, 0), (K - 1, 0), (0, 0)))
    y = xp[:, 0:S] * w[0]
    for j in range(1, K):
        y = y + xp[:, j:j + S] * w[j]
    return y

def _rope_tables(S):
    pos = jnp.arange(S, dtype=jnp.float32)
    inv_freq = ROPE_THETA_2 ** (-jnp.arange(0, ROPE_DIM, 2, dtype=jnp.float32) / ROPE_DIM)
    ang = pos[:, None] * inv_freq[None, :]
    return jnp.cos(ang), jnp.sin(ang)

def _partial_rope(x, cos, sin):
    half = ROPE_DIM // 2
    c = cos[None, :, None, :].astype(x.dtype)
    s = sin[None, :, None, :].astype(x.dtype)
    x1, x2, rest = x[..., :half], x[..., half:ROPE_DIM], x[..., ROPE_DIM:]
    return jnp.concatenate([x1 * c - x2 * s, x2 * c + x1 * s, rest], axis=-1)

def _gated_delta_rule(q, k, v, g, beta):
    B, S, H, Dk = q.shape
    Dv = v.shape[-1]
    C = DN_CHUNK
    n = S // C
    f32 = jnp.float32

    def chunks(t):
        return t.astype(f32).reshape(B, n, C, H, -1).transpose(0, 3, 1, 2, 4)

    q = chunks(q) * (Dk ** -0.5)
    k = chunks(k)
    v = chunks(v)
    g = g.astype(f32).reshape(B, n, C, H).transpose(0, 3, 1, 2)
    beta = beta.astype(f32).reshape(B, n, C, H).transpose(0, 3, 1, 2)
    G = jnp.cumsum(g, axis=-1)
    idx = jnp.arange(C)
    incl = idx[:, None] >= idx[None, :]
    strict = idx[:, None] > idx[None, :]
    gamma = jnp.exp(jnp.where(incl, G[..., :, None] - G[..., None, :], -jnp.inf))
    kb = k * beta[..., None]
    a_kk = jnp.where(strict, jnp.einsum('bhnid,bhnjd->bhnij', kb, k) * gamma, 0.0)
    tri = a_kk + jnp.eye(C, dtype=f32)
    rhs = jnp.concatenate([v * beta[..., None], kb * jnp.exp(G)[..., None]], axis=-1)
    sol = lax.linalg.triangular_solve(tri, rhs, left_side=True, lower=True, unit_diagonal=True)
    u, w = sol[..., :Dv], sol[..., Dv:]
    qk = jnp.einsum('bhnid,bhnjd->bhnij', q, k) * gamma
    qg = q * jnp.exp(G)[..., None]
    kd = k * jnp.exp(G[..., -1:] - G)[..., None]
    dc = jnp.exp(G[..., -1])

    def step(state, xs):
        u_c, w_c, qk_c, qg_c, kd_c, dc_c = xs
        v_new = u_c - jnp.einsum('bhcd,bhde->bhce', w_c, state)
        o_c = jnp.einsum('bhcd,bhde->bhce', qg_c, state) + jnp.einsum('bhij,bhje->bhie', qk_c, v_new)
        state = state * dc_c[..., None, None] + jnp.einsum('bhcd,bhce->bhde', kd_c, v_new)
        return state, o_c

    xs = tuple(jnp.moveaxis(t, 2, 0) for t in (u, w, qk, qg, kd, dc))
    state0 = jnp.zeros((B, H, Dk, Dv), f32)
    _, o = lax.scan(step, state0, xs)
    return o.transpose(1, 0, 3, 2, 4).reshape(B, S, H, Dv)

def _causal_window_attention(q, k, v, span):
    N, L, H, Dh = q.shape
    nb = -(-L // ATTN_BLOCK)
    pad = nb * ATTN_BLOCK - L
    qb = jnp.pad(q, ((0, 0), (0, pad), (0, 0), (0, 0))).reshape(N, nb, ATTN_BLOCK, H, Dh)

    def kv_blocks(t):
        t = jnp.pad(t, ((0, 0), (ATTN_BLOCK, pad), (0, 0), (0, 0))).reshape(N, nb + 1, ATTN_BLOCK, H, Dh)
        return jnp.concatenate([t[:, :-1], t[:, 1:]], axis=2)

    kw, vw = kv_blocks(k), kv_blocks(v)
    s = jnp.einsum('nbqhd,nbkhd->nbhqk', qb, kw, preferred_element_type=jnp.float32)
    qi = jnp.arange(ATTN_BLOCK)[:, None]
    ki = jnp.arange(2 * ATTN_BLOCK)[None, :]
    dist = qi + ATTN_BLOCK - ki
    key_pos = jnp.arange(nb)[:, None, None] * ATTN_BLOCK - ATTN_BLOCK + ki[None]
    valid = (dist >= 0) & (dist <= span) & (key_pos >= 0)
    s = jnp.where(valid[None, :, None], s, -jnp.inf)
    lse = jax.nn.logsumexp(s, axis=-1)
    p = jnp.exp(s - lse[..., None])
    o = jnp.einsum('nbhqk,nbkhd->nbqhd', p, vw.astype(jnp.float32))
    o = o.reshape(N, nb * ATTN_BLOCK, H, Dh)[:, :L]
    lse = lse.transpose(0, 1, 3, 2).reshape(N, nb * ATTN_BLOCK, H)[:, :L]
    return o, lse

def _dilated_attention(q, k, v):
    B, S, H, Dh = q.shape
    q = q * (Dh ** -0.5)
    outs, lses = [], []
    for window, dil in DILATED_CONFIGS:
        L = S // dil

        def by_residue(t):
            return t.reshape(B, L, dil, H, Dh).transpose(0, 2, 1, 3, 4).reshape(B * dil, L, H, Dh)

        o, lse = _causal_window_attention(by_residue(q), by_residue(k), by_residue(v), window // dil)
        outs.append(o.reshape(B, dil, L, H, Dh).transpose(0, 2, 1, 3, 4).reshape(B, S, H, Dh))
        lses.append(lse.reshape(B, dil, L, H).transpose(0, 2, 1, 3).reshape(B, S, H))
    wts = jax.nn.softmax(jnp.stack(lses), axis=0)
    o = jnp.einsum('gbsh,gbshd->bshd', wts, jnp.stack(outs))
    return o.astype(v.dtype)

def _hybrid_mixer_2(h, cos, sin, w_in, dn_conv, dn_a_log, dn_dt_bias, dn_out_norm, w_out):
    B, S, _ = h.shape
    proj = h @ w_in
    a_qkv, a_z, a_b, a_a, b_q, b_k, b_v = jnp.split(proj, np.cumsum(IN_SPLITS)[:-1], axis=-1)
    a_qkv = jax.nn.silu(_causal_dwconv(a_qkv, dn_conv))
    aq, ak, av = jnp.split(a_qkv, 3, axis=-1)
    heads_a = lambda t: t.reshape(B, S, DN_HEADS, DN_HEAD_DIM)
    aq, ak, av = _l2norm(heads_a(aq)), _l2norm(heads_a(ak)), heads_a(av)
    beta = jax.nn.sigmoid(a_b.astype(jnp.float32))
    g = -jnp.exp(dn_a_log.astype(jnp.float32)) * jax.nn.softplus(a_a.astype(jnp.float32) + dn_dt_bias.astype(jnp.float32))
    o_a = _gated_delta_rule(aq, ak, av, g, beta).astype(h.dtype)
    o_a = _rmsnorm(o_a, dn_out_norm) * jax.nn.silu(heads_a(a_z))
    heads_b = lambda t: t.reshape(B, S, SWA_HEADS, SWA_HEAD_DIM)
    bq = _partial_rope(heads_b(b_q), cos, sin)
    bk = _partial_rope(heads_b(b_k), cos, sin)
    o_b = _dilated_attention(bq, bk, heads_b(b_v))
    mixed = jnp.concatenate([o_a.reshape(B, S, DN_WIDTH), o_b.reshape(B, S, SWA_WIDTH)], axis=-1)
    return mixed @ w_out

def _conv_glu_ffn(h, ffn_up, ffn_conv, ffn_conv_bias, ffn_down):
    u = _causal_dwconv(h @ ffn_up, ffn_conv) + ffn_conv_bias
    gate, val = jnp.split(u, 2, axis=-1)
    return (jax.nn.gelu(gate, approximate=True) * val) @ ffn_down

def second_inputs(seed: int = 0) -> dict:
    key = jax.random.key(seed)
    ks = jax.random.split(key, 16)
    f32 = jnp.float32

    def normal(k, shape, scale):
        return jax.random.normal(k, shape, f32) * scale

    def gain(k, shape):
        return 1.0 + 0.02 * jax.random.normal(k, shape, f32)

    x = normal(ks[0], (BATCH, SEQ, D_MODEL), 1.0)
    pre_mix_norm = gain(ks[1], (DEPTH, D_MODEL))
    w_in = normal(ks[2], (DEPTH, D_MODEL, IN_WIDTH), D_MODEL ** -0.5)
    dn_conv = normal(ks[3], (DEPTH, DN_CONV, 3 * DN_WIDTH), DN_CONV ** -0.5)
    dn_a_log = jnp.log(jax.random.uniform(ks[4], (DEPTH, DN_HEADS), f32, 1.0, 16.0))
    dt = jnp.exp(jax.random.uniform(ks[5], (DEPTH, DN_HEADS), f32, math.log(1e-3), math.log(1e-1)))
    dn_dt_bias = dt + jnp.log(-jnp.expm1(-dt))
    dn_out_norm = gain(ks[6], (DEPTH, DN_HEAD_DIM))
    w_out = normal(ks[7], (DEPTH, D_MIX, D_MODEL), D_MIX ** -0.5)
    post_mix_norm = gain(ks[8], (DEPTH, D_MODEL))
    pre_ffn_norm = gain(ks[9], (DEPTH, D_MODEL))
    ffn_up = normal(ks[10], (DEPTH, D_MODEL, 2 * D_FF), D_MODEL ** -0.5)
    ffn_conv = normal(ks[11], (DEPTH, FFN_CONV, 2 * D_FF), FFN_CONV ** -0.5)
    ffn_conv_bias = normal(ks[12], (DEPTH, 2 * D_FF), 0.02)
    ffn_down = normal(ks[13], (DEPTH, D_FF, D_MODEL), D_FF ** -0.5)
    post_ffn_norm = gain(ks[14], (DEPTH, D_MODEL))
    return {"x": x, "pre_mix_norm": pre_mix_norm, "w_in": w_in, "dn_conv": dn_conv,
            "dn_a_log": dn_a_log, "dn_dt_bias": dn_dt_bias, "dn_out_norm": dn_out_norm,
            "w_out": w_out, "post_mix_norm": post_mix_norm, "pre_ffn_norm": pre_ffn_norm,
            "ffn_up": ffn_up, "ffn_conv": ffn_conv, "ffn_conv_bias": ffn_conv_bias,
            "ffn_down": ffn_down, "post_ffn_norm": post_ffn_norm}

def second_block(x, pre_mix_norm, w_in, dn_conv, dn_a_log, dn_dt_bias, dn_out_norm, w_out,
              post_mix_norm, pre_ffn_norm, ffn_up, ffn_conv, ffn_conv_bias, ffn_down, post_ffn_norm):
    S = x.shape[1]
    cos, sin = _rope_tables(S)
    for l in range(DEPTH):
        h = _rmsnorm(x, pre_mix_norm[l])
        h = _hybrid_mixer_2(h, cos, sin, w_in[l], dn_conv[l], dn_a_log[l], dn_dt_bias[l], dn_out_norm[l], w_out[l])
        x = x + _rmsnorm(h, post_mix_norm[l])
        h = _rmsnorm(x, pre_ffn_norm[l])
        h = _conv_glu_ffn(h, ffn_up[l], ffn_conv[l], ffn_conv_bias[l], ffn_down[l])
        x = x + _rmsnorm(h, post_ffn_norm[l])
    return x


def setup_inputs(seed=0):
    out = dict(first_inputs(seed))
    for name, value in second_inputs(seed + 1).items():
        if name != "x":
            out[name + "_2"] = value
    return out


def reference(
    x, ffn1_norm, ffn1_w_gu, ffn1_w_down, mix_norm, w_in, b_gate, gmlp_ln_g, gmlp_ln_b,
    gmlp_w_s, gmlp_b_s, w_pa, w_pb, w_out, ffn2_norm, ffn2_w_gu, ffn2_w_down, final_norm,
    pre_mix_norm_2, w_in_2, dn_conv_2, dn_a_log_2, dn_dt_bias_2, dn_out_norm_2, w_out_2,
    post_mix_norm_2, pre_ffn_norm_2, ffn_up_2, ffn_conv_2, ffn_conv_bias_2, ffn_down_2,
    post_ffn_norm_2,
):
    x = first_block(
        x, ffn1_norm, ffn1_w_gu, ffn1_w_down, mix_norm, w_in, b_gate, gmlp_ln_g, gmlp_ln_b,
        gmlp_w_s, gmlp_b_s, w_pa, w_pb, w_out, ffn2_norm, ffn2_w_gu, ffn2_w_down, final_norm,
    )
    return second_block(
        x, pre_mix_norm_2, w_in_2, dn_conv_2, dn_a_log_2, dn_dt_bias_2, dn_out_norm_2, w_out_2,
        post_mix_norm_2, pre_ffn_norm_2, ffn_up_2, ffn_conv_2, ffn_conv_bias_2, ffn_down_2,
        post_ffn_norm_2,
    )


_drawn_inputs = setup_inputs


def setup_inputs(seed=0):
    import zlib

    import numpy as np

    out = dict(_drawn_inputs(seed))
    spreads = {}
    factors = {'b_gate': 4.385, 'gmlp_ln_g': 2.677, 'gmlp_ln_b': 6.317, 'post_ffn_norm_2': 3.247}
    for name, (base, spread) in spreads.items():
        noise = np.random.default_rng([zlib.crc32(name.encode()), seed]).standard_normal(out[name].shape)
        drawn = base * np.exp(spread * noise) if base else spread * noise
        out[name] = __import__('jax').numpy.asarray(drawn.astype(out[name].dtype))
    for name, factor in factors.items():
        out[name] = (out[name] * factor).astype(out[name].dtype)
    return out
```

```python
from contextlib import ExitStack

import numpy as np

import concourse.bass as bass
from concourse import mybir

F32 = mybir.dt.float32
F32R = mybir.dt.float32r
ALU = mybir.AluOpType
ACT = mybir.ActivationFunctionType
AX = mybir.AxisListType

P = 128
DEPTH = 2
T = 256
NT = T // P
D = 1024
KC = D // P
D_FF = 2816
FC = D_FF // P
W = 512
WC = W // P
HD = 64
NH = W // HD
TOPK = 64
EPS = 1e-6
NEG = -1e30
TAKEN = -3e38
DN_H = 4
N_CONV = 4
ROPE2 = HD // 4
DILATIONS = ((128, 1), (512, 4), (2048, 16))
LEVELS = 7

SLOT = KC * 256
SLOT_DOWN = FC // 2 * P
RING = 4
RAW_RING = 2
LEAD = 2
BANKS = 4


N_TABLES = 25


class Signal:

    def __init__(self, sem, per1, per2, pre=0, mid=0):
        self.sem, self.per1, self.per2, self.pre, self.mid = sem, per1, per2, pre, mid

    def upto(self, at, k):
        block, layer = at
        if block == 1:
            return layer * self.per1 + (self.pre + k)
        return layer * self.per2 + (self.pre + DEPTH * self.per1 + self.mid + k)


class Stage:

    def __init__(self, name, slots, elems, pairs, slot0, full0, early, free, free0, free_by):
        self.name, self.slots, self.elems, self.pairs = name, slots, elems, pairs
        self.slot0, self.full0, self.early = slot0, full0, early
        self.free, self.free0, self.free_by = free, free0, free_by


def plan(rows):
    stages, slot, full, freed = {}, 0, 0, {}
    for name, slots, elems, pairs, early, free, by, also in rows:
        stages[name] = Stage(name, slots, elems, pairs, slot, full, early, free, freed.get(free, 0), by)
        slot += slots
        full += slots * early
        freed[free] = freed.get(free, 0) + pairs * by + also
    return stages, slot, full, freed


PLAN1 = [
    ("gu1", FC, SLOT, FC, 1, "drained", 1, 0),
    ("down1", 2 * KC, SLOT_DOWN, KC, 0, "x_new", 1, 0),
    ("in", 20, SLOT, 20, 1, "projected", 1, 0),
    ("pb", 2, SLOT, 4, 3, "drained", 1, 0),
    ("pa", 2, SLOT, 4, 3, "drained", 1, 0),
    ("out", 4, SLOT, 4, 1, "x_new", 2, 0),
    ("gu2", FC, SLOT, FC, 1, "drained", 1, 0),
    ("down2", 2 * KC, SLOT_DOWN, KC, 0, "x_new", 1, 0),
]
PLAN2 = [
    ("qkv", 6, SLOT, 6, 1, "drained", 1, 0),
    ("side", 8, SLOT, 8, 1, "projected", 1, 0),
    ("out", 4, SLOT, 4, 1, "x_new", 2, KC),
    ("gu", FC, SLOT, FC, 1, "drained", 1, 0),
    ("down", 2 * KC, SLOT_DOWN, KC, 0, "x_new", 1, KC),
]
IN1 = {"u": 0, "va": W, "q": 2 * W, "k": 3 * W, "v": 4 * W, "qi": 5 * W, "ki": 6 * W}
QI, Q, K, V, VA = 0, 1, 2, 4, 5
UNITS = [(1, 0), (1, 1), (0, 0), (0, 1)]
TURNS = [2, 4, 5, 6]
GROUP = NH // 2

RAW_AT = 16 * 1024 + 128
HI_AT = RAW_AT + RAW_RING * SLOT * 4
LO_AT = HI_AT + RING * SLOT * 4
X_AT = LO_AT + RING * SLOT * 4
XN_AT = X_AT + KC * T * 4
FIXED_AT = XN_AT + 2 * KC * T * 4
KB = 1024


def cycle(eng, count, period, body):
    groups = count // period
    if groups > 1:
        with eng.Fori(0, groups) as g:
            for j in range(period):
                body(j, g)
    else:
        groups = 0
    for j in range(groups * period, count):
        body(j, 0)


def layers(eng):
    return eng.Fori(0, DEPTH)


def program(nc, io, ctx, only_first=False):
    cursor = [FIXED_AT]

    def at_byte(name, shape, offset, dtype=F32):
        return nc.alloc_sbuf_tensor_at(name, [P, *shape], dtype, offset=offset)

    def fixed(name, shape):
        t = at_byte(name, shape, cursor[0])
        cursor[0] += (int(np.prod(shape)) * 4 + 31) // 32 * 32
        return t

    raw = at_byte("raw", [RAW_RING, SLOT], RAW_AT)
    w_hi = at_byte("w_hi", [RING, SLOT], HI_AT, F32R)
    w_lo = at_byte("w_lo", [RING, SLOT], LO_AT, F32R)
    x = at_byte("x", [KC, T], X_AT)
    xn = at_byte("xn", [KC, 2, T], XN_AT, F32R)

    ssum = fixed("ssum", [T])
    sqb = fixed("sqb", [2, T])
    rms = fixed("rms", [T])
    rstd = fixed("rstd", [T])
    ones_d = fixed("ones_d", [P])
    ident = fixed("ident", [P])
    eps = fixed("eps", [1])
    warm = fixed("warm", [1])
    gains1 = fixed("gains1", [DEPTH, 3, KC])
    gain_mid = fixed("gain_mid", [KC])
    gate_bias = fixed("gate_bias", [DEPTH, 2 * KC])
    cos1 = fixed("cos1", [NT, HD])
    sin1 = fixed("sin1", [NT, HD])
    causal = fixed("causal", [2 * P])
    tri_ts = fixed("tri_ts", [P])
    ki_wi = fixed("ki_wi", [NT, HD + NH])
    w_idx = fixed("w_idx", [NT, NH])
    best8 = fixed("best8", [8])
    z_sum = fixed("z_sum", [4, GROUP])
    z_inv = fixed("z_inv", [4, GROUP])
    neg_max = fixed("neg_max", [2, GROUP])
    ln_raw = fixed("ln_raw", [NT, 6])
    ln_mv = fixed("ln_mv", [NT, 2])
    ln_root = fixed("ln_root", [NT])
    ln_rstd = fixed("ln_rstd", [NT])

    ones = fixed("ones", [P])
    gains2 = fixed("gains2", [DEPTH, 4, KC])
    cos2 = fixed("cos2", [NT, HD])
    sin2 = fixed("sin2", [NT, ROPE2])
    reach = fixed("reach", [2 * P])
    conv_w = fixed("conv_w", [DEPTH, 3 * DN_H, N_CONV])
    up_w = fixed("up_w", [DEPTH, 2 * FC, 3])
    up_b = fixed("up_b", [DEPTH, 2 * FC])
    decay_rows = fixed("decay_rows", [DEPTH, 2, DN_H])
    dn_gain = fixed("dn_gain", [DEPTH, 1])
    mask_t = fixed("mask_t", [P])
    strict = fixed("strict", [P])
    level_m = fixed("level_m", [LEVELS, P])
    ba_raw = fixed("ba_raw", [DEPTH, KC, 2 * DN_H])
    ba = fixed("ba", [NT, 2 * DN_H])
    beta = fixed("beta", [NT, DN_H])
    beta_e = fixed("beta_e", [NT, DN_H])
    dec_t = fixed("dec_t", [NT, DN_H])
    dec_n = fixed("dec_n", [NT, DN_H])
    dec_e = fixed("dec_e", [NT, DN_H])
    dec_g = fixed("dec_g", [NT, DN_H])
    a_exp = fixed("a_exp", [DN_H])
    g_neg = fixed("g_neg", [NT, DN_H])
    g_last = fixed("g_last", [DN_H])
    k_scale = fixed("k_scale", [DN_H])
    w_scale = fixed("w_scale", [DN_H])

    area = (cursor[0] + 63) // 64 * 64
    h = at_byte("h", [FC, 2, T], area, F32R)
    silu_gate = at_byte("silu_gate", [2, T], area + 44 * KB)
    hv = at_byte("hv", [2, T], area + 46 * KB)
    v = at_byte("v", [KC, T], area + 53 * KB)
    tok = at_byte("tok", [6, NT, W], area)
    gates = at_byte("gates", [2 * KC, T], area)
    roped = at_byte("roped", [2, NT, W], area + 24 * KB)
    q_t = at_byte("q_t", [WC, T], area + 32 * KB)
    k_t = at_byte("k_t", [WC, T], area + 36 * KB)
    qi_t = at_byte("qi_t", [WC, T], area + 40 * KB)
    u_t = at_byte("u_t", [WC, T], area + 40 * KB)
    ki_t = at_byte("ki_t", [T], area + 44 * KB)
    soft = at_byte("soft", [2, GROUP, T], area + 45 * KB)
    p_t = at_byte("p_t", [2, GROUP, P], area + 24 * KB)
    rope_tmp = at_byte("rope_tmp", [NT, W], area + 53 * KB)
    mix_b = at_byte("mix_b", [NT, W], area + 53 * KB)
    ya_v = at_byte("ya_v", [NT, W], area + 57 * KB)
    att = at_byte("att", [NT, W], area + 28 * KB)
    work = at_byte("work", [NT, 2 * P], area + 61 * KB)
    ya = at_byte("ya", [WC, 2, T], area + 45 * KB, F32R)
    ws_raw = at_byte("ws_raw", [WC, P], area + 66 * KB)
    yb = at_byte("yb", [WC, 2, T], area + 63 * KB, F32R)
    ws_m = at_byte("ws_m", [WC, P], area + 71 * KB)
    rows = at_byte("rows", [3, W], area + 73 * KB)
    ki_rope = at_byte("ki_rope", [NT, 2, HD], area + 79 * KB)
    sm_raw = at_byte("sm_raw", [KC, HD + NH], area + 63 * KB)
    sm_hi = at_byte("sm_hi", [KC, HD + NH], area + 20 * KB, F32R)
    sm_lo = at_byte("sm_lo", [KC, HD + NH], area + 28 * KB, F32R)
    m = at_byte("m", [KC, 2, T], area + 24 * KB, F32R)

    conv = at_byte("conv", [2, 2, T], area + 48 * KB)
    hm = at_byte("hm", [KC, T], area + 44 * KB)
    y2 = at_byte("y2", [KC, 2, T], area + 67 * KB, F32R)
    dn_k = at_byte("dn_k", [DN_H, T], area + 67 * KB)
    dn_q = at_byte("dn_q", [DN_H, T], area + 24 * KB)
    dn_v = at_byte("dn_v", [DN_H, T], area)
    z_t = at_byte("z_t", [DN_H, T], area)
    dn_sq = at_byte("dn_sq", [DN_H, T], area + 61 * KB)
    dn_rn = at_byte("dn_rn", [DN_H, T], area + 57 * KB)
    gb = at_byte("gb", [2, DN_H, P], area + 53 * KB)
    k_dec = at_byte("k_dec", [DN_H, P], area + 12 * KB)
    rhs_w = at_byte("rhs_w", [DN_H, P], area + 14 * KB)
    rhs_v = at_byte("rhs_v", [NT, DN_H, P], area + 20 * KB)
    a_t = at_byte("a_t", [NT, DN_H, P], area + 61 * KB)
    qk = at_byte("qk", [NT, DN_H, P], area + 40 * KB)
    qg = at_byte("qg", [DN_H, P], area + 65 * KB)
    gam = at_byte("gam", [NT, DN_H, P], area + 71 * KB)
    beta_s = at_byte("beta_s", [NT, DN_H, P], area + 75 * KB)
    u_inv = at_byte("u_inv", [NT, DN_H, P], area + 67 * KB)
    t_inv = at_byte("t_inv", [NT, DN_H, P], area + 57 * KB)
    lev_p = at_byte("lev_p", [NT, DN_H, P], area + 71 * KB)
    lev_c = at_byte("lev_c", [NT, DN_H, P], area + 75 * KB)
    w_neg = at_byte("w_neg", [DN_H, P], area + 75 * KB)
    state = at_byte("state", [DN_H, P], area + 77 * KB)
    v_new = at_byte("v_new", [NT, DN_H, P], area + 57 * KB)
    o_t = at_byte("o_t", [DN_H, T], area + 61 * KB)
    o_sq = at_byte("o_sq", [DN_H, T], area + 20 * KB)
    o_rn = at_byte("o_rn", [DN_H, T], area + 12 * KB)
    ba_hi = at_byte("ba_hi", [KC, 2 * DN_H], area + 20 * KB, F32R)
    ba_lo = at_byte("ba_lo", [KC, 2 * DN_H], area + 28 * KB, F32R)

    ps = ctx.enter_context(nc.psum_tensor("ps", [P, 8, 512], F32))
    SC, AUX = 4, 6

    st1, slots1, full1, freed1 = plan(PLAN1)
    st2, slots2, full2, freed2 = plan(PLAN2)

    def sig(name, per1, per2, pre=0, mid=0):
        return Signal(ctx.enter_context(nc.semaphore(name)), per1, per2, pre, mid)

    landed = [sig(f"landed{r}", 8 * slots1, 8 * slots2) for r in range(RAW_RING)]
    hi = sig("hi", slots1, slots2)
    lo = sig("lo", slots1, slots2, pre=RAW_RING)
    used = sig("used", slots1, slots2, pre=RING)
    full = sig("full", full1, full2)
    drained = sig("drained", freed1["drained"], freed2["drained"], pre=2)
    x_new = sig("x_new", 3 * KC, 4 * KC, pre=2, mid=KC)
    projected = sig("projected", 20, 8)
    squared = sig("squared", 3 * KC, 4 * KC, pre=KC, mid=KC)
    summed = sig("summed", 21, 28, pre=7, mid=7)
    mean_sq = sig("mean_sq", 3, 4, mid=1)
    rooted = sig("rooted", 3, 4, mid=1)
    rstd_ok = sig("rstd_ok", 3, 4, mid=1)
    v_ok = sig("v_ok", 3 * KC, 4 * KC)
    xn_hi = sig("xn_hi", 3 * KC, 2 * KC)
    xn_lo_even = sig("xn_lo_even", 3 * KC // 2, KC)
    xn_lo_odd = sig("xn_lo_odd", 3 * KC // 2, KC)
    gate_ok = sig("gate_ok", 2 * FC, FC)
    h_hi = sig("h_hi", 2 * FC, FC)
    h_lo = sig("h_lo", 2 * FC, FC, pre=2)
    params = sig("params", 48, 0)
    ready = sig("ready", 0, 0)
    small = sig("small", 1, 1)
    small_out = sig("small_out", 1, 1)
    sm_split = sig("sm_split", 2, 2)
    idx_roped = sig("idx_roped", 8, 0)
    qk_roped = sig("qk_roped", 8, 8)
    turned = sig("turned", 7, 4)
    turn_out = sig("turn_out", 7, 4)
    logits = sig("logits", 4, 0)
    relu_ok = sig("relu_ok", 4, 0)
    idx_sum = sig("idx_sum", 16, 0)
    top8 = sig("top8", 32, 0)
    bias_ok = sig("bias_ok", 4, 0)
    scores = sig("scores", 4, 4)
    masked = sig("masked", 8, 8)
    max_ok = sig("max_ok", 4, 4)
    probs = sig("probs", 16, 16)
    p_turned = sig("p_turned", 6, 6)
    p_out = sig("p_out", 6, 6)
    pv = sig("pv", 4, 4)
    zi = sig("zi", 4, 4)
    att_ok = sig("att_ok", 4, 4)
    att_turned = sig("att_turned", 2, 2)
    yb_hi = sig("yb_hi", 2, 2)
    yb_lo = sig("yb_lo", 2, 2)
    ws_ok = sig("ws_ok", 1, 0)
    ln_stats = sig("ln_stats", 4, 0)
    ln_rooted = sig("ln_rooted", 1, 0)
    ln_inv = sig("ln_inv", 1, 0)
    ln_norm = sig("ln_norm", 2, 0)
    ln_ok = sig("ln_ok", 4, 0)
    mixed = sig("mixed", 2, 0)
    mix_ok = sig("mix_ok", 2, 0)
    ya_ok = sig("ya_ok", 2, 0)
    ya_hi = sig("ya_hi", 2, 0)
    ya_lo = sig("ya_lo", 2, 0)
    gate_sig = sig("gate_sig", 2, 0)
    merge = sig("merge", KC, 0)
    merge_even = sig("merge_even", 8, 0)
    w_idx_ok = sig("w_idx_ok", 1, 0)
    m_hi = sig("m_hi", KC, 0)
    m_lo = sig("m_lo", KC, 0)
    stored = sig("stored", 0, 0)
    held = sig("held", 0, 0)
    tap = sig("tap", 0, 12 + 2 * FC)
    conv_ok = sig("conv_ok", 0, 30 + 3 * FC)
    act_ok = sig("act_ok", 0, 6)
    hv_ok = sig("hv_ok", 0, FC)
    ba_split = sig("ba_split", 0, 2)
    beta_exp = sig("beta_exp", 0, 1)
    beta_ok = sig("beta_ok", 0, 2)
    dec_in = sig("dec_in", 0, 2)
    dec_exp = sig("dec_exp", 0, 2)
    dec_ln = sig("dec_ln", 0, 1)
    dec_ok = sig("dec_ok", 0, 2)
    g_col = sig("g_col", 0, 1)
    g_neg_ok = sig("g_neg_ok", 0, 1)
    gb_ok = sig("gb_ok", 0, 4)
    g_rows = sig("g_rows", 0, 2)
    gam_in = sig("gam_in", 0, 2)
    beta_out = sig("beta_out", 0, 2)
    gam_ok = sig("gam_ok", 0, 2)
    g_last_ok = sig("g_last_ok", 0, 1)
    qg_e = sig("qg_e", 0, 1)
    k_exp_in = sig("k_exp_in", 0, 1)
    k_scale_ok = sig("k_scale_ok", 0, 1)
    w_exp = sig("w_exp", 0, 1)
    w_scale_ok = sig("w_scale_ok", 0, 1)
    dn_squared = sig("dn_squared", 0, 2)
    dn_summed = sig("dn_summed", 0, 2)
    dn_rooted = sig("dn_rooted", 0, 2)
    dn_inv = sig("dn_inv", 0, 2)
    dn_unit = sig("dn_unit", 0, 2)
    dn_turned = sig("dn_turned", 0, 4)
    dn_scaled = sig("dn_scaled", 0, 4)
    grams = sig("grams", 0, 4)
    a_raw = sig("a_raw", 0, 2)
    a_ok = sig("a_ok", 0, 2)
    qk_ok = sig("qk_ok", 0, 2)
    qg_ok = sig("qg_ok", 0, 1)
    u_first = sig("u_first", 0, 4)
    t_first = sig("t_first", 0, 2)
    t_first_out = sig("t_first_out", 0, 2)
    c_ok = sig("c_ok", 0, 12)
    lp = sig("lp", 0, 12)
    lp_out = sig("lp_out", 0, 12)
    lt = sig("lt", 0, 10)
    t_ok = sig("t_ok", 0, 10)
    lu = sig("lu", 0, 12)
    u_ok = sig("u_ok", 0, 12)
    dn_out = sig("dn_out", 0, 6)
    dn_copy = sig("dn_copy", 0, 6)
    o_squared = sig("o_squared", 0, 1)
    o_summed = sig("o_summed", 0, 1)
    o_rooted = sig("o_rooted", 0, 1)
    o_inv = sig("o_inv", 0, 1)
    o_norm = sig("o_norm", 0, 1)
    o_gated = sig("o_gated", 0, 1)
    o_hi = sig("o_hi", 0, 1)
    o_lo = sig("o_lo", 0, 1)
    signals = {"drained": drained, "x_new": x_new, "projected": projected}

    def soft_view(buf, kl):
        return soft[:, buf].rearrange("p (a b) k -> p a b k", a=2)[:, :, :, 0:kl]

    def sc_view(kl):
        return ps[:, SC:SC + 2, 0:2 * kl].rearrange("p a (b k) -> p a b k", b=2)

    def heads(a, width=HD):
        return a.rearrange("p t (h d) -> p t h d", d=width)

    block = ctx.enter_context(nc.Block())
    END1 = (1, DEPTH)

    @block.sync
    def _(sp):
        tables = [(x[:], io["x"]), (ones_d[:], io["ones_d"]), (ident[:], io["ident"]), (eps[:], io["eps"]),
                  (gains1[:], io["gains1"]), (gain_mid[:], io["gain_mid"]), (gate_bias[:], io["gate_bias"]),
                  (cos1[:], io["cos1"]), (sin1[:], io["sin1"]), (causal[:], io["causal"]),
                  (tri_ts[:], io["tri_ts"]),
                  (ones[:], io["ones"]), (gains2[:], io["gains2"]), (cos2[:], io["cos2"]),
                  (sin2[:], io["sin2"]), (reach[:], io["reach"]), (conv_w[:], io["conv_w"]),
                  (up_w[:], io["up_w"]), (up_b[:], io["up_b"]), (decay_rows[:], io["decay_rows"]),
                  (dn_gain[:], io["dn_gain"]), (mask_t[:], io["mask_t"]), (strict[:], io["strict"]),
                  (level_m[:], io["level_m"]), (ba_raw[:], io["small2"])]
        assert len(tables) == N_TABLES
        for dst, src in tables:
            sp.dma_start(dst, src).then_inc(ready.sem, 16)

        def load(at, k, g, dst_elems, src):
            sp.wait_ge(lo.sem, lo.upto(at, k + 4 * g + 1 - RAW_RING))
            sp.dma_start(raw[:, k % RAW_RING, 0:dst_elems], src).then_inc(landed[k % RAW_RING].sem, 16)

        def stream(at, st, src, first=0, last=None):
            n = (st.slots if last is None else last) - first
            cycle(sp, n, 4, lambda j, g: load(at, st.slot0 + first + j, g, st.elems,
                                              src[at[1], first + j + 4 * g]))

        first = True
        with layers(sp) as layer:
            at = (1, layer)
            stream(at, st1["gu1"], io["gu1"], 0, 2)
            stream(at, st1["gu1"], io["gu1"], 2)
            stream(at, st1["down1"], io["down1"])
            stream(at, st1["in"], io["in1"], 0, 2)
            sp.wait_ge(used.sem, used.upto(at, st1["in"].slot0))
            for dst, src in [(sm_raw[:], io["small1"]), (ws_raw[:], io["ws1"]), (rows[:], io["rows1"])]:
                sp.dma_start(dst, src[layer]).then_inc(params.sem, 16)
            stream(at, st1["in"], io["in1"], 2)
            stream(at, st1["pb"], io["pb1"])
            stream(at, st1["pa"], io["pa1"])
            stream(at, st1["out"], io["out1"])
            stream(at, st1["gu2"], io["gu2"])
            stream(at, st1["down2"], io["down2"])
        if only_first:
            for k in range(LEAD):
                load(END1, k, 0, SLOT, io["in1"][0, k])
            sp.wait_ge(x_new.sem, x_new.upto(END1, KC))
            sp.dma_start(io["out"], x[:]).then_inc(stored.sem, 16)
            sp.wait_ge(stored.sem, 16)
            return
        with layers(sp) as layer:
            at = (2, layer)
            stream(at, st2["qkv"], io["in2"])
            cycle(sp, 8, 4, lambda j, g: load(at, st2["side"].slot0 + j, g, SLOT, io["in2"][layer, 6 + j + 4 * g]))
            stream(at, st2["out"], io["out2"])
            stream(at, st2["gu"], io["gu3"])
            stream(at, st2["down"], io["down3"])
        for k in range(LEAD):
            load((2, DEPTH), k, 0, SLOT, io["in2"][0, k])
        for c in range(KC):
            sp.wait_ge(x_new.sem, x_new.upto((2, DEPTH - 1), 3 * KC + c + 1))
            sp.dma_start(io["out"][:, c], x[:, c]).then_inc(stored.sem, 16)
        sp.wait_ge(stored.sem, 16 * KC)

    @block.tensor
    def _(pe):
        pe.sem_inc(used.sem, RING)

        def mac(out, w, wl, xh, xl, first, last):
            pe.matmul(out, w, xh, start=first, stop=False)
            pe.matmul(out, w, xl, start=False, stop=False)
            return pe.matmul(out, wl, xh, start=False, stop=last)

        def mac_tok(out, xh, xl, w, wl, first, last):
            pe.matmul(out, xh, w, start=first, stop=False)
            pe.matmul(out, xh, wl, start=False, stop=False)
            return pe.matmul(out, xl, w, start=False, stop=last)

        def mean_square(at, k):
            pe.wait_ge(summed.sem, summed.upto(at, 7 * k))
            pe.matmul(ps[:, AUX, 0:T], ones_d[:], ssum[:], start=True, stop=True).then_inc(mean_sq.sem, 1)

        def xn_ready(at, k, c):
            s = xn_lo_even if c % 2 == 0 else xn_lo_odd
            pe.wait_ge(s.sem, s.upto(at, k * KC // 2 + c // 2 + 1))

        def slot(at, st, j, g=0):
            pe.wait_ge(lo.sem, lo.upto(at, st.slot0 + j + 4 * g + 1))
            r = (st.slot0 + j) % RING
            return w_hi[:, r], w_lo[:, r]

        def pair(at, st, i):
            if not isinstance(i, int) or i >= 2 or st.name != "in":
                pe.wait_ge(signals[st.free].sem, signals[st.free].upto(at, st.free0 + (i - 1) * st.free_by))

        def stage_open(at, prev):
            pe.wait_ge(signals[prev.free].sem, signals[prev.free].upto(at, prev.free0 + prev.pairs * prev.free_by))
            pe.sem_inc(held.sem, 1)

        def wide(at, st, j, g, x_of, chunks, k_norm=None, between=None):
            whs, wls = slot(at, st, j, g)
            tiles = SLOT // P // chunks
            wh = whs.rearrange("p (c n) -> p c n", c=chunks)
            wl = wls.rearrange("p (c n) -> p c n", c=chunks)
            for f in range(tiles):
                q = (tiles // 2) * j + f // 2
                if f % 2 == 0:
                    pair(at, st, q + 4 * g)
                out = ps[:, 2 * (q % 2) + f % 2, 0:T]
                for c in range(chunks):
                    if k_norm is not None and f == 0 and j == 0:
                        xn_ready(at, k_norm, c)
                    last = mac(out, wh[:, c, f * P:(f + 1) * P], wl[:, c, f * P:(f + 1) * P],
                               x_of[:, c, 0], x_of[:, c, 1], c == 0, c == chunks - 1)
                last.then_inc(full.sem if f < tiles - 1 else used.sem, 1)
                if between and f == 0:
                    between()

        def down(at, st, hk):
            def tile(j, g):
                pair(at, st, j + 2 * g)
                out = ps[:, 2 * (j % 2), 0:T]
                for half in range(2):
                    pe.wait_ge(lo.sem, lo.upto(at, st.slot0 + 2 * j + half + 4 * g + 1))
                    pe.wait_ge(h_lo.sem, h_lo.upto(at, hk + (half + 1) * FC // 2))
                    r = (st.slot0 + 2 * j + half) % RING
                    wh = w_hi[:, r, 0:SLOT_DOWN].rearrange("p (c n) -> p c n", n=P)
                    wl = w_lo[:, r, 0:SLOT_DOWN].rearrange("p (c n) -> p c n", n=P)
                    for c in range(FC // 2):
                        k = half * FC // 2 + c
                        last = mac(out, wh[:, c], wl[:, c], h[:, k, 0], h[:, k, 1], k == 0, k == FC - 1)
                    last.then_inc(used.sem, 1)
            cycle(pe, st.pairs, 2, tile)

        def tokens(at, st, j, k_norm=None, between=None):
            whs, wls = slot(at, st, j)
            pair(at, st, j)
            wh = whs.rearrange("p (c n) -> p c n", c=KC)
            wl = wls.rearrange("p (c n) -> p c n", c=KC)
            for t in range(NT):
                for c in range(KC):
                    if k_norm is not None and t == 0:
                        xn_ready(at, k_norm, c)
                    last = mac_tok(ps[:, 2 * (j % 2) + t, 0:256], xn[:, c, 0, t * P:(t + 1) * P],
                                   xn[:, c, 1, t * P:(t + 1) * P], wh[:, c], wl[:, c], c == 0, c == KC - 1)
                last.then_inc(full.sem if t == 0 else used.sem, 1)
                if between and t == 0:
                    between()

        def turn(at, k, src, bank=AUX):
            if k >= 2:
                pe.wait_ge(turn_out.sem, turn_out.upto(at, k - 1))
            n = len(src)
            for i, s in enumerate(src):
                last = pe.transpose(ps[:, bank + k % 2, i * P:(i + 1) * P], s, ident[:])
            last.then_inc(turned.sem, 1)

        def score(at, u, q, k, done):
            t, g = UNITS[u]
            kl = P * (t + 1)
            view = sc_view(kl)
            for hh in range(GROUP):
                hd = GROUP * g + hh
                lane = slice(HD * (hd % 2), HD * (hd % 2) + HD)
                last = pe.matmul(view[:, hh % 2, hh // 2], q[lane, hd // 2, t * P:(t + 1) * P], k(lane, hd, kl),
                                 start=True, stop=True)
            last.then_inc(done.sem, 1)

        def attend_scores(at, u, n_turns, bank=AUX):
            if u == 0:
                pe.wait_ge(turn_out.sem, turn_out.upto(at, n_turns))
            elif bank == SC:
                pe.wait_ge(att_ok.sem, att_ok.upto(at, u))
                if u == 2:
                    pe.wait_ge(yb_lo.sem, yb_lo.upto(at, 1))
            else:
                pe.wait_ge(masked.sem, masked.upto(at, 2 * u))
            score(at, u, q_t, lambda lane, hd, kl: k_t[lane, hd // 2, 0:kl], scores)

        def attend_turn(at, u, bank=AUX):
            t, _ = UNITS[u]
            pe.wait_ge(probs.sem, probs.upto(at, GROUP * (u + 1)))
            if u:
                pe.wait_ge(p_out.sem, p_out.upto(at, TURNS[u - 1]))
            if u and t:
                pe.wait_ge(att_ok.sem, att_ok.upto(at, u))
            if u >= 2:
                pe.wait_ge(yb_lo.sem, yb_lo.upto(at, 1))
            if bank == SC:
                pe.wait_ge(masked.sem, masked.upto(at, 2 * u + 2))
            for b in range(t + 1):
                for k in range(GROUP):
                    last = pe.transpose(ps[:, bank + b, k * P:(k + 1) * P], soft[:, u % 2, k, b * P:(b + 1) * P],
                                        ident[:])
                last.then_inc(p_turned.sem, 1)

        def attend_pv(at, u, v_at, bank=AUX):
            t, g = UNITS[u]
            pe.wait_ge(p_out.sem, p_out.upto(at, TURNS[u]))
            if u:
                pe.wait_ge(att_ok.sem, att_ok.upto(at, u))
            for hh in range(GROUP):
                k = GROUP // 2 * (hh % 2) + hh // 2
                for b in range(t + 1):
                    last = pe.matmul(ps[:, bank + 1, hh * HD:(hh + 1) * HD], p_t[:, b, k],
                                     v_at[:, b, (GROUP * g + hh) * HD:(GROUP * g + hh + 1) * HD],
                                     start=(b == 0), stop=(b == t))
            last.then_inc(pv.sem, 1)

        def attend_out(at, t, bank=AUX):
            pe.wait_ge(att_ok.sem, att_ok.upto(at, 2 if t else 4))
            pe.wait_ge(p_out.sem, p_out.upto(at, TURNS[1] if t else TURNS[3]))
            for c in range(WC):
                last = pe.transpose(ps[:, bank, c * P:(c + 1) * P], att[:, t, c * P:(c + 1) * P], ident[:])
            last.then_inc(att_turned.sem, 1)

        def small_product(at, n, split_ok, w, wl):
            pe.wait_ge(split_ok.sem, split_ok.upto(at, 2))
            for t in range(NT):
                for c in range(KC):
                    last = mac_tok(ps[:, AUX + 1, t * n:(t + 1) * n], xn[:, c, 0, t * P:(t + 1) * P],
                                   xn[:, c, 1, t * P:(t + 1) * P], w[:, c], wl[:, c],
                                   c == 0, c == KC - 1)
            last.then_inc(small.sem, 1)

        def index_scores(at, u):
            if u == 0:
                pe.wait_ge(turn_out.sem, turn_out.upto(at, 3))
            else:
                pe.wait_ge(relu_ok.sem, relu_ok.upto(at, u))
            score(at, u, qi_t, lambda lane, hd, kl: ki_t[lane, 0:kl], logits)

        def gmlp_mix(at, n):
            if n == 0:
                pe.wait_ge(ln_ok.sem, ln_ok.upto(at, 4))
                pe.wait_ge(ws_ok.sem, ws_ok.upto(at, 1))
                pe.wait_ge(att_ok.sem, att_ok.upto(at, 4))
            else:
                pe.wait_ge(mix_ok.sem, mix_ok.upto(at, n))
            for g in range(WC):
                last = pe.matmul(ps[:, AUX + 1, g * P:(g + 1) * P], tok[:, VA, n, g * P:(g + 1) * P], ws_m[:, g],
                                 start=True, stop=True)
            last.then_inc(mixed.sem, 1)

        def turns_of(buf, t):
            return [roped[:, buf, t, c * P:(c + 1) * P] for c in range(WC)]

        pe.wait_ge(ready.sem, 16 * N_TABLES)
        with layers(pe) as layer:
            at = (1, layer)
            mean_square(at, 0)
            cycle(pe, FC, 4, lambda j, g: wide(at, st1["gu1"], j, g, xn, KC, 0))
            stage_open(at, st1["gu1"])
            down(at, st1["down1"], 0)
            mean_square(at, 1)

            stage_open(at, st1["down1"])
            for k in range(20):
                if k < 10:
                    tokens(at, st1["in"], k, 1 if k == 0 else None)
                else:
                    wide(at, st1["in"], k, 0, xn, KC)
                if k == 1:
                    small_product(at, HD + NH, sm_split, sm_hi, sm_lo)
                if k == 3:
                    pe.wait_ge(idx_roped.sem, idx_roped.upto(at, 4))
                    turn(at, 0, turns_of(0, 0))
                    pe.wait_ge(small_out.sem, small_out.upto(at, 1))
                    turn(at, 1, turns_of(0, 1))
                    pe.wait_ge(idx_roped.sem, idx_roped.upto(at, 8))
                    turn(at, 2, [ki_rope[:, t].rearrange("p a d -> p (a d)") for t in range(NT)])
                if k in (4, 5, 6, 7):
                    index_scores(at, k - 4)
                if k == 7:
                    pe.wait_ge(qk_roped.sem, qk_roped.upto(at, 4))
                    turn(at, 3, turns_of(1, 0))
                    turn(at, 4, turns_of(1, 1))
                if k == 8:
                    pe.wait_ge(qk_roped.sem, qk_roped.upto(at, 8))
                    turn(at, 5, turns_of(0, 0))
                    turn(at, 6, turns_of(0, 1))
                if k == 9:
                    pe.wait_ge(relu_ok.sem, relu_ok.upto(at, 4))
                    attend_scores(at, 0, 7)
                if k == 10:
                    attend_scores(at, 1, 7)
                    attend_turn(at, 0)
                if k == 11:
                    attend_pv(at, 0, tok[:, V])
                    attend_turn(at, 1)
                if k == 12:
                    attend_pv(at, 1, tok[:, V])
                    attend_scores(at, 2, 7)
                if k == 13:
                    attend_out(at, 1)
                    attend_scores(at, 3, 7)
                    attend_turn(at, 2)
                if k == 14:
                    attend_pv(at, 2, tok[:, V])
                    attend_turn(at, 3)
                if k == 15:
                    attend_pv(at, 3, tok[:, V])
                if k == 16:
                    attend_out(at, 0)
                    gmlp_mix(at, 0)
                if k == 17:
                    gmlp_mix(at, 1)

            stage_open(at, st1["in"])
            pe.wait_ge(yb_lo.sem, yb_lo.upto(at, 2))
            for j in range(2):
                wide(at, st1["pb"], j, 0, yb, WC)
            pe.wait_ge(ya_lo.sem, ya_lo.upto(at, 2))
            for j in range(2):
                wide(at, st1["pa"], j, 0, ya, WC)
            stage_open(at, st1["pa"])
            pe.wait_ge(m_lo.sem, m_lo.upto(at, KC))
            for j in range(4):
                wide(at, st1["out"], j, 0, m, KC)
            mean_square(at, 2)
            cycle(pe, FC, 4, lambda j, g: wide(at, st1["gu2"], j, g, xn, KC, 2))
            stage_open(at, st1["gu2"])
            down(at, st1["down2"], FC)
        mean_square(END1, 0)
        if only_first:
            return
        with layers(pe) as layer:
            at = (2, layer)
            sq, ss, so = st2["qkv"], st2["side"], st2["out"]

            def turn4(bank, src, done):
                for i in range(DN_H):
                    last = pe.transpose(ps[:, bank, i * P:(i + 1) * P], src(i), ident[:])
                last.then_inc(done.sem, 1)

            def heads4(bank, lhs, rhs, done, start=True, stop=True):
                for i in range(DN_H):
                    last = pe.matmul(ps[:, bank, i * P:(i + 1) * P], lhs(i), rhs(i), start=start, stop=stop)
                if done is not None:
                    last.then_inc(done.sem, 1)

            def lane(t):
                return slice(t * P, (t + 1) * P)

            def decay_column():
                pe.wait_ge(dec_ok.sem, dec_ok.upto(at, 2))
                pe.wait_ge(small_out.sem, small_out.upto(at, 1))
                for t in range(NT):
                    last = pe.matmul(ps[:, AUX + 1, t * DN_H:(t + 1) * DN_H], tri_ts[:], dec_g[:, t],
                                     start=True, stop=True)
                last.then_inc(g_col.sem, 1)

            def decay_rows_of(t):
                pe.wait_ge(gb_ok.sem, gb_ok.upto(at, 2 * t + 2))
                if t == 0:
                    pe.wait_ge(g_neg_ok.sem, g_neg_ok.upto(at, 1))
                else:
                    pe.wait_ge(dn_rooted.sem, dn_rooted.upto(at, 1))
                pe.matmul(ps[:, AUX, :], ones[:], gb[:, 0].rearrange("p h q -> p (h q)"), start=True, stop=True)
                pe.matmul(ps[:, AUX + 1, :], ones[:], gb[:, 1].rearrange("p h q -> p (h q)"),
                          start=True, stop=True).then_inc(g_rows.sem, 1)

            def unit_sums(i):
                pe.wait_ge(dn_squared.sem, dn_squared.upto(at, i + 1))
                pe.wait_ge(beta_out.sem, beta_out.upto(at, i + 1))
                pe.wait_ge(gam_in.sem, gam_in.upto(at, i + 1))
                if i == 0:
                    pe.wait_ge(g_last_ok.sem, g_last_ok.upto(at, 1))
                else:
                    pe.wait_ge(qg_e.sem, qg_e.upto(at, 1))
                for b in range(2):
                    last = pe.matmul(ps[:, AUX + b, :], ones[:],
                                     dn_sq[:, 2 * b:2 * b + 2].rearrange("p h q -> p (h q)"), start=True, stop=True)
                last.then_inc(dn_summed.sem, 1)

            def turn_k():
                pe.wait_ge(dn_rooted.sem, dn_rooted.upto(at, 2))
                pe.wait_ge(dn_unit.sem, dn_unit.upto(at, 1))
                for t in range(NT):
                    turn4(AUX + t, lambda i, t=t: dn_k[:, i, lane(t)], dn_turned)

            def turn_v():
                pe.wait_ge(act_ok.sem, act_ok.upto(at, 6))
                for t in range(NT):
                    if t == 0:
                        pe.wait_ge(a_ok.sem, a_ok.upto(at, 1))
                    else:
                        pe.wait_ge(qk_ok.sem, qk_ok.upto(at, 1))
                    turn4(AUX + t, lambda i, t=t: dn_v[:, i, lane(t)], dn_turned)

            def gram(t):
                pe.wait_ge(dn_unit.sem, dn_unit.upto(at, 2))
                if t == 0:
                    pe.wait_ge(dn_scaled.sem, dn_scaled.upto(at, 2))
                else:
                    pe.wait_ge(dn_scaled.sem, dn_scaled.upto(at, 4))
                heads4(AUX, lambda i: dn_k[:, i, lane(t)], lambda i: dn_k[:, i, lane(t)], grams)
                heads4(AUX + 1, lambda i: dn_k[:, i, lane(t)], lambda i: dn_q[:, i, lane(t)], grams)

            def inverse_first():
                pe.wait_ge(a_raw.sem, a_raw.upto(at, 2))
                pe.wait_ge(qk_ok.sem, qk_ok.upto(at, 2))
                for t in range(NT):
                    pe.wait_ge(u_first.sem, u_first.upto(at, 2 * t + 2))
                    turn4(AUX + t, lambda i, t=t: u_inv[:, t, i], t_first)

            def level_p(n):
                for t in range(NT):
                    pe.wait_ge(c_ok.sem, c_ok.upto(at, 2 * (n - 1) + t + 1))
                    if n == 1:
                        pe.wait_ge(t_first_out.sem, t_first_out.upto(at, t + 1))
                    else:
                        pe.wait_ge(t_ok.sem, t_ok.upto(at, 2 * (n - 2) + t + 1))
                        pe.wait_ge(u_ok.sem, u_ok.upto(at, 2 * (n - 2) + t + 1))
                    heads4(AUX + t, lambda i: lev_c[:, t, i], lambda i: t_inv[:, t, i], lp)

            def level_t(n):
                for t in range(NT):
                    pe.wait_ge(lp_out.sem, lp_out.upto(at, 2 * (n - 1) + t + 1))
                    heads4(AUX + t, lambda i: u_inv[:, t, i], lambda i: lev_p[:, t, i], lt)

            def level_u(n):
                for t in range(NT):
                    if n < LEVELS - 1:
                        pe.wait_ge(t_ok.sem, t_ok.upto(at, 2 * (n - 1) + t + 1))
                    else:
                        pe.wait_ge(lp_out.sem, lp_out.upto(at, 2 * (n - 1) + t + 1))
                    heads4(AUX + t, lambda i: lev_p[:, t, i], lambda i: u_inv[:, t, i], lu)

            def mid(k):
                if k == 0:
                    gram(0)
                if k == 1:
                    gram(1)
                if k == 2:
                    level_p(1)
                if k in (3, 4, 5, 6, 7):
                    level_u(k - 2)
                    level_p(k - 1)

            mean_square(at, 0)
            for k in range(6):
                def between(k=k):
                    if k == 3:
                        decay_column()
                    if k == 4:
                        unit_sums(0)
                    if k == 5:
                        unit_sums(1)
                wide(at, sq, k, 0, xn, KC, 0 if k == 0 else None, between)
                if k == 1:
                    small_product(at, 2 * DN_H, ba_split, ba_hi, ba_lo)
                if k == 3:
                    decay_rows_of(0)
                if k == 4:
                    decay_rows_of(1)
                if k == 5:
                    turn_k()
            stage_open(at, sq)
            for k in range(8):
                if k < 6:
                    tokens(at, ss, k, None, lambda: mid(k))
                else:
                    wide(at, ss, k, 0, xn, KC, None, lambda: mid(k))
                if k == 0:
                    turn_v()
                if k == 1:
                    inverse_first()
                if k in (2, 3, 4, 5, 6):
                    level_t(k - 1)
                if k == 2:
                    pe.wait_ge(qk_roped.sem, qk_roped.upto(at, 4))
                    turn(at, 0, turns_of(1, 0), SC)
                    turn(at, 1, turns_of(1, 1), SC)
                if k == 4:
                    pe.wait_ge(qk_roped.sem, qk_roped.upto(at, 8))
                    turn(at, 2, turns_of(0, 0), SC)
                    turn(at, 3, turns_of(0, 1), SC)
                if k == 5:
                    attend_scores(at, 0, 4, SC)
                if k == 6:
                    attend_turn(at, 0, SC)
                if k == 7:
                    attend_pv(at, 0, tok[:, V], SC)
                    level_u(LEVELS - 1)
                    attend_scores(at, 1, 4, SC)

            pe.wait_ge(u_ok.sem, u_ok.upto(at, 11))
            heads4(AUX, lambda i: u_inv[:, 0, i], lambda i: rhs_v[:, 0, i], dn_out)
            pe.wait_ge(u_ok.sem, u_ok.upto(at, 12))
            heads4(AUX + 1, lambda i: rhs_w[:, i], lambda i: u_inv[:, 1, i], dn_out)
            attend_turn(at, 1, SC)
            pe.wait_ge(dn_copy.sem, dn_copy.upto(at, 1))
            heads4(AUX, lambda i: k_dec[:, i], lambda i: v_new[:, 0, i], dn_out)
            attend_pv(at, 1, tok[:, V], SC)
            pe.wait_ge(dn_copy.sem, dn_copy.upto(at, 3))
            for i in range(DN_H):
                out = ps[:, AUX + 1, i * P:(i + 1) * P]
                pe.matmul(out, u_inv[:, 1, i], rhs_v[:, 1, i], start=True, stop=False)
                last = pe.matmul(out, w_neg[:, i], state[:, i], start=False, stop=True)
            last.then_inc(dn_out.sem, 1)
            heads4(AUX, lambda i: v_new[:, 0, i], lambda i: qk[:, 0, i], dn_out)
            attend_out(at, 1, SC)
            pe.wait_ge(dn_copy.sem, dn_copy.upto(at, 4))
            attend_scores(at, 2, 4, SC)
            for i in range(DN_H):
                out = ps[:, AUX + 1, i * P:(i + 1) * P]
                pe.matmul(out, v_new[:, 1, i], qk[:, 1, i], start=True, stop=False)
                last = pe.matmul(out, state[:, i], qg[:, i], start=False, stop=True)
            last.then_inc(dn_out.sem, 1)
            attend_turn(at, 2, SC)
            attend_pv(at, 2, tok[:, V], SC)
            attend_scores(at, 3, 4, SC)
            pe.wait_ge(o_squared.sem, o_squared.upto(at, 1))
            for b in range(2):
                last = pe.matmul(ps[:, AUX + b, :], ones[:],
                                 o_sq[:, 2 * b:2 * b + 2].rearrange("p h q -> p (h q)"), start=True, stop=True)
            last.then_inc(o_summed.sem, 1)
            attend_turn(at, 3, SC)
            attend_pv(at, 3, tok[:, V], SC)
            attend_out(at, 0, SC)

            stage_open(at, ss)
            pe.wait_ge(o_lo.sem, o_lo.upto(at, 1))
            pe.wait_ge(yb_lo.sem, yb_lo.upto(at, 2))
            for j in range(4):
                wide(at, so, j, 0, y2, KC)
            mean_square(at, 1)
            mean_square(at, 2)
            cycle(pe, FC, 4, lambda j, g: wide(at, st2["gu"], j, g, xn, KC, 1))
            stage_open(at, st2["gu"])
            down(at, st2["down"], 0)
            mean_square(at, 3)

    def slot_done(eng, at, st, j, g=0):
        eng.wait_ge(used.sem, used.upto(at, st.slot0 + j + 4 * g + 1))

    def tile_done(eng, at, st, j, f, g=0):
        if f < st.early:
            eng.wait_ge(full.sem, full.upto(at, st.full0 + st.early * j + f + 1 + 4 * st.early * g))
        else:
            slot_done(eng, at, st, j, g)

    def rounds(eng, at, st, nxt, count, per, split, body):
        ahead = LEAD // per
        period = RING // per

        def step(j, g):
            for s in range(per):
                split(at, st.slot0 + per * j + LEAD + s, g, st.elems)
            body(j, g)

        cycle(eng, count - ahead, period, step)
        for j in range(count - ahead, count):
            for s in range(per):
                split(at, st.slot0 + per * j + LEAD + s, 0, nxt)
            body(j, 0)

    @block.scalar
    def _(act):
        def copy(out, src):
            return act.activation(out, src, ACT.Copy)

        def split(at, k, g, elems):
            r = k % RING
            act.wait_ge(landed[k % RAW_RING].sem, landed[k % RAW_RING].upto(at, 16 * (k // RAW_RING + 1) + 32 * g))
            act.wait_ge(used.sem, used.upto(at, k + 1 + 4 * g - RING))
            copy(w_hi[:, r, 0:elems], raw[:, k % RAW_RING, 0:elems]).then_inc(hi.sem, 1)

        def square(at, k, c, src, first=False):
            if not first:
                act.wait_ge(x_new.sem, x_new.upto(at, KC * k + c + 1))
            if isinstance(c, int) and c == 0:
                dst = ssum[:]
            else:
                dst = sqb[:, c % 2]
                if c >= 3:
                    act.wait_ge(summed.sem, summed.upto(at, 7 * k + c - 2))
            act.activation(dst, src, ACT.Square).then_inc(squared.sem, 1)

        def root(at, k):
            act.activation(warm[:], eps[:], ACT.Sqrt)
            act.wait_ge(mean_sq.sem, mean_sq.upto(at, k + 1))
            act.activation(rms[:], ps[:, AUX, 0:T], ACT.Sqrt, bias=eps[:, 0:1]).then_inc(rooted.sem, 1)

        def split_xn(at, k, kv):
            for c in range(KC):
                act.wait_ge(v_ok.sem, v_ok.upto(at, KC * kv + c + 1))
                copy(xn[:, c, 0], v[:, c]).then_inc(xn_hi.sem, 1)

        def taps(at, st, j, f, w, n0, bias=None, g=0):
            tile_done(act, at, st, j, f, g)
            func = ACT.Copy if bias is None else ACT.Identity
            more = {} if bias is None else {"bias": bias}
            act.activation(conv[:, j % 2, f], ps[:, 2 * (j % 2) + f, 0:T], func, scale=w, **more)\
               .then_inc(tap.sem, 1)

        def gate_silu(at, st, gk):
            def body(j, g):
                tile_done(act, at, st, j, 0, g)
                act.activation(silu_gate[:, j % 2], ps[:, 2 * (j % 2), 0:T], ACT.Silu).then_inc(gate_ok.sem, 1)
            return body

        def squares_of_down(at, st, k, src, nxt):
            def body(j, g):
                act.wait_ge(x_new.sem, x_new.upto(at, KC * k + j + 1 + 2 * g))
                if j == 0 and isinstance(g, int):
                    act.activation(ssum[:], src[:, 0], ACT.Square).then_inc(squared.sem, 1)
                    return
                f = j + 2 * g
                act.wait_ge(summed.sem, summed.upto(at, 7 * k + f - 2))
                act.activation(sqb[:, j % 2], src[:, f], ACT.Square).then_inc(squared.sem, 1)

            def splits(j, g, elems):
                for s in range(2):
                    split(at, st.slot0 + 2 * j + LEAD + s, g, elems)

            splits(0, 0, st.elems)
            body(0, 0)
            with act.Fori(0, (KC - 2) // 2) as g:
                for j in (1, 2):
                    splits(j, g, st.elems)
                    body(j, g)
            splits(KC - 1, 0, nxt)
            body(KC - 1, 0)

        def turn_copy(at, k, dst, n=WC, bank=AUX):
            act.wait_ge(turned.sem, turned.upto(at, k + 1))
            src = ps[:, bank + k % 2, 0:n * P]
            if n == WC:
                src = src.rearrange("p (c q) -> p c q", c=WC)
            copy(dst, src).then_inc(turn_out.sem, 1)

        def attend_exp(at, u):
            t, _ = UNITS[u]
            act.wait_ge(max_ok.sem, max_ok.upto(at, u + 1))
            for k in range(GROUP):
                s = soft[:, u % 2, k, 0:P * (t + 1)]
                act.activation(s, s, ACT.Exp, bias=neg_max[:, u % 2, k:k + 1],
                               accum_out=z_sum[:, u, k:k + 1]).then_inc(probs.sem, 1)

        def attend_copy(at, u, bank=AUX):
            t, _ = UNITS[u]
            if u:
                act.wait_ge(pv.sem, pv.upto(at, u))
            for b in range(t + 1):
                act.wait_ge(p_turned.sem, p_turned.upto(at, TURNS[u] - t + b))
                copy(p_t[:, b], ps[:, bank + b, :].rearrange("p (k q) -> p k q", k=GROUP)).then_inc(p_out.sem, 1)

        def attend_hi(at, t, dst, bank=AUX):
            act.wait_ge(att_turned.sem, att_turned.upto(at, 2 - t))
            copy(dst[:, :, 0, t * P:(t + 1) * P],
                 ps[:, bank, :].rearrange("p (c q) -> p c q", c=WC)).then_inc(yb_hi.sem, 1)

        def small_copies(at, n, dst):
            act.wait_ge(small.sem, small.upto(at, 1))
            copy(dst, ps[:, AUX + 1, 0:NT * n].rearrange("p (t n) -> p t n", n=n)).then_inc(small_out.sem, 1)

        act.wait_ge(ready.sem, 16 * N_TABLES)
        for c in range(KC):
            if c == 0:
                act.activation(ssum[:], x[:, 0], ACT.Square).then_inc(squared.sem, 1)
            else:
                if c >= 3:
                    act.wait_ge(summed.sem, c - 2)
                act.activation(sqb[:, c % 2], x[:, c], ACT.Square).then_inc(squared.sem, 1)
        for k in range(LEAD):
            split((1, 0), k, 0, SLOT)
        with layers(act) as layer:
            at = (1, layer)

            def ffn(k, gu, dn, nxt):
                root(at, k)
                split_xn(at, k, k)
                act.activation(warm[:], eps[:], ACT.Silu)
                rounds(act, at, gu, dn.elems, FC, 1, split, gate_silu(at, gu, 0))
                squares_of_down(at, dn, k, x, nxt)

            ffn(0, st1["gu1"], st1["down1"], SLOT)
            root(at, 1)
            split_xn(at, 1, 1)
            si = st1["in"]
            act.wait_ge(params.sem, params.upto(at, 48))
            copy(sm_hi[:], sm_raw[:]).then_inc(sm_split.sem, 1)
            act.activation(warm[:], eps[:], ACT.Exp)
            for k in range(20):
                split(at, si.slot0 + k + LEAD, 0, SLOT)
                if k == 10:
                    act.wait_ge(relu_ok.sem, relu_ok.upto(at, 4))
                if k == 12:
                    act.wait_ge(idx_roped.sem, idx_roped.upto(at, 8))
                    act.wait_ge(qk_roped.sem, qk_roped.upto(at, 8))
                for t in range(2):
                    tile_done(act, at, si, k, t)
                    bank = 2 * (k % 2) + t
                    if k < 10:
                        part = (QI, Q, K, V, VA)[k // 2]
                        dst = tok[:, part, t, 256 * (k % 2):256 * (k % 2) + 256]
                        f = ACT.Gelu_apprx_tanh if k >= 8 else ACT.Copy
                        ins = act.activation(dst, ps[:, bank, 0:256], f)
                    elif k < 12:
                        ins = act.activation(u_t[:, 2 * (k - 10) + t], ps[:, bank, 0:T], ACT.Gelu_apprx_tanh)
                    else:
                        f = 2 * (k - 12) + t
                        ins = act.activation(gates[:, f], ps[:, bank, 0:T], ACT.Identity,
                                             bias=gate_bias[:, layer, f:f + 1])
                ins.then_inc(projected.sem, 1)
                if k == 1:
                    small_copies(at, HD + NH, ki_wi[:])
                if k == 3:
                    turn_copy(at, 0, qi_t[:, :, 0:P])
                    turn_copy(at, 1, qi_t[:, :, P:T])
                    turn_copy(at, 2, ki_t[:], 2)
                if k in (4, 5, 6, 7):
                    u = k - 4
                    act.wait_ge(logits.sem, logits.upto(at, u + 1))
                    if u >= 2:
                        act.wait_ge(idx_sum.sem, idx_sum.upto(at, 4 * (u - 1)))
                    kl = P * (UNITS[u][0] + 1)
                    act.activation(soft_view(u % 2, kl), sc_view(kl), ACT.Relu).then_inc(relu_ok.sem, 1)
                if k == 7:
                    turn_copy(at, 3, q_t[:, :, 0:P])
                    turn_copy(at, 4, q_t[:, :, P:T])
                if k == 8:
                    turn_copy(at, 5, k_t[:, :, 0:P])
                    turn_copy(at, 6, k_t[:, :, P:T])
                if k == 9:
                    attend_exp(at, 0)
                if k == 10:
                    attend_copy(at, 0)
                    attend_exp(at, 1)
                if k == 11:
                    attend_copy(at, 1)
                if k == 12:
                    attend_exp(at, 2)
                if k == 13:
                    attend_hi(at, 1, yb)
                    attend_copy(at, 2)
                    attend_exp(at, 3)
                if k == 14:
                    attend_copy(at, 3)
                if k == 15:
                    act.wait_ge(ln_stats.sem, ln_stats.upto(at, 4))
                    act.activation(ln_root[:], ln_mv[:, :, 1], ACT.Sqrt, bias=eps[:, 0:1]).then_inc(ln_rooted.sem, 1)
                if k == 16:
                    attend_hi(at, 0, yb)
                if k in (17, 18):
                    n = k - 17
                    act.wait_ge(ya_ok.sem, ya_ok.upto(at, n + 1))
                    copy(ya[:, :, 0, n * P:(n + 1) * P],
                         ya_v[:, n].rearrange("p (c q) -> p c q", c=WC)).then_inc(ya_hi.sem, 1)
            act.wait_ge(projected.sem, projected.upto(at, 20))
            for n in (1, 0):
                part = gates[:, n * KC:(n + 1) * KC]
                act.activation(part, part, ACT.Sigmoid).then_inc(gate_sig.sem, 1)
            for st, nxt in ((st1["pb"], SLOT), (st1["pa"], SLOT)):
                for j in range(2):
                    split(at, st.slot0 + j + LEAD, 0, SLOT)
                    if st is st1["pa"]:
                        for c in range(4 * j, 4 * j + 4):
                            act.wait_ge(merge.sem, merge.upto(at, c + 1))
                            copy(m[:, c, 0], v[:, c]).then_inc(m_hi.sem, 1)
            so = st1["out"]
            for j in range(4):
                split(at, so.slot0 + j + LEAD, 0, SLOT)
                square(at, 1, 2 * j, x[:, 2 * j])
                square(at, 1, 2 * j + 1, x[:, 2 * j + 1])
            ffn(2, st1["gu2"], st1["down2"], SLOT)
        root(END1, 0)
        for c in range(KC):
            square(END1, 0, c, x[:, c])
        if only_first:
            return
        with layers(act) as layer:
            at = (2, layer)
            sq, ss, so = st2["qkv"], st2["side"], st2["out"]

            def four(t):
                return t.rearrange("p h q -> p (h q)")

            def silu_of(k):
                act.wait_ge(drained.sem, drained.upto(at, sq.free0 + k + 1))
                dst = (dn_k, dn_q, dn_v)[k // 2][:, 2 * (k % 2):2 * (k % 2) + 2]
                act.activation(dst, conv[:, k % 2], ACT.Silu).then_inc(act_ok.sem, 1)

            def decays():
                act.activation(beta_e[:], ba[:, :, 0:DN_H], ACT.Exp, scale=-1.0).then_inc(beta_exp.sem, 1)
                act.activation(a_exp[:], decay_rows[:, layer, 1], ACT.Exp).then_inc(dec_exp.sem, 1)
                act.wait_ge(dec_in.sem, dec_in.upto(at, 2))
                act.activation(dec_e[:], dec_n[:], ACT.Exp).then_inc(dec_exp.sem, 1)
                act.wait_ge(dec_exp.sem, dec_exp.upto(at, 2))
                act.activation(dec_n[:], dec_e[:], ACT.Ln, bias=ones[:, 0:1]).then_inc(dec_ln.sem, 1)

            def decay_copy():
                act.wait_ge(g_col.sem, g_col.upto(at, 1))
                act.activation(g_neg[:], ps[:, AUX + 1, 0:NT * DN_H].rearrange("p (t h) -> p t h", h=DN_H),
                               ACT.Copy, scale=-1.0).then_inc(g_neg_ok.sem, 1)
                act.wait_ge(g_neg_ok.sem, g_neg_ok.upto(at, 1))
                act.activation(w_scale[:], g_neg[:, 1], ACT.Exp, scale=-1.0).then_inc(w_exp.sem, 1)

            def decay_exps(t):
                act.wait_ge(g_rows.sem, g_rows.upto(at, t + 1))
                rows4 = ps[:, AUX, :].rearrange("p (h q) -> p h q", h=DN_H)
                if t == 0:
                    act.activation(g_last[:], rows4[:, :, P - 1], ACT.Copy).then_inc(g_last_ok.sem, 1)
                    act.wait_ge(k_exp_in.sem, k_exp_in.upto(at, 1))
                    act.activation(k_scale[:], k_scale[:], ACT.Exp).then_inc(k_scale_ok.sem, 1)
                else:
                    act.activation(qg[:], rows4, ACT.Exp).then_inc(qg_e.sem, 1)
                act.wait_ge(gam_in.sem, gam_in.upto(at, t + 1))
                for i in range(DN_H):
                    last = act.activation(gam[:, t, i], gam[:, t, i], ACT.Exp, bias=g_neg[:, t, i:i + 1])
                last.then_inc(gam_ok.sem, 1)

            def unit_squares(i):
                src = (dn_k, dn_q)[i]
                act.wait_ge(act_ok.sem, act_ok.upto(at, 2 * i + 2))
                if i:
                    act.wait_ge(dn_summed.sem, dn_summed.upto(at, 1))
                act.activation(four(dn_sq[:]), four(src[:]), ACT.Square).then_inc(dn_squared.sem, 1)

            def unit_roots(i):
                act.wait_ge(dn_summed.sem, dn_summed.upto(at, i + 1))
                if i:
                    act.wait_ge(dn_unit.sem, dn_unit.upto(at, 1))
                act.activation(dn_rn[:].rearrange("p (b h) q -> p b (h q)", b=2), ps[:, AUX:AUX + 2, :], ACT.Sqrt,
                               bias=eps[:, 0:1]).then_inc(dn_rooted.sem, 1)

            def first_copy():
                for t in range(NT):
                    act.wait_ge(t_first.sem, t_first.upto(at, t + 1))
                    copy(four(t_inv[:, t]), ps[:, AUX + t, :]).then_inc(t_first_out.sem, 1)

            def level_copy(n):
                for t in range(NT):
                    act.wait_ge(lp.sem, lp.upto(at, 2 * (n - 1) + t + 1))
                    copy(four(lev_p[:, t]), ps[:, AUX + t, :]).then_inc(lp_out.sem, 1)

            def out_copy(n, dst, bank, sign=1.0):
                act.wait_ge(dn_out.sem, dn_out.upto(at, n))
                src = ps[:, bank, :].rearrange("p (h q) -> p h q", h=DN_H)
                act.activation(dst, src, ACT.Copy, scale=sign).then_inc(dn_copy.sem, 1)

            root(at, 0)
            split_xn(at, 2, 0)
            copy(ba_hi[:], ba_raw[:, layer]).then_inc(ba_split.sem, 1)
            act.activation(warm[:], eps[:], ACT.Silu)
            for k in range(6):
                split(at, sq.slot0 + k + LEAD, 0, SLOT)
                if k:
                    silu_of(k - 1)
                taps(at, sq, k, 0, conv_w[:, layer, 2 * k, 3:4], 0)
                if k == 3:
                    decay_copy()
                    unit_squares(0)
                if k == 4:
                    unit_roots(0)
                if k == 5:
                    unit_squares(1)
                    unit_roots(1)
                taps(at, sq, k, 1, conv_w[:, layer, 2 * k + 1, 3:4], 0)
                if k == 1:
                    act.wait_ge(small.sem, small.upto(at, 1))
                    copy(ba[:], ps[:, AUX + 1, 0:NT * 2 * DN_H].rearrange("p (t n) -> p t n", n=2 * DN_H))\
                        .then_inc(small_out.sem, 1)
                if k == 2:
                    act.wait_ge(small_out.sem, small_out.upto(at, 1))
                    decays()
                if k == 3:
                    decay_exps(0)
                if k == 4:
                    decay_exps(1)
            for k in range(8):
                split(at, ss.slot0 + k + LEAD, 0, SLOT)
                if k == 0:
                    silu_of(5)
                if k in (2, 3, 4, 5, 6, 7):
                    level_copy(k - 1)
                for t in range(2):
                    tile_done(act, at, ss, k, t)
                    bank = 2 * (k % 2) + t
                    if k < 6:
                        part = (Q, K, V)[k // 2]
                        ins = act.activation(tok[:, part, t, 256 * (k % 2):256 * (k % 2) + 256],
                                             ps[:, bank, 0:256], ACT.Copy)
                    else:
                        if k == 6 and t == 0:
                            act.wait_ge(dn_scaled.sem, dn_scaled.upto(at, 4))
                        ins = act.activation(z_t[:, 2 * (k - 6) + t], ps[:, bank, 0:T], ACT.Silu)
                ins.then_inc(projected.sem, 1)
                if k == 1:
                    first_copy()
                if k == 2:
                    turn_copy(at, 0, q_t[:, :, 0:P], WC, SC)
                    turn_copy(at, 1, q_t[:, :, P:T], WC, SC)
                if k == 4:
                    turn_copy(at, 2, k_t[:, :, 0:P], WC, SC)
                    turn_copy(at, 3, k_t[:, :, P:T], WC, SC)
                if k == 5:
                    attend_exp(at, 0)
                if k == 6:
                    attend_copy(at, 0, SC)
            attend_exp(at, 1)
            out_copy(1, v_new[:, 0], AUX)
            out_copy(2, w_neg[:], AUX + 1, -1.0)
            attend_copy(at, 1, SC)
            out_copy(3, state[:], AUX)
            out_copy(4, v_new[:, 1], AUX + 1)
            out_copy(5, o_t[:, :, 0:P], AUX)
            attend_hi(at, 1, y2[:, 0:WC], SC)
            attend_exp(at, 2)
            out_copy(6, o_t[:, :, P:T], AUX + 1)
            act.wait_ge(dn_copy.sem, dn_copy.upto(at, 6))
            act.activation(four(o_sq[:]), four(o_t[:]), ACT.Square).then_inc(o_squared.sem, 1)
            attend_copy(at, 2, SC)
            attend_exp(at, 3)
            act.wait_ge(o_summed.sem, o_summed.upto(at, 1))
            act.activation(o_rn[:].rearrange("p (b h) q -> p b (h q)", b=2), ps[:, AUX:AUX + 2, :], ACT.Sqrt,
                           bias=eps[:, 0:1], scale=1.0 / P).then_inc(o_rooted.sem, 1)
            attend_copy(at, 3, SC)
            act.wait_ge(o_gated.sem, o_gated.upto(at, 1))
            copy(y2[:, WC:KC, 0], o_t[:]).then_inc(o_hi.sem, 1)
            attend_hi(at, 0, y2[:, 0:WC], SC)
            for j in range(4):
                split(at, so.slot0 + j + LEAD, 0, SLOT)
                square(at, 0, 2 * j, hm[:, 2 * j])
                square(at, 0, 2 * j + 1, hm[:, 2 * j + 1])
            root(at, 1)
            for c in range(KC):
                square(at, 1, c, x[:, c])
            root(at, 2)
            split_xn(at, 2, 2)

            def gate_gelu(j, g):
                st = st2["gu"]
                i = j + 4 * g
                taps(at, st, j, 0, up_w[:, layer, i, 2:3], 12, up_b[:, layer, bass.ds(i, 1)], g)
                taps(at, st, j, 1, up_w[:, layer, i + FC, 2:3], 12, up_b[:, layer, bass.ds(i + FC, 1)], g)
                act.wait_ge(conv_ok.sem, conv_ok.upto(at, 30 + 3 * j + 3 + 12 * g))
                act.activation(silu_gate[:, j % 2], conv[:, j % 2, 0], ACT.Gelu_apprx_tanh).then_inc(gate_ok.sem, 1)

            act.activation(warm[:], eps[:], ACT.Gelu_apprx_tanh)
            rounds(act, at, st2["gu"], SLOT_DOWN, FC, 1, split, gate_gelu)
            squares_of_down(at, st2["down"], 2, hm, SLOT)
            root(at, 3)
            for c in range(KC):
                square(at, 3, c, x[:, c])

    @block.vector
    def _(dve):
        dve.sem_inc(lo.sem, RAW_RING)
        dve.sem_inc(drained.sem, 2)
        dve.sem_inc(x_new.sem, 2)

        def split(at, k, g, elems):
            r = k % RING
            dve.wait_ge(hi.sem, hi.upto(at, k + 1 + 4 * g))
            dve.tensor_tensor(w_lo[:, r, 0:elems], raw[:, k % RAW_RING, 0:elems], w_hi[:, r, 0:elems],
                              ALU.subtract).then_inc(lo.sem, 1)

        def inverse(at, k):
            dve.wait_ge(rooted.sem, rooted.upto(at, k + 1))
            dve.reciprocal(rstd[:], rms[:]).then_inc(rstd_ok.sem, 1)
            dve.wait_ge(rstd_ok.sem, rstd_ok.upto(at, k + 1))

        def normed(at, k, kv, src, gain):
            inverse(at, k)

            def low(c):
                dve.wait_ge(xn_hi.sem, xn_hi.upto(at, KC * (k if at[0] == 1 else k // 2) + c + 1))
                dve.tensor_tensor(xn[:, c, 1], v[:, c], xn[:, c, 0], ALU.subtract).then_inc(xn_lo_even.sem, 1)

            for c in range(KC):
                dve.scalar_tensor_tensor(v[:, c], src[:, c], gain(c), rstd[:], ALU.mult, ALU.mult)\
                   .then_inc(v_ok.sem, 1)
                if c >= 2 and c % 2 == 0:
                    low(c - 2)
            low(KC - 2)

        def gated(at, st, gk, hk):
            def body(j, g):
                dve.wait_ge(gate_ok.sem, gate_ok.upto(at, gk + j + 1 + 4 * g))
                slot_done(dve, at, st, j, g)
                dve.wait_ge(h_lo.sem, h_lo.upto(at, hk + j - 1 + 4 * g))
                dve.tensor_tensor(hv[:, j % 2], silu_gate[:, j % 2], ps[:, 2 * (j % 2) + 1, 0:T], ALU.mult)\
                   .then_inc(drained.sem, 1)
            return body

        def residual(at, st):
            def body(j, g):
                slot_done(dve, at, st, 2 * j + 1, g)
                f = j + 2 * g
                dve.scalar_tensor_tensor(x[:, f], ps[:, 2 * (j % 2), 0:T], 0.5, x[:, f], ALU.mult, ALU.add)\
                   .then_inc(x_new.sem, 1)
            return body

        def rope(eng, signal, at, done, raw_v, out, tmp, cos, sin, n_heads, half):
            shape = [P, NT, n_heads, HD]
            part = [P, NT, n_heads, half]
            c = cos[:].unsqueeze(2).broadcast_to(shape)
            eng.tensor_tensor(out, raw_v, c, ALU.mult).then_inc(signal.sem, 1)
            for i in range(2):
                s = sin[:, :, i * half:(i + 1) * half].unsqueeze(2).broadcast_to(part)
                o = (1 - i) * half
                eng.tensor_tensor(tmp[:, :, :, i * half:(i + 1) * half], raw_v[:, :, :, o:o + half], s,
                                  ALU.mult).then_inc(signal.sem, 1)
            eng.wait_ge(signal.sem, signal.upto(at, done + 3))
            eng.tensor_tensor(out[:, :, :, 0:2 * half], out[:, :, :, 0:2 * half], tmp[:, :, :, 0:2 * half],
                              ALU.add).then_inc(signal.sem, 1)

        def attend_mask(at, u, bias):
            t, _ = UNITS[u]
            kl = P * (t + 1)
            dve.wait_ge(scores.sem, scores.upto(at, u + 1))
            if u >= 2:
                dve.wait_ge(p_turned.sem, p_turned.upto(at, TURNS[u - 2]))
            b = bias.unsqueeze(1).broadcast_to([P, 2, kl])
            for a in range(2):
                dve.scalar_tensor_tensor(soft_view(u % 2, kl)[:, a], sc_view(kl)[:, a], float(HD) ** -0.5, b,
                                         ALU.mult, ALU.add).then_inc(masked.sem, 1)
            dve.wait_ge(masked.sem, masked.upto(at, 2 * u + 2))
            dve.tensor_reduce(neg_max[:, u % 2], soft[:, u % 2, :, 0:kl], AX.X, ALU.max, negate=True)\
               .then_inc(max_ok.sem, 1)

        def attend_norm(at, u, bank=AUX):
            t, g = UNITS[u]
            dve.wait_ge(probs.sem, probs.upto(at, GROUP * (u + 1)))
            dve.reciprocal(z_inv[:, u], z_sum[:, u]).then_inc(zi.sem, 1)
            dve.wait_ge(zi.sem, zi.upto(at, u + 1))
            dve.wait_ge(pv.sem, pv.upto(at, u + 1))
            z = z_inv[:, u].rearrange("p (a b) -> p b a", a=2).unsqueeze(3).broadcast_to([P, 2, 2, HD])
            view = "p (b a d) -> p b a d"
            dve.tensor_tensor(att[:, t, g * 256:(g + 1) * 256].rearrange(view, a=2, d=HD),
                              ps[:, bank + 1, 0:256].rearrange(view, a=2, d=HD), z, ALU.mult)\
               .then_inc(att_ok.sem, 1)

        def attend_lo(at, t, dst, bank=AUX):
            dve.wait_ge(yb_hi.sem, yb_hi.upto(at, 2 - t))
            lane = slice(t * P, (t + 1) * P)
            dve.tensor_tensor(dst[:, :, 1, lane], ps[:, bank, :].rearrange("p (c q) -> p c q", c=WC),
                              dst[:, :, 0, lane], ALU.subtract).then_inc(yb_lo.sem, 1)

        def index_sum(at, u):
            t, g = UNITS[u]
            kl = P * (t + 1)
            dve.wait_ge(relu_ok.sem, relu_ok.upto(at, u + 1))
            w_t = work[:, t, 0:kl]
            for k in range(GROUP):
                hh = 2 * (k % 2) + k // 2
                n = GROUP * u + k
                if n:
                    dve.wait_ge(idx_sum.sem, idx_sum.upto(at, n))
                acc = causal[:, T - kl:T] if g == 0 and k == 0 else w_t
                dve.scalar_tensor_tensor(w_t, soft[:, u % 2, k, 0:kl], w_idx[:, t, GROUP * g + hh:GROUP * g + hh + 1],
                                         acc, ALU.mult, ALU.add).then_inc(idx_sum.sem, 1)

        def top_k(at, i):
            t = UNITS[2 * i][0]
            kl = P * (t + 1)
            w_t = work[:, t, 0:kl]
            dve.wait_ge(idx_sum.sem, idx_sum.upto(at, 8 * (i + 1)))
            dve.sem_inc(held.sem, 1)
            for r in range(TOPK // 8):
                n = 2 * (TOPK // 8 * i + r)
                if n:
                    dve.wait_ge(top8.sem, top8.upto(at, n))
                    dve.sem_inc(held.sem, 1)
                dve.max(best8[:], w_t).then_inc(top8.sem, 1)
                dve.wait_ge(top8.sem, top8.upto(at, n + 1))
                dve.sem_inc(held.sem, 1)
                dve.match_replace(w_t, best8[:], w_t, TAKEN).then_inc(top8.sem, 1)
            dve.wait_ge(top8.sem, top8.upto(at, 16 * (i + 1)))
            dve.tensor_scalar(w_t, w_t, TAKEN / 2, NEG, ALU.is_gt, ALU.mult).then_inc(bias_ok.sem, 1)
            dve.wait_ge(bias_ok.sem, bias_ok.upto(at, 2 * i + 1))
            dve.tensor_tensor(w_t, w_t, causal[:, T - kl:T], ALU.add).then_inc(bias_ok.sem, 1)
            dve.wait_ge(bias_ok.sem, bias_ok.upto(at, 2 * i + 2))

        dve.wait_ge(ready.sem, 16 * N_TABLES)
        for k in range(LEAD):
            split((1, 0), k, 0, SLOT)
        with layers(dve) as layer:
            at = (1, layer)

            def ffn(k, gu, dn, hk):
                normed(at, k, k, x, lambda c: gains1[:, layer, k, c:c + 1])
                rounds(dve, at, gu, dn.elems, FC, 1, split, gated(at, gu, hk, hk))
                rounds(dve, at, dn, SLOT, KC, 2, split, residual(at, dn))

            ffn(0, st1["gu1"], st1["down1"], 0)
            normed(at, 1, 1, x, lambda c: gains1[:, layer, 1, c:c + 1])
            si = st1["in"]
            for k in range(20):
                split(at, si.slot0 + k + LEAD, 0, SLOT)
                if k == 0:
                    dve.wait_ge(sm_split.sem, sm_split.upto(at, 1))
                    dve.tensor_tensor(sm_lo[:], sm_raw[:], sm_hi[:], ALU.subtract).then_inc(sm_split.sem, 1)
                if k == 1:
                    dve.wait_ge(projected.sem, projected.upto(at, 2))
                    rope(dve, idx_roped, at, 0, heads(tok[:, QI]), heads(roped[:, 0]),
                         heads(soft[:, 0].rearrange("p a k -> p (a k)").rearrange("p (t n) -> p t n", t=NT)),
                         cos1, sin1, NH, HD // 2)
                if k == 2:
                    dve.wait_ge(small_out.sem, small_out.upto(at, 1))
                    kis = ki_wi[:, :, 0:HD].unsqueeze(2).broadcast_to([P, NT, 2, HD])
                    tmp = soft[:, 1, 0, 0:2 * NT * HD].rearrange("p (t a d) -> p t a d", t=NT, a=2)
                    rope(dve, idx_roped, at, 4, kis, ki_rope[:], tmp, cos1, sin1, 2, HD // 2)
                    dve.tensor_scalar(w_idx[:], ki_wi[:, :, HD:HD + NH], float(HD) ** -0.5 * float(NH) ** -0.5,
                                      None, ALU.mult).then_inc(w_idx_ok.sem, 1)
                    dve.wait_ge(w_idx_ok.sem, w_idx_ok.upto(at, 1))
                if k == 4:
                    index_sum(at, 0)
                if k == 5:
                    index_sum(at, 1)
                    top_k(at, 0)
                if k == 6:
                    index_sum(at, 2)
                if k == 7:
                    index_sum(at, 3)
                    top_k(at, 1)
                if k == 9:
                    attend_mask(at, 0, work[:, 1, 0:T])
                if k == 10:
                    attend_mask(at, 1, work[:, 1, 0:T])
                if k == 11:
                    attend_norm(at, 0)
                if k == 12:
                    attend_norm(at, 1)
                    attend_mask(at, 2, work[:, 0, 0:P])
                if k == 13:
                    attend_lo(at, 1, yb)
                    attend_mask(at, 3, work[:, 0, 0:P])
                if k == 14:
                    attend_norm(at, 2)
                    dve.wait_ge(projected.sem, projected.upto(at, 10))
                    for t in range(NT):
                        dve.bn_stats(ln_raw[:, t], tok[:, VA, t]).then_inc(ln_stats.sem, 1)
                    dve.wait_ge(ln_stats.sem, ln_stats.upto(at, 2))
                    dve.sem_inc(held.sem, 1)
                    for t in range(NT):
                        dve.bn_aggr(ln_mv[:, t], ln_raw[:, t]).then_inc(ln_stats.sem, 1)
                if k == 15:
                    attend_norm(at, 3)
                    dve.wait_ge(ln_rooted.sem, ln_rooted.upto(at, 1))
                    dve.reciprocal(ln_rstd[:], ln_root[:]).then_inc(ln_inv.sem, 1)
                    dve.wait_ge(ln_inv.sem, ln_inv.upto(at, 1))
                    for t in range(NT):
                        dve.tensor_scalar(tok[:, VA, t], tok[:, VA, t], ln_mv[:, t, 0:1], ln_rstd[:, t:t + 1],
                                          ALU.subtract, ALU.mult).then_inc(ln_norm.sem, 1)
                if k == 16:
                    attend_lo(at, 0, yb)
                if k in (17, 18):
                    n = k - 17
                    lane = slice(n * P, (n + 1) * P)
                    dve.wait_ge(mixed.sem, mixed.upto(at, n + 1))
                    dve.tensor_tensor(mix_b[:, n], ps[:, AUX + 1, :], rows[:, 2], ALU.add).then_inc(mix_ok.sem, 1)
                    dve.wait_ge(mix_ok.sem, mix_ok.upto(at, n + 1))
                    dve.tensor_tensor(ya_v[:, n].rearrange("p (c q) -> p c q", c=WC),
                                      mix_b[:, n].rearrange("p (c q) -> p c q", c=WC), u_t[:, :, lane],
                                      ALU.mult).then_inc(ya_ok.sem, 1)
            for name in ("pb", "pa"):
                st = st1[name]
                for j in range(2):
                    split(at, st.slot0 + j + LEAD, 0, SLOT)
                    for f in range(4):
                        c = 4 * j + f
                        tile_done(dve, at, st, j, f)
                        src = ps[:, 2 * ((c // 2) % 2) + f % 2, 0:T]
                        gate = gates[:, c + (KC if name == "pb" else 0)]
                        if c == 0:
                            dve.wait_ge(gate_sig.sem, gate_sig.upto(at, 1 if name == "pb" else 2))
                        dst = gate if name == "pb" else v[:, c]
                        ins = dve.tensor_tensor(dst, src, gate, ALU.mult)
                        if f % 2:
                            ins.then_inc(drained.sem, 1)
                        else:
                            ins.then_inc(merge_even.sem, 1)
                        if name == "pa":
                            if f % 2:
                                dve.wait_ge(drained.sem, drained.upto(at, st.free0 + c // 2 + 1))
                            else:
                                dve.wait_ge(merge_even.sem, merge_even.upto(at, 4 + c // 2 + 1))
                            dve.tensor_tensor(v[:, c], v[:, c], gates[:, KC + c], ALU.add).then_inc(merge.sem, 1)
            so = st1["out"]
            for j in range(4):
                split(at, so.slot0 + j + LEAD, 0, SLOT)
                for f in range(2):
                    c = 2 * j + f
                    tile_done(dve, at, so, j, f)
                    dve.tensor_tensor(x[:, c], x[:, c], ps[:, 2 * (j % 2) + f, 0:T], ALU.add)\
                       .then_inc(x_new.sem, 1)
            ffn(2, st1["gu2"], st1["down2"], FC)
        inverse(END1, 0)
        for c in range(KC):
            dve.scalar_tensor_tensor(x[:, c], x[:, c], gain_mid[:, c:c + 1], rstd[:], ALU.mult, ALU.mult)\
               .then_inc(x_new.sem, 1)
        if only_first:
            return
        with layers(dve) as layer:
            at = (2, layer)
            sq, ss, so = st2["qkv"], st2["side"], st2["out"]

            def four(t):
                return t.rearrange("p h q -> p (h q)")

            def bank4(b):
                return ps[:, b, :].rearrange("p (h q) -> p h q", h=DN_H)

            def over_heads(m):
                return m.unsqueeze(1).broadcast_to([P, DN_H, P])

            def over_cols(m):
                return m.unsqueeze(2).broadcast_to([P, DN_H, P])

            def taps(st, j, g, w, taps0, conv0, last_tap):
                n_early = 2 * (last_tap - 1) + 1
                for s in range(1, last_tap + 1):
                    for f in range(2):
                        k = 2 * (s - 1) + f
                        if k < 2:
                            dve.wait_ge(tap.sem, tap.upto(at, taps0 + 2 * j + f + 1 + 8 * g))
                        else:
                            dve.wait_ge(conv_ok.sem, conv_ok.upto(at, conv0 + n_early * j + k - 1 + 4 * n_early * g))
                        c = conv[:, j % 2, f, s:T]
                        ins = dve.scalar_tensor_tensor(c, ps[:, 2 * (j % 2) + f, 0:T - s], w(f, last_tap - s), c,
                                                       ALU.mult, ALU.add)
                        if k == n_early:
                            ins.then_inc(drained.sem, 1)
                        else:
                            ins.then_inc(conv_ok.sem, 1)

            def decays():
                a = ba[:, :, DN_H:2 * DN_H]
                rows_b = decay_rows[:, layer, 0].unsqueeze(1).broadcast_to([P, NT, DN_H])
                dve.wait_ge(small_out.sem, small_out.upto(at, 1))
                dve.tensor_tensor(dec_t[:], a, rows_b, ALU.add).then_inc(dec_in.sem, 1)
                dve.wait_ge(dec_in.sem, dec_in.upto(at, 1))
                dve.scalar_tensor_tensor(dec_n[:], dec_t[:], -1.0, dec_t[:], ALU.mult, ALU.min)\
                   .then_inc(dec_in.sem, 1)
                dve.wait_ge(beta_exp.sem, beta_exp.upto(at, 1))
                dve.tensor_scalar(beta_e[:], beta_e[:], 1.0, None, ALU.add).then_inc(beta_ok.sem, 1)
                dve.wait_ge(beta_ok.sem, beta_ok.upto(at, 1))
                dve.reciprocal(beta[:], beta_e[:]).then_inc(beta_ok.sem, 1)
                dve.wait_ge(dec_ln.sem, dec_ln.upto(at, 1))
                dve.scalar_tensor_tensor(dec_g[:], dec_t[:], 0.0, dec_n[:], ALU.max, ALU.add)\
                   .then_inc(dec_ok.sem, 1)
                dve.wait_ge(dec_ok.sem, dec_ok.upto(at, 1))
                dve.scalar_tensor_tensor(dec_g[:], dec_g[:], -1.0, a_exp[:].unsqueeze(1).broadcast_to([P, NT, DN_H]),
                                         ALU.mult, ALU.mult).then_inc(dec_ok.sem, 1)

            def decay_in(t):
                dve.wait_ge(g_rows.sem, g_rows.upto(at, t + 1))
                dve.tensor_tensor(beta_s[:, t], bank4(AUX + 1), over_heads(strict[:]), ALU.mult)\
                   .then_inc(beta_out.sem, 1)
                if t == 0:
                    dve.wait_ge(g_last_ok.sem, g_last_ok.upto(at, 1))
                else:
                    dve.wait_ge(qg_e.sem, qg_e.upto(at, 1))
                dve.tensor_tensor(gam[:, t], bank4(AUX), over_heads(mask_t[:]), ALU.add).then_inc(gam_in.sem, 1)
                if t == 0:
                    dve.tensor_tensor(k_scale[:], g_last[:], g_neg[:, 0], ALU.add).then_inc(k_exp_in.sem, 1)
                else:
                    dve.wait_ge(w_exp.sem, w_exp.upto(at, 1))
                    dve.tensor_tensor(w_scale[:], w_scale[:], beta[:, 1], ALU.mult).then_inc(w_scale_ok.sem, 1)

            def unit(i):
                dst = (dn_k, dn_q)[i]
                dve.wait_ge(dn_rooted.sem, dn_rooted.upto(at, i + 1))
                dve.reciprocal(four(dn_rn[:]), four(dn_rn[:])).then_inc(dn_inv.sem, 1)
                dve.wait_ge(dn_inv.sem, dn_inv.upto(at, i + 1))
                dve.scalar_tensor_tensor(four(dst[:]), four(dst[:]), float(P) ** -0.5 if i else 1.0, four(dn_rn[:]),
                                         ALU.mult, ALU.mult).then_inc(dn_unit.sem, 1)

            def scaled(n, dst, scale, bank):
                dve.wait_ge(dn_turned.sem, dn_turned.upto(at, n))
                dve.tensor_tensor(dst, bank4(bank), over_cols(scale), ALU.mult).then_inc(dn_scaled.sem, 1)

            def grams_in(t):
                dve.wait_ge(gam_ok.sem, gam_ok.upto(at, t + 1))
                dve.wait_ge(grams.sem, grams.upto(at, 2 * t + 1))
                dve.tensor_tensor(a_t[:, t], bank4(AUX), gam[:, t], ALU.mult).then_inc(a_raw.sem, 1)
                dve.wait_ge(grams.sem, grams.upto(at, 2 * t + 2))
                dve.tensor_tensor(qk[:, t], bank4(AUX + 1), gam[:, t], ALU.mult).then_inc(qk_ok.sem, 1)
                dve.wait_ge(a_raw.sem, a_raw.upto(at, t + 1))
                dve.tensor_tensor(a_t[:, t], a_t[:, t], beta_s[:, t], ALU.mult).then_inc(a_ok.sem, 1)

            def level_t(n):
                for t in range(NT):
                    dve.wait_ge(lt.sem, lt.upto(at, 2 * (n - 1) + t + 1))
                    dve.tensor_tensor(four(t_inv[:, t]), four(t_inv[:, t]), ps[:, AUX + t, :], ALU.subtract)\
                       .then_inc(t_ok.sem, 1)

            def level_u(n):
                for t in range(NT):
                    dve.wait_ge(lu.sem, lu.upto(at, 2 * (n - 1) + t + 1))
                    dve.tensor_tensor(four(u_inv[:, t]), four(u_inv[:, t]), ps[:, AUX + t, :], ALU.subtract)\
                       .then_inc(u_ok.sem, 1)

            def reach_of(kl):
                return reach[:, T - kl:T]

            normed(at, 0, 0, x, lambda c: gains2[:, layer, 0, c:c + 1])
            for k in range(6):
                split(at, sq.slot0 + k + LEAD, 0, SLOT)
                if k == 0:
                    dve.wait_ge(ba_split.sem, ba_split.upto(at, 1))
                    dve.tensor_tensor(ba_lo[:], ba_raw[:, layer], ba_hi[:], ALU.subtract).then_inc(ba_split.sem, 1)
                if k == 4:
                    unit(0)
                if k == 5:
                    unit(1)
                taps(sq, k, 0, lambda f, n: conv_w[:, layer, 2 * k + f, n:n + 1], 0, 0, N_CONV - 1)
                if k == 2:
                    decays()
                if k == 3:
                    decay_in(0)
                if k == 4:
                    decay_in(1)
                if k == 5:
                    scaled(1, k_dec[:], k_scale[:], AUX)
                    scaled(2, rhs_w[:], w_scale[:], AUX + 1)
            for k in range(8):
                split(at, ss.slot0 + k + LEAD, 0, SLOT)
                if k == 0:
                    grams_in(0)
                    dve.wait_ge(qg_e.sem, qg_e.upto(at, 1))
                    dve.tensor_tensor(qg[:], qg[:], dn_q[:, :, P:T], ALU.mult).then_inc(qg_ok.sem, 1)
                if k == 1:
                    grams_in(1)
                if k in (3, 4, 5, 6, 7):
                    level_u(k - 2)
                if k == 0:
                    scaled(3, rhs_v[:, 0], beta[:, 0], AUX)
                    scaled(4, rhs_v[:, 1], beta[:, 1], AUX + 1)
                if k in (2, 3, 4, 5, 6):
                    level_t(k - 1)
                if k == 5:
                    attend_mask(at, 0, reach_of(T))
                if k == 7:
                    attend_norm(at, 0, SC)
                    level_u(LEVELS - 1)
            attend_mask(at, 1, reach_of(T))
            attend_norm(at, 1, SC)
            attend_lo(at, 1, y2[:, 0:WC], SC)
            attend_mask(at, 2, reach_of(P))
            attend_norm(at, 2, SC)
            attend_mask(at, 3, reach_of(P))
            dve.wait_ge(o_rooted.sem, o_rooted.upto(at, 1))
            dve.reciprocal(four(o_rn[:]), four(o_rn[:])).then_inc(o_inv.sem, 1)
            dve.wait_ge(o_inv.sem, o_inv.upto(at, 1))
            dve.scalar_tensor_tensor(four(o_t[:]), four(o_t[:]), dn_gain[:, layer], four(o_rn[:]), ALU.mult,
                                     ALU.mult).then_inc(o_norm.sem, 1)
            dve.wait_ge(o_norm.sem, o_norm.upto(at, 1))
            dve.tensor_tensor(four(o_t[:]), four(o_t[:]), four(z_t[:]), ALU.mult).then_inc(o_gated.sem, 1)
            attend_norm(at, 3, SC)
            attend_lo(at, 0, y2[:, 0:WC], SC)
            for j in range(4):
                split(at, so.slot0 + j + LEAD, 0, SLOT)
                for f in range(2):
                    tile_done(dve, at, so, j, f)
                    dve.tensor_copy(hm[:, 2 * j + f], ps[:, 2 * (j % 2) + f, 0:T]).then_inc(x_new.sem, 1)

            def post(k):
                inverse(at, k)
                for c in range(KC):
                    dve.scalar_tensor_tensor(v[:, c], hm[:, c], gains2[:, layer, k, c:c + 1], rstd[:], ALU.mult,
                                             ALU.mult).then_inc(v_ok.sem, 1)
                    if c:
                        dve.wait_ge(v_ok.sem, v_ok.upto(at, KC * k + c))
                        dve.tensor_tensor(x[:, c - 1], x[:, c - 1], v[:, c - 1], ALU.add).then_inc(x_new.sem, 1)
                dve.wait_ge(v_ok.sem, v_ok.upto(at, KC * k + KC))
                dve.tensor_tensor(x[:, KC - 1], x[:, KC - 1], v[:, KC - 1], ALU.add).then_inc(x_new.sem, 1)

            post(1)
            normed(at, 2, 2, x, lambda c: gains2[:, layer, 2, c:c + 1])

            def gated2(j, g):
                i = j + 4 * g
                taps(st2["gu"], j, g, lambda f, n: up_w[:, layer, i + FC * f, n:n + 1], 12, 30, 2)
                dve.wait_ge(gate_ok.sem, gate_ok.upto(at, i + 1))
                dve.wait_ge(drained.sem, drained.upto(at, st2["gu"].free0 + i + 1))
                dve.wait_ge(h_lo.sem, h_lo.upto(at, i - 1))
                dve.tensor_tensor(hv[:, j % 2], silu_gate[:, j % 2], conv[:, j % 2, 1], ALU.mult)\
                   .then_inc(hv_ok.sem, 1)

            rounds(dve, at, st2["gu"], SLOT_DOWN, FC, 1, split, gated2)

            def out_of_down(j, g):
                f = j + 2 * g
                slot_done(dve, at, st2["down"], 2 * j + 1, g)
                dve.tensor_copy(hm[:, f], ps[:, 2 * (j % 2), 0:T]).then_inc(x_new.sem, 1)

            rounds(dve, at, st2["down"], SLOT, KC, 2, split, out_of_down)
            post(3)

    @block.gpsimd
    def _(pool):
        pool.sem_inc(h_lo.sem, 2)

        def add_squares(at, k, chunks=range(1, KC), body=None):
            for c in chunks:
                pool.wait_ge(squared.sem, squared.upto(at, KC * k + c + 1))
                if c > 1:
                    pool.wait_ge(summed.sem, summed.upto(at, 7 * k + c - 1))
                pool.tensor_tensor(ssum[:], ssum[:], sqb[:, c % 2], ALU.add).then_inc(summed.sem, 1)

        def low_odd(at, k):
            for c in range(1, KC, 2):
                pool.wait_ge(xn_hi.sem, xn_hi.upto(at, KC * k + c + 1))
                pool.tensor_tensor(xn[:, c, 1], v[:, c], xn[:, c, 0], ALU.subtract).then_inc(xn_lo_odd.sem, 1)

        def split_h(at, ready_sig, base, hk):
            def body(j, g):
                i = j + 4 * g
                pool.wait_ge(ready_sig.sem, ready_sig.upto(at, base + i + 1))
                pool.sem_inc(held.sem, 1)
                pool.tensor_copy(h[:, i, 0], hv[:, j % 2]).then_inc(h_hi.sem, 1)
                pool.wait_ge(h_hi.sem, h_hi.upto(at, hk + i + 1))
                pool.tensor_tensor(h[:, i, 1], hv[:, j % 2], h[:, i, 0], ALU.subtract).then_inc(h_lo.sem, 1)
            cycle(pool, FC, 4, body)

        def rope(signal, at, done, raw_v, out, tmp, cos, sin, half):
            shape = [P, NT, NH, HD]
            part = [P, NT, NH, half]
            pool.tensor_tensor(out, raw_v, cos[:].unsqueeze(2).broadcast_to(shape), ALU.mult).then_inc(signal.sem, 1)
            for i in range(2):
                s = sin[:, :, i * half:(i + 1) * half].unsqueeze(2).broadcast_to(part)
                o = (1 - i) * half
                pool.tensor_tensor(tmp[:, :, :, i * half:(i + 1) * half], raw_v[:, :, :, o:o + half], s,
                                   ALU.mult).then_inc(signal.sem, 1)
            pool.wait_ge(signal.sem, signal.upto(at, done + 3))
            pool.tensor_tensor(out[:, :, :, 0:2 * half], out[:, :, :, 0:2 * half], tmp[:, :, :, 0:2 * half],
                               ALU.add).then_inc(signal.sem, 1)

        pool.wait_ge(ready.sem, 16 * N_TABLES)
        for c in range(1, KC):
            pool.wait_ge(squared.sem, c + 1)
            if c > 1:
                pool.wait_ge(summed.sem, c - 1)
            pool.tensor_tensor(ssum[:], ssum[:], sqb[:, c % 2], ALU.add).then_inc(summed.sem, 1)
        with layers(pool) as layer:
            at = (1, layer)
            low_odd(at, 0)
            split_h(at, drained, st1["gu1"].free0, 0)
            add_squares(at, 0)
            low_odd(at, 1)
            pool.wait_ge(params.sem, params.upto(at, 48))
            pool.tensor_tensor(ws_m[:], ws_raw[:], tri_ts[:].unsqueeze(1).broadcast_to([P, WC, P]), ALU.mult)\
                .then_inc(ws_ok.sem, 1)
            pool.wait_ge(projected.sem, projected.upto(at, 4))
            rope(qk_roped, at, 0, heads(tok[:, Q]), heads(roped[:, 1]), heads(rope_tmp[:]), cos1, sin1, HD // 2)
            pool.wait_ge(projected.sem, projected.upto(at, 6))
            pool.wait_ge(turned.sem, turned.upto(at, 2))
            pool.wait_ge(qk_roped.sem, qk_roped.upto(at, 4))
            rope(qk_roped, at, 4, heads(tok[:, K]), heads(roped[:, 0]), heads(rope_tmp[:]), cos1, sin1, HD // 2)
            for t in range(NT):
                pool.wait_ge(ln_norm.sem, ln_norm.upto(at, t + 1))
                pool.tensor_tensor(tok[:, VA, t], tok[:, VA, t], rows[:, 0], ALU.mult).then_inc(ln_ok.sem, 1)
                pool.wait_ge(ln_ok.sem, ln_ok.upto(at, 2 * t + 1))
                pool.tensor_tensor(tok[:, VA, t], tok[:, VA, t], rows[:, 1], ALU.add).then_inc(ln_ok.sem, 1)
            for n in range(NT):
                lane = slice(n * P, (n + 1) * P)
                pool.wait_ge(ya_hi.sem, ya_hi.upto(at, n + 1))
                pool.tensor_tensor(ya[:, :, 1, lane], ya_v[:, n].rearrange("p (c q) -> p c q", c=WC),
                                   ya[:, :, 0, lane], ALU.subtract).then_inc(ya_lo.sem, 1)
            for c in range(KC):
                pool.wait_ge(m_hi.sem, m_hi.upto(at, c + 1))
                pool.tensor_tensor(m[:, c, 1], v[:, c], m[:, c, 0], ALU.subtract).then_inc(m_lo.sem, 1)
            add_squares(at, 1)
            low_odd(at, 2)
            split_h(at, drained, st1["gu2"].free0, FC)
            add_squares(at, 2)
        add_squares(END1, 0)
        if only_first:
            return
        with layers(pool) as layer:
            at = (2, layer)

            def over_heads(m):
                return m.unsqueeze(1).broadcast_to([P, DN_H, P])

            def over_cols(m):
                return m.unsqueeze(2).broadcast_to([P, DN_H, P])

            def level_c(n):
                for t in range(NT):
                    if n > 1:
                        pool.wait_ge(lp.sem, lp.upto(at, 2 * (n - 2) + t + 1))
                    pool.tensor_tensor(lev_c[:, t], a_t[:, t], over_heads(level_m[:, n]), ALU.mult)\
                        .then_inc(c_ok.sem, 1)

            low_odd(at, 0)
            pool.wait_ge(dec_ok.sem, dec_ok.upto(at, 2))
            for t in range(NT):
                if t:
                    pool.wait_ge(g_rows.sem, g_rows.upto(at, 1))
                pool.tensor_tensor(gb[:, 0], over_heads(tri_ts[:]), over_cols(dec_g[:, t]), ALU.mult)\
                    .then_inc(gb_ok.sem, 1)
                pool.tensor_tensor(gb[:, 1], over_heads(ident[:]), over_cols(beta[:, t]), ALU.mult)\
                    .then_inc(gb_ok.sem, 1)
            for t in range(NT):
                pool.wait_ge(a_ok.sem, a_ok.upto(at, t + 1))
                if t == 0:
                    pool.wait_ge(grams.sem, grams.upto(at, 4))
                pool.tensor_tensor(lev_c[:, t], a_t[:, t], over_heads(level_m[:, 0]), ALU.mult)\
                    .then_inc(u_first.sem, 1)
                pool.wait_ge(u_first.sem, u_first.upto(at, 2 * t + 1))
                pool.tensor_tensor(u_inv[:, t], over_heads(ident[:]), lev_c[:, t], ALU.subtract)\
                    .then_inc(u_first.sem, 1)
            pool.wait_ge(u_first.sem, u_first.upto(at, 4))
            level_c(1)
            pool.wait_ge(projected.sem, projected.upto(at, 2))
            rope(qk_roped, at, 0, heads(tok[:, Q]), heads(roped[:, 1]), heads(rope_tmp[:]), cos2, sin2, ROPE2 // 2)
            level_c(2)
            pool.wait_ge(projected.sem, projected.upto(at, 4))
            pool.wait_ge(qk_roped.sem, qk_roped.upto(at, 4))
            rope(qk_roped, at, 4, heads(tok[:, K]), heads(roped[:, 0]), heads(rope_tmp[:]), cos2, sin2, ROPE2 // 2)
            for n in range(3, LEVELS):
                level_c(n)
            pool.wait_ge(o_hi.sem, o_hi.upto(at, 1))
            pool.tensor_tensor(y2[:, WC:KC, 1], o_t[:], y2[:, WC:KC, 0], ALU.subtract).then_inc(o_lo.sem, 1)
            add_squares(at, 0)
            add_squares(at, 1)
            low_odd(at, 1)
            split_h(at, hv_ok, 0, 0)
            add_squares(at, 2)
            add_squares(at, 3)


def lay_out(inp):
    f = lambda a: np.ascontiguousarray(a)

    def slots(w, chunks, cols):
        l, _, n = w.shape
        return f(w.reshape(l, chunks, P, n // cols, cols).transpose(0, 3, 2, 1, 4)
                 .reshape(l, n // cols, P, chunks * cols))

    def gate_up(w):
        return f(w.reshape(DEPTH, KC, P, 2, FC, P).transpose(0, 4, 2, 1, 3, 5).reshape(DEPTH, FC, P, SLOT))

    def down(w):
        return f(w.reshape(DEPTH, 2, FC // 2, P, KC, P).transpose(0, 4, 1, 3, 2, 5)
                 .reshape(DEPTH, 2 * KC, P, SLOT_DOWN))

    def columns(g):
        g = g.reshape(*g.shape[:-1], -1, P)
        return f(np.moveaxis(g, -1, 0))

    w = inp["w_in"]
    cut = np.cumsum([W, W, W, W, W, W, HD, NH, D, D])
    u, va, q, k, vv, qi, ki, wi, ga, gb = np.split(w, cut[:-1], axis=-1)
    main = np.concatenate([qi, q, k, vv, va, u, ga, gb], axis=-1)
    side = np.concatenate([ki, wi], axis=-1)
    out = {
        "x": f(inp["x"][0].T.reshape(KC, P, T).transpose(1, 0, 2)),
        "gu1": gate_up(inp["ffn1_w_gu"]), "down1": down(inp["ffn1_w_down"]),
        "gu2": gate_up(inp["ffn2_w_gu"]), "down2": down(inp["ffn2_w_down"]),
        "in1": slots(main, KC, 256),
        "small1": f(side.reshape(DEPTH, KC, P, HD + NH).transpose(0, 2, 1, 3)),
        "pb1": slots(inp["w_pb"], WC, 512), "pa1": slots(inp["w_pa"], WC, 512),
        "out1": slots(inp["w_out"], KC, 256),
        "gains1": columns(np.stack([inp["ffn1_norm"], inp["mix_norm"], inp["ffn2_norm"]], 1)),
        "gain_mid": columns(inp["final_norm"]),
        "gate_bias": columns(inp["b_gate"]),
        "ws1": f(inp["gmlp_w_s"].transpose(0, 3, 1, 2)),
        "rows1": f(np.broadcast_to(np.stack([inp["gmlp_ln_g"], inp["gmlp_ln_b"],
                                             inp["gmlp_b_s"].reshape(DEPTH, W)], 1)[:, None],
                                   (DEPTH, P, 3, W))),
    }
    w = inp["w_in_2"]
    cut = np.cumsum([W, W, W, W, DN_H, DN_H, W, W, W])
    dq, dk, dv, z, b, a, bq, bk, bv = np.split(w, cut[:-1], axis=-1)
    taps_of = lambda c: f(np.moveaxis(c.reshape(DEPTH, c.shape[1], -1, P), (3, 0, 2, 1), (0, 1, 2, 3)))
    cq, ck, cv = np.split(inp["dn_conv_2"], 3, axis=-1)
    out.update({
        "in2": slots(np.concatenate([dk, dq, dv, bq, bk, bv, z], axis=-1), KC, 256),
        "small2": f(np.concatenate([b, a], axis=-1).reshape(DEPTH, KC, P, 2 * DN_H).transpose(2, 0, 1, 3)),
        "out2": slots(np.concatenate([inp["w_out_2"][:, W:], inp["w_out_2"][:, :W]], axis=1), KC, 256),
        "gu3": gate_up(inp["ffn_up_2"]), "down3": down(inp["ffn_down_2"]),
        "gains2": columns(np.stack([inp["pre_mix_norm_2"], inp["post_mix_norm_2"], inp["pre_ffn_norm_2"],
                                    inp["post_ffn_norm_2"]], 1)),
        "conv_w": taps_of(np.concatenate([ck, cq, cv], axis=-1)),
        "up_w": taps_of(inp["ffn_conv_2"]),
        "up_b": columns(inp["ffn_conv_bias_2"]),
        "decay_rows": f(np.broadcast_to(np.stack([inp["dn_dt_bias_2"], inp["dn_a_log_2"]], 1)[None],
                                        (P, DEPTH, 2, DN_H))),
        "dn_gain": columns(inp["dn_out_norm_2"]),
    })
    out.update(tables())
    return out


def tables():
    f = lambda a: np.ascontiguousarray(np.asarray(a, np.float32))

    def angles(theta, dim):
        inv = np.float32(theta) ** (-np.arange(0, dim, 2, dtype=np.float32) / np.float32(dim))
        ang = np.arange(T, dtype=np.float32)[:, None] * inv[None, :]
        return np.cos(ang), np.sin(ang)

    by_tile = lambda a: f(a.reshape(NT, P, -1).transpose(1, 0, 2))
    c, s = angles(10000.0, HD)
    p = np.arange(P)
    q = P + p[:, None]
    dist = q - np.arange(T)[None, :]
    c2, s2 = angles(500000.0, ROPE2)
    count = sum((dist >= 0) & (dist % dil == 0) & (dist <= window) for window, dil in DILATIONS)
    return {
        "ones_d": f(np.full((P, P), 1.0 / D)), "ident": f(np.eye(P)), "eps": f(np.full((P, 1), EPS)),
        "cos1": by_tile(np.concatenate([c, c], 1)), "sin1": by_tile(np.concatenate([-s, s], 1)),
        "causal": f(np.where(dist >= 0, 0.0, NEG)),
        "ones": f(np.ones((P, P))),
        "cos2": by_tile(np.concatenate([c2, c2, np.ones((T, HD - ROPE2), np.float32)], 1)),
        "sin2": by_tile(np.concatenate([-s2, s2], 1)),
        "reach": f(np.where(count > 0, np.log(np.maximum(count, 1)), NEG)),
        "mask_t": f(np.where(p[:, None] <= p[None, :], 0.0, NEG)),
        "strict": f(p[:, None] < p[None, :]),
        "level_m": f(np.stack([(p[None, :] // b % 2 == 1) & (p[:, None] // b == p[None, :] // b - 1)
                               for b in 2 ** np.arange(LEVELS)], 1)),
        "tri_ts": f(p[:, None] <= p[None, :]),
    }


def kernel(**inputs):
    import concourse.bacc as _bacc
    from concourse.bass_utils import run_bass_kernel_spmd as _run

    nc = _bacc.Bacc("TRN2", target_bir_lowering=False, num_devices=1)
    arrays, io = {}, {}
    for name, a in lay_out({name: np.asarray(a) for name, a in inputs.items()}).items():
        arrays[f"in_{name}_dram"] = a
        io[name] = nc.dram_tensor(f"in_{name}_dram", a.shape, mybir.dt.from_np(a.dtype), kind="ExternalInput").ap()
    io["out"] = nc.dram_tensor("out_dram", (P, KC, T), F32, kind="ExternalOutput").ap()
    with ExitStack() as ctx:
        program(nc, io, ctx)
    r = _run(nc, [arrays], core_ids=[0])
    return np.ascontiguousarray(r.results[0]["out_dram"].transpose(1, 0, 2).reshape(D, T).T)[None]
```

```python
from contextlib import ExitStack

import numpy as np

import concourse.bass as bass
from concourse import mybir

F32 = mybir.dt.float32
F32R = mybir.dt.float32r
ALU = mybir.AluOpType
ACT = mybir.ActivationFunctionType
AX = mybir.AxisListType

P = 128
DEPTH = 2
T = 256
NT = T // P
D = 1024
KC = D // P
D_FF = 2816
FC = D_FF // P
W = 512
WC = W // P
HD = 64
NH = W // HD
TOPK = 64
EPS = 1e-6
NEG = -1e30
TAKEN = -3e38
DN_H = 4
N_CONV = 4
ROPE2 = HD // 4
DILATIONS = ((128, 1), (512, 4), (2048, 16))
LEVELS = 7

SLOT = KC * 256
SLOT_DOWN = FC // 2 * P
RING = 4
RAW_RING = 2
LEAD = 2
BANKS = 4


N_INPUTS = 4
N_TABLES = 21


class Signal:

    def __init__(self, sem, per1, per2, pre=0, mid=0):
        self.sem, self.per1, self.per2, self.pre, self.mid = sem, per1, per2, pre, mid

    def upto(self, at, k):
        block, layer = at
        if block == 1:
            return layer * self.per1 + (self.pre + k)
        return layer * self.per2 + (self.pre + DEPTH * self.per1 + self.mid + k)


class Stage:

    def __init__(self, name, slots, elems, pairs, slot0, full0, early, free, free0, free_by):
        self.name, self.slots, self.elems, self.pairs = name, slots, elems, pairs
        self.slot0, self.full0, self.early = slot0, full0, early
        self.free, self.free0, self.free_by = free, free0, free_by


def plan(rows):
    stages, slot, full, freed = {}, 0, 0, {}
    for name, slots, elems, pairs, early, free, by, also in rows:
        stages[name] = Stage(name, slots, elems, pairs, slot, full, early, free, freed.get(free, 0), by)
        slot += slots
        full += slots * early
        freed[free] = freed.get(free, 0) + pairs * by + also
    return stages, slot, full, freed


PLAN1 = [
    ("gu1", FC, SLOT, FC, 1, "drained", 1, 0),
    ("down1", 2 * KC, SLOT_DOWN, KC, 0, "x_new", 1, 0),
    ("in", 20, SLOT, 20, 1, "projected", 1, 0),
    ("pb", 2, SLOT, 4, 3, "drained", 1, 0),
    ("pa", 2, SLOT, 4, 3, "drained", 1, 0),
    ("out", 4, SLOT, 4, 1, "x_new", 2, 0),
    ("gu2", FC, SLOT, FC, 1, "drained", 1, 0),
    ("down2", 2 * KC, SLOT_DOWN, KC, 0, "x_new", 1, 0),
]
PLAN2 = [
    ("qkv", 6, SLOT, 6, 1, "drained", 1, 0),
    ("side", 8, SLOT, 8, 1, "projected", 1, 0),
    ("out", 4, SLOT, 4, 1, "x_new", 2, KC),
    ("gu", FC, SLOT, FC, 1, "drained", 1, 0),
    ("down", 2 * KC, SLOT_DOWN, KC, 0, "x_new", 1, KC),
]
IN1 = {"u": 0, "va": W, "q": 2 * W, "k": 3 * W, "v": 4 * W, "qi": 5 * W, "ki": 6 * W}
QI, Q, K, V, VA = 0, 1, 2, 4, 5
UNITS = [(1, 0), (1, 1), (0, 0), (0, 1)]
TURNS = [2, 4, 5, 6]
GROUP = NH // 2

RAW_AT = 16 * 1024 + 128
HI_AT = RAW_AT + RAW_RING * SLOT * 4
LO_AT = HI_AT + RING * SLOT * 4
X_AT = LO_AT + RING * SLOT * 4
XN_AT = X_AT + KC * T * 4
FIXED_AT = XN_AT + 2 * KC * T * 4
KB = 1024


def cycle(eng, count, period, body):
    groups = count // period
    if groups > 1:
        with eng.Fori(0, groups) as g:
            for j in range(period):
                body(j, g)
    else:
        groups = 0
    for j in range(groups * period, count):
        body(j, 0)


def layers(eng):
    return eng.Fori(0, DEPTH)


def program(nc, io, ctx):
    cursor = [FIXED_AT]

    def at_byte(name, shape, offset, dtype=F32):
        return nc.alloc_sbuf_tensor_at(name, [P, *shape], dtype, offset=offset)

    def fixed(name, shape):
        t = at_byte(name, shape, cursor[0])
        cursor[0] += (int(np.prod(shape)) * 4 + 31) // 32 * 32
        return t

    raw = at_byte("raw", [RAW_RING, SLOT], RAW_AT)
    w_hi = at_byte("w_hi", [RING, SLOT], HI_AT, F32R)
    w_lo = at_byte("w_lo", [RING, SLOT], LO_AT, F32R)
    x = at_byte("x", [KC, T], X_AT)
    xn = at_byte("xn", [KC, 2, T], XN_AT, F32R)

    ssum = fixed("ssum", [T])
    sqb = fixed("sqb", [2, T])
    rms = fixed("rms", [T + NT])
    rstd = fixed("rstd", [T + NT])
    ones_d = fixed("ones_d", [P])
    ident = fixed("ident", [P])
    eps = fixed("eps", [2])
    warm = fixed("warm", [4])
    gains1 = fixed("gains1", [DEPTH * 3 + 1, KC])
    gate_bias = fixed("gate_bias", [DEPTH, 2 * KC])
    cos1 = fixed("cos1", [NT, HD])
    sin1 = fixed("sin1", [NT, HD])
    causal = fixed("causal", [2 * P])
    tri_ts = fixed("tri_ts", [P])
    ki_wi = fixed("ki_wi", [NT, HD + NH])
    w_idx = fixed("w_idx", [NT, NH])
    best8 = fixed("best8", [8])
    z_sum = fixed("z_sum", [4, GROUP])
    z_inv = fixed("z_inv", [4, GROUP])
    neg_max = fixed("neg_max", [2, GROUP])
    ln_raw = fixed("ln_raw", [NT, 6])
    ln_mv = fixed("ln_mv", [NT, 2])
    ln_root = fixed("ln_root", [NT])
    ln_rstd = fixed("ln_rstd", [NT])

    ones = fixed("ones", [P])
    ones_q = fixed("ones_q", [P])
    gains2 = fixed("gains2", [DEPTH * 4 + 1, KC])
    cos2 = fixed("cos2", [NT, HD])
    sin2 = fixed("sin2", [NT, ROPE2])
    reach = fixed("reach", [2 * P])
    conv_w = fixed("conv_w", [DEPTH, 3 * DN_H, N_CONV])
    up_w = fixed("up_w", [DEPTH, 2 * FC, 3])
    up_b = fixed("up_b", [DEPTH, 2 * FC])
    decay_rows = fixed("decay_rows", [DEPTH, 2, DN_H])
    dn_gain = fixed("dn_gain", [DEPTH, 1])
    mask_t = fixed("mask_t", [P])
    strict = fixed("strict", [P])
    level_m = fixed("level_m", [LEVELS, P])
    ba_raw = fixed("ba_raw", [DEPTH, KC, 2 * DN_H])
    ba = fixed("ba", [NT, 2 * DN_H])
    beta = fixed("beta", [NT, DN_H])
    beta_e = fixed("beta_e", [NT, DN_H])
    dec_t = fixed("dec_t", [NT, DN_H])
    dec_n = fixed("dec_n", [NT, DN_H])
    dec_e = fixed("dec_e", [NT, DN_H])
    dec_g = fixed("dec_g", [NT, DN_H])
    a_exp = fixed("a_exp", [DN_H])
    g_neg = fixed("g_neg", [NT, DN_H])
    g_last = fixed("g_last", [DN_H])
    k_scale = fixed("k_scale", [DN_H])
    k_ln = fixed("k_ln", [NT, DN_H])
    k_inv = fixed("k_inv", [NT, DN_H])
    k_bias = fixed("k_bias", [NT, DN_H])
    beta_k = fixed("beta_k", [NT, DN_H])
    q2 = fixed("q2", [NT, DN_H])
    w_scale = fixed("w_scale", [DN_H])

    area = (cursor[0] + 63) // 64 * 64
    h = at_byte("h", [FC, 2, T], area, F32R)
    silu_gate = at_byte("silu_gate", [2, T], area + 44 * KB)
    hv = at_byte("hv", [2, T], area + 46 * KB)
    v = at_byte("v", [KC, T], area + 53 * KB)
    tok = at_byte("tok", [6, NT, W], area)
    gates = at_byte("gates", [2 * KC, T], area)
    roped = at_byte("roped", [2, NT, W], area + 24 * KB)
    q_t = at_byte("q_t", [WC, T], area + 32 * KB)
    k_t = at_byte("k_t", [WC, T], area + 36 * KB)
    qi_t = at_byte("qi_t", [WC, T], area + 40 * KB)
    u_t = at_byte("u_t", [WC, T], area + 40 * KB)
    ki_t = at_byte("ki_t", [T], area + 44 * KB)
    soft = at_byte("soft", [2, GROUP, T], area + 45 * KB)
    p_t = at_byte("p_t", [2, GROUP, P], area + 24 * KB)
    rope_tmp = at_byte("rope_tmp", [NT, W], area + 53 * KB)
    mix_b = at_byte("mix_b", [NT, W], area + 53 * KB)
    ya_v = at_byte("ya_v", [NT, W], area + 57 * KB)
    att = at_byte("att", [NT, W], area + 28 * KB)
    work = at_byte("work", [NT, 2 * P], area + 61 * KB)
    ya = at_byte("ya", [WC, 2, T], area + 45 * KB, F32R)
    ws_raw = at_byte("ws_raw", [WC, P], area + 66 * KB)
    yb = at_byte("yb", [WC, 2, T], area + 63 * KB, F32R)
    ws_m = at_byte("ws_m", [WC, P], area + 71 * KB)
    rows = at_byte("rows", [3, W], area + 73 * KB)
    ki_rope = at_byte("ki_rope", [NT, 2, HD], area + 79 * KB)
    sm_raw = at_byte("sm_raw", [KC, HD + NH], area + 63 * KB)
    sm_hi = at_byte("sm_hi", [KC, HD + NH], area + 20 * KB, F32R)
    sm_lo = at_byte("sm_lo", [KC, HD + NH], area + 28 * KB, F32R)
    m = at_byte("m", [KC, 2, T], area + 24 * KB, F32R)

    conv = at_byte("conv", [2, 2, T], area + 48 * KB)
    conv_in = at_byte("conv_in", [2, 2, T], area + 57 * KB)
    sq8 = at_byte("sq8", [KC, T], area + 67 * KB)
    hm = at_byte("hm", [KC, T], area + 44 * KB)
    y2 = at_byte("y2", [KC, 2, T], area + 67 * KB, F32R)
    dn_k = at_byte("dn_k", [DN_H, T], area + 67 * KB)
    dn_q = at_byte("dn_q", [DN_H, T], area + 24 * KB)
    dn_v = at_byte("dn_v", [DN_H, T], area)
    z_t = at_byte("z_t", [DN_H, T], area)
    dn_sq = at_byte("dn_sq", [DN_H, T], area + 61 * KB)
    q_diag = at_byte("q_diag", [DN_H, T], area + 53 * KB)
    gb = at_byte("gb", [2, DN_H, P], area + 53 * KB)
    k_dec = at_byte("k_dec", [DN_H, P], area + 12 * KB)
    rhs_w = at_byte("rhs_w", [DN_H, P], area + 14 * KB)
    rhs_v = at_byte("rhs_v", [NT, DN_H, P], area + 20 * KB)
    a_t = at_byte("a_t", [NT, DN_H, P], area + 61 * KB)
    qk = at_byte("qk", [NT, DN_H, P], area + 40 * KB)
    qg = at_byte("qg", [DN_H, P], area + 65 * KB)
    gam = at_byte("gam", [NT, DN_H, P], area + 71 * KB)
    beta_s = at_byte("beta_s", [NT, DN_H, P], area + 75 * KB)
    u_inv = at_byte("u_inv", [NT, DN_H, P], area + 67 * KB)
    t_inv = at_byte("t_inv", [NT, DN_H, P], area + 57 * KB)
    lev_p = at_byte("lev_p", [NT, DN_H, P], area + 71 * KB)
    lev_c = at_byte("lev_c", [NT, DN_H, P], area + 75 * KB)
    w_neg = at_byte("w_neg", [DN_H, P], area + 75 * KB)
    state = at_byte("state", [DN_H, P], area + 77 * KB)
    v_new = at_byte("v_new", [NT, DN_H, P], area + 57 * KB)
    o_t = at_byte("o_t", [DN_H, T], area + 61 * KB)
    o_sq = at_byte("o_sq", [DN_H, T], area + 20 * KB)
    o_rn = at_byte("o_rn", [DN_H, T], area + 12 * KB)
    ba_hi = at_byte("ba_hi", [KC, 2 * DN_H], area + 20 * KB, F32R)
    ba_lo = at_byte("ba_lo", [KC, 2 * DN_H], area + 28 * KB, F32R)

    ps = ctx.enter_context(nc.psum_tensor("ps", [P, 8, 512], F32))
    SC, AUX = 4, 6

    st1, slots1, full1, freed1 = plan(PLAN1)
    st2, slots2, full2, freed2 = plan(PLAN2)

    def sig(name, per1, per2, pre=0, mid=0):
        return Signal(ctx.enter_context(nc.semaphore(name)), per1, per2, pre, mid)

    landed = [sig(f"landed{r}", 8 * slots1, 8 * slots2) for r in range(RAW_RING)]
    hi = sig("hi", slots1, slots2)
    lo = sig("lo", slots1, slots2, pre=RAW_RING)
    used = sig("used", slots1, slots2, pre=RING)
    full = sig("full", full1, full2)
    drained = sig("drained", freed1["drained"], freed2["drained"], pre=2)
    x_new = sig("x_new", 3 * KC, 4 * KC, pre=2, mid=KC)
    projected = sig("projected", 20, 8)
    squared = sig("squared", 3 * KC, 4 * KC, pre=KC, mid=KC)
    summed = sig("summed", 21, 21, pre=7, mid=7)
    mean_sq = sig("mean_sq", 3, 4, mid=1)
    rooted = sig("rooted", 3, 4, mid=1)
    rstd_ok = sig("rstd_ok", 3, 4, mid=1)
    v_ok = sig("v_ok", 3 * KC, 2 * KC, pre=KC, mid=KC)
    post_v = sig("post_v", 0, 2 * KC)
    xn_hi = sig("xn_hi", 3 * KC, 2 * KC, pre=KC)
    xn_lo_even = sig("xn_lo_even", 3 * KC // 2, KC, pre=KC // 2)
    xn_lo_odd = sig("xn_lo_odd", 3 * KC // 2, KC, pre=KC // 2)
    gate_ok = sig("gate_ok", 2 * FC, FC)
    h_hi = sig("h_hi", 2 * FC, FC)
    h_lo = sig("h_lo", 2 * FC, FC, pre=2)
    params = sig("params", 48, 0)
    inputs = sig("inputs", 0, 0)
    ready = sig("ready", 0, 0)
    small = sig("small", 1, 1)
    small_out = sig("small_out", 1, 1)
    sm_split = sig("sm_split", 2, 2)
    idx_roped = sig("idx_roped", 8, 0)
    qk_roped = sig("qk_roped", 8, 8)
    turned = sig("turned", 7, 4)
    turn_out = sig("turn_out", 7, 4)
    logits = sig("logits", 4, 0)
    relu_ok = sig("relu_ok", 4, 0)
    idx_sum = sig("idx_sum", 16, 0)
    top8 = sig("top8", 32, 0)
    bias_ok = sig("bias_ok", 4, 0)
    scores = sig("scores", 4, 4)
    masked = sig("masked", 8, 8)
    max_ok = sig("max_ok", 4, 4)
    probs = sig("probs", 16, 16)
    p_turned = sig("p_turned", 6, 6)
    p_out = sig("p_out", 6, 6)
    pv = sig("pv", 4, 4)
    zi = sig("zi", 4, 4)
    att_ok = sig("att_ok", 4, 4)
    att_turned = sig("att_turned", 2, 2)
    yb_hi = sig("yb_hi", 2, 2)
    yb_lo = sig("yb_lo", 2, 2)
    ws_ok = sig("ws_ok", 1, 0)
    ln_stats = sig("ln_stats", 4, 0)
    ln_rooted = sig("ln_rooted", 1, 0)
    ln_inv = sig("ln_inv", 1, 0)
    ln_norm = sig("ln_norm", 2, 0)
    ln_ok = sig("ln_ok", 4, 0)
    mixed = sig("mixed", 2, 0)
    mix_ok = sig("mix_ok", 2, 0)
    ya_ok = sig("ya_ok", 2, 0)
    ya_hi = sig("ya_hi", 2, 0)
    ya_lo = sig("ya_lo", 2, 0)
    gate_sig = sig("gate_sig", 2 * KC, 0)
    gate_in = sig("gate_in", 2 * FC, 0)
    h_scaled = sig("h_scaled", 2 * FC, 0)
    u_gelu = sig("u_gelu", 1, 0)
    merge = sig("merge", KC, 0)
    merge_even = sig("merge_even", 8, 0)
    w_idx_ok = sig("w_idx_ok", 1, 0)
    m_hi = sig("m_hi", KC, 0)
    m_lo = sig("m_lo", KC, 0)
    stored = sig("stored", 0, 0)
    held = sig("held", 0, 0)
    tap = sig("tap", 0, 12 + 2 * FC)
    conv_ok = sig("conv_ok", 0, 36 + 3 * FC)
    conv_src = sig("conv_src", 0, 6)
    z_ok = sig("z_ok", 0, 2)
    act_ok = sig("act_ok", 0, 6)
    hv_ok = sig("hv_ok", 0, FC, pre=2)
    ba_split = sig("ba_split", 0, 2)
    beta_exp = sig("beta_exp", 0, 1)
    beta_ok = sig("beta_ok", 0, 2)
    dec_in = sig("dec_in", 0, 2)
    dec_exp = sig("dec_exp", 0, 2)
    dec_ln = sig("dec_ln", 0, 1)
    dec_ok = sig("dec_ok", 0, 2)
    g_col = sig("g_col", 0, 1)
    g_neg_ok = sig("g_neg_ok", 0, 1)
    gb_ok = sig("gb_ok", 0, 4)
    g_rows = sig("g_rows", 0, 2)
    gam_in = sig("gam_in", 0, 2)
    beta_out = sig("beta_out", 0, 2)
    gam_ok = sig("gam_ok", 0, 2)
    g_last_ok = sig("g_last_ok", 0, 1)
    qg_e = sig("qg_e", 0, 1)
    k_exp_in = sig("k_exp_in", 0, 1)
    k_scale_ok = sig("k_scale_ok", 0, 1)
    w_exp = sig("w_exp", 0, 1)
    w_scale_ok = sig("w_scale_ok", 0, 1)
    dn_squared = sig("dn_squared", 0, 2)
    k_ln_ok = sig("k_ln_ok", 0, 1)
    k_inv_ok = sig("k_inv_ok", 0, 1)
    k_bias_ok = sig("k_bias_ok", 0, 1)
    w_in = sig("w_in", 0, 1)
    beta_k_ok = sig("beta_k_ok", 0, 1)
    q_col = sig("q_col", 0, 1)
    q2_ok = sig("q2_ok", 0, 1)
    q_diag_ok = sig("q_diag_ok", 0, 2)
    dn_turned = sig("dn_turned", 0, 4)
    dn_scaled = sig("dn_scaled", 0, 4)
    grams = sig("grams", 0, 4)
    a_raw = sig("a_raw", 0, 2)
    a_ok = sig("a_ok", 0, 2)
    qk_ok = sig("qk_ok", 0, 2)
    qg_ok = sig("qg_ok", 0, 1)
    u_first = sig("u_first", 0, 4)
    t_first = sig("t_first", 0, 2)
    t_first_out = sig("t_first_out", 0, 2)
    c_ok = sig("c_ok", 0, 12)
    lp = sig("lp", 0, 12)
    lp_out = sig("lp_out", 0, 12)
    lt = sig("lt", 0, 10)
    t_ok = sig("t_ok", 0, 10)
    lu = sig("lu", 0, 12)
    u_ok = sig("u_ok", 0, 12)
    dn_out = sig("dn_out", 0, 6)
    dn_copy = sig("dn_copy", 0, 6)
    o_squared = sig("o_squared", 0, 1)
    o_summed = sig("o_summed", 0, 1)
    o_rooted = sig("o_rooted", 0, 1)
    o_inv = sig("o_inv", 0, 1)
    o_norm = sig("o_norm", 0, 1)
    o_gated = sig("o_gated", 0, 1)
    o_hi = sig("o_hi", 0, 1)
    o_lo = sig("o_lo", 0, 1)
    signals = {"drained": drained, "x_new": x_new, "projected": projected}

    def soft_view(buf, kl):
        return soft[:, buf].rearrange("p (a b) k -> p a b k", a=2)[:, :, :, 0:kl]

    def sc_view(kl):
        return ps[:, SC:SC + 2, 0:2 * kl].rearrange("p a (b k) -> p a b k", b=2)

    def heads(a, width=HD):
        return a.rearrange("p t (h d) -> p t h d", d=width)

    def run_of(at, k):
        return k - 1 if at[0] == 2 and k >= 2 else k

    block = ctx.enter_context(nc.Block())
    END1 = (1, DEPTH)

    @block.sync
    def _(sp):
        for dst, src in [(x[:], io["x"]), (gains1[:], io["gains1"]), (ones_d[:], io["ones_d"]), (eps[:], io["eps"])]:
            sp.dma_start(dst, src).then_inc(inputs.sem, 16)

        def load(at, k, g, dst_elems, src):
            sp.wait_ge(lo.sem, lo.upto(at, k + 4 * g + 1 - RAW_RING))
            sp.dma_start(raw[:, k % RAW_RING, 0:dst_elems], src).then_inc(landed[k % RAW_RING].sem, 16)

        def stream(at, st, src, first=0, last=None):
            n = (st.slots if last is None else last) - first
            cycle(sp, n, 4, lambda j, g: load(at, st.slot0 + first + j, g, st.elems,
                                              src[at[1], first + j + 4 * g]))

        first = True
        with layers(sp) as layer:
            at = (1, layer)
            stream(at, st1["gu1"], io["gu1"], 0, 2)
            stream(at, st1["gu1"], io["gu1"], 2)
            stream(at, st1["down1"], io["down1"])
            stream(at, st1["in"], io["in1"], 0, 2)
            sp.wait_ge(used.sem, used.upto(at, st1["in"].slot0))
            for dst, src in [(sm_raw[:], io["small1"]), (ws_raw[:], io["ws1"]), (rows[:], io["rows1"])]:
                sp.dma_start(dst, src[layer]).then_inc(params.sem, 16)
            stream(at, st1["in"], io["in1"], 2)
            stream(at, st1["pb"], io["pb1"])
            stream(at, st1["pa"], io["pa1"])
            stream(at, st1["out"], io["out1"])
            stream(at, st1["gu2"], io["gu2"])
            stream(at, st1["down2"], io["down2"])
        with layers(sp) as layer:
            at = (2, layer)
            stream(at, st2["qkv"], io["in2"])
            cycle(sp, 8, 4, lambda j, g: load(at, st2["side"].slot0 + j, g, SLOT, io["in2"][layer, 6 + j + 4 * g]))
            stream(at, st2["out"], io["out2"])
            stream(at, st2["gu"], io["gu3"])
            stream(at, st2["down"], io["down3"])
        for k in range(LEAD):
            load((2, DEPTH), k, 0, SLOT, io["in2"][0, k])
        for c in range(KC):
            sp.wait_ge(x_new.sem, x_new.upto((2, DEPTH - 1), 3 * KC + c + 1))
            sp.dma_start(io["out"][:, c], x[:, c]).then_inc(stored.sem, 16)
        sp.wait_ge(stored.sem, 16 * KC)

    @block.tensor
    def _(pe):
        pe.sem_inc(used.sem, RING)

        def mac(out, w, wl, xh, xl, first, last):
            pe.matmul(out, w, xh, start=first, stop=False)
            pe.matmul(out, w, xl, start=False, stop=False)
            return pe.matmul(out, wl, xh, start=False, stop=last)

        def mac_tok(out, xh, xl, w, wl, first, last):
            pe.matmul(out, xh, w, start=first, stop=False)
            pe.matmul(out, xh, wl, start=False, stop=False)
            return pe.matmul(out, xl, w, start=False, stop=last)

        def mean_square(at, k, by_token=False):
            pe.wait_ge(summed.sem, summed.upto(at, 7 * run_of(at, k)))
            if by_token:
                for t in range(NT):
                    pe.matmul(ps[:, AUX, T + t:T + t + 1], ssum[:, t * P:(t + 1) * P], ones_d[:, 0:1],
                              start=True, stop=True)
            pe.matmul(ps[:, AUX, 0:T], ones_d[:], ssum[:], start=True, stop=True).then_inc(mean_sq.sem, 1)

        def mean_square_direct(at):
            for c in range(KC):
                pe.wait_ge(squared.sem, squared.upto(at, KC + c + 1))
                last = pe.matmul(ps[:, AUX, 0:T], ones_d[:], sq8[:, c], start=c == 0, stop=c == KC - 1)
            last.then_inc(mean_sq.sem, 1)

        def xn_ready(at, k, c):
            s = xn_lo_even if c % 2 == 0 else xn_lo_odd
            pe.wait_ge(s.sem, s.upto(at, k * KC // 2 + c // 2 + 1))

        def gate_up(at, st, k, prev):
            wide(at, st, 0, 0, xn, KC, k - 1, lambda: mean_square(at, k), prev)
            wide(at, st, 1, 0, xn, KC, None, None, prev)
            with pe.Fori(0, (FC - 2) // 4) as g:
                for j in range(2, 6):
                    wide(at, st, j, g, xn, KC)

        def slot(at, st, j, g=0):
            pe.wait_ge(lo.sem, lo.upto(at, st.slot0 + j + 4 * g + 1))
            r = (st.slot0 + j) % RING
            return w_hi[:, r], w_lo[:, r]

        def pair(at, st, i):
            if not isinstance(i, int) or i >= 2 or st.name != "in":
                pe.wait_ge(signals[st.free].sem, signals[st.free].upto(at, st.free0 + (i - 1) * st.free_by))

        def stage_open(at, prev):
            pe.wait_ge(signals[prev.free].sem, signals[prev.free].upto(at, prev.free0 + prev.pairs * prev.free_by))
            pe.sem_inc(held.sem, 1)

        def after(at, behind, q):
            signal, count, by = behind
            pe.wait_ge(signal.sem, signal.upto(at, count - by * (1 - q)))

        def behind(st):
            return signals[st.free], st.free0 + st.pairs * st.free_by, st.free_by

        def wide(at, st, j, g, x_of, chunks, k_norm=None, between=None, prev=None):
            whs, wls = slot(at, st, j, g)
            tiles = SLOT // P // chunks
            wh = whs.rearrange("p (c n) -> p c n", c=chunks)
            wl = wls.rearrange("p (c n) -> p c n", c=chunks)
            for f in range(tiles):
                q = (tiles // 2) * j + f // 2
                if f % 2 == 0 and prev is not None:
                    after(at, prev, q)
                elif f % 2 == 0:
                    pair(at, st, q + 4 * g)
                out = ps[:, 2 * (q % 2) + f % 2, 0:T]
                for c in range(chunks):
                    if k_norm is not None and f == 0 and j == 0:
                        xn_ready(at, k_norm, c)
                    last = mac(out, wh[:, c, f * P:(f + 1) * P], wl[:, c, f * P:(f + 1) * P],
                               x_of[:, c, 0], x_of[:, c, 1], c == 0, c == chunks - 1)
                last.then_inc(full.sem if f < tiles - 1 else used.sem, 1)
                if between and f == 0:
                    between()

        def down(at, st, hk):
            def tile(j, g):
                pair(at, st, j + 2 * g)
                out = ps[:, 2 * (j % 2), 0:T]
                for half in range(2):
                    pe.wait_ge(lo.sem, lo.upto(at, st.slot0 + 2 * j + half + 4 * g + 1))
                    pe.wait_ge(h_lo.sem, h_lo.upto(at, hk + (half + 1) * FC // 2))
                    r = (st.slot0 + 2 * j + half) % RING
                    wh = w_hi[:, r, 0:SLOT_DOWN].rearrange("p (c n) -> p c n", n=P)
                    wl = w_lo[:, r, 0:SLOT_DOWN].rearrange("p (c n) -> p c n", n=P)
                    for c in range(FC // 2):
                        k = half * FC // 2 + c
                        last = mac(out, wh[:, c], wl[:, c], h[:, k, 0], h[:, k, 1], k == 0, k == FC - 1)
                    last.then_inc(used.sem, 1)
            cycle(pe, st.pairs, 2, tile)

        def tokens(at, st, j, k_norm=None, between=None, prev=None):
            whs, wls = slot(at, st, j)
            if prev is not None:
                after(at, prev, j)
            else:
                pair(at, st, j)
            wh = whs.rearrange("p (c n) -> p c n", c=KC)
            wl = wls.rearrange("p (c n) -> p c n", c=KC)
            for t in range(NT):
                for c in range(KC):
                    if k_norm is not None and t == 0:
                        xn_ready(at, k_norm, c)
                    last = mac_tok(ps[:, 2 * (j % 2) + t, 0:256], xn[:, c, 0, t * P:(t + 1) * P],
                                   xn[:, c, 1, t * P:(t + 1) * P], wh[:, c], wl[:, c], c == 0, c == KC - 1)
                last.then_inc(full.sem if t == 0 else used.sem, 1)
                if between and t == 0:
                    between()

        def turn(at, k, src, bank=AUX):
            if k >= 2:
                pe.wait_ge(turn_out.sem, turn_out.upto(at, k - 1))
            n = len(src)
            for i, s in enumerate(src):
                last = pe.transpose(ps[:, bank + k % 2, i * P:(i + 1) * P], s, ident[:])
            last.then_inc(turned.sem, 1)

        def score(at, u, q, k, done):
            t, g = UNITS[u]
            kl = P * (t + 1)
            view = sc_view(kl)
            for hh in range(GROUP):
                hd = GROUP * g + hh
                lane = slice(HD * (hd % 2), HD * (hd % 2) + HD)
                last = pe.matmul(view[:, hh % 2, hh // 2], q[lane, hd // 2, t * P:(t + 1) * P], k(lane, hd, kl),
                                 start=True, stop=True)
            last.then_inc(done.sem, 1)

        def attend_scores(at, u, n_turns, bank=AUX):
            if u == 0:
                pe.wait_ge(turn_out.sem, turn_out.upto(at, n_turns))
            elif bank == SC:
                pe.wait_ge(att_ok.sem, att_ok.upto(at, u))
                if u == 2:
                    pe.wait_ge(yb_lo.sem, yb_lo.upto(at, 1))
            else:
                pe.wait_ge(masked.sem, masked.upto(at, 2 * u))
            score(at, u, q_t, lambda lane, hd, kl: k_t[lane, hd // 2, 0:kl], scores)

        def attend_turn(at, u, bank=AUX):
            t, _ = UNITS[u]
            pe.wait_ge(probs.sem, probs.upto(at, GROUP * (u + 1)))
            if u:
                pe.wait_ge(p_out.sem, p_out.upto(at, TURNS[u - 1]))
            if u and t:
                pe.wait_ge(att_ok.sem, att_ok.upto(at, u))
            if u >= 2:
                pe.wait_ge(yb_lo.sem, yb_lo.upto(at, 1))
            if bank == SC:
                pe.wait_ge(masked.sem, masked.upto(at, 2 * u + 2))
            for b in range(t + 1):
                for k in range(GROUP):
                    last = pe.transpose(ps[:, bank + b, k * P:(k + 1) * P], soft[:, u % 2, k, b * P:(b + 1) * P],
                                        ident[:])
                last.then_inc(p_turned.sem, 1)

        def attend_pv(at, u, v_at, bank=AUX):
            t, g = UNITS[u]
            pe.wait_ge(p_out.sem, p_out.upto(at, TURNS[u]))
            if u:
                pe.wait_ge(att_ok.sem, att_ok.upto(at, u))
            for hh in range(GROUP):
                k = GROUP // 2 * (hh % 2) + hh // 2
                for b in range(t + 1):
                    last = pe.matmul(ps[:, bank + 1, hh * HD:(hh + 1) * HD], p_t[:, b, k],
                                     v_at[:, b, (GROUP * g + hh) * HD:(GROUP * g + hh + 1) * HD],
                                     start=(b == 0), stop=(b == t))
            last.then_inc(pv.sem, 1)

        def attend_out(at, t, bank=AUX):
            pe.wait_ge(att_ok.sem, att_ok.upto(at, 2 if t else 4))
            pe.wait_ge(p_out.sem, p_out.upto(at, TURNS[1] if t else TURNS[3]))
            for c in range(WC):
                last = pe.transpose(ps[:, bank, c * P:(c + 1) * P], att[:, t, c * P:(c + 1) * P], ident[:])
            last.then_inc(att_turned.sem, 1)

        def small_product(at, n, split_ok, w, wl):
            pe.wait_ge(split_ok.sem, split_ok.upto(at, 2))
            for t in range(NT):
                for c in range(KC):
                    last = mac_tok(ps[:, AUX + 1, t * n:(t + 1) * n], xn[:, c, 0, t * P:(t + 1) * P],
                                   xn[:, c, 1, t * P:(t + 1) * P], w[:, c], wl[:, c],
                                   c == 0, c == KC - 1)
            last.then_inc(small.sem, 1)

        def index_scores(at, u):
            if u == 0:
                pe.wait_ge(turn_out.sem, turn_out.upto(at, 3))
            else:
                pe.wait_ge(relu_ok.sem, relu_ok.upto(at, u))
            score(at, u, qi_t, lambda lane, hd, kl: ki_t[lane, 0:kl], logits)

        def gmlp_mix(at, n):
            if n == 0:
                pe.wait_ge(ln_ok.sem, ln_ok.upto(at, 4))
                pe.wait_ge(ws_ok.sem, ws_ok.upto(at, 1))
                pe.wait_ge(att_ok.sem, att_ok.upto(at, 4))
            else:
                pe.wait_ge(mix_ok.sem, mix_ok.upto(at, n))
            for g in range(WC):
                last = pe.matmul(ps[:, AUX + 1, g * P:(g + 1) * P], tok[:, VA, n, g * P:(g + 1) * P], ws_m[:, g],
                                 start=True, stop=True)
            last.then_inc(mixed.sem, 1)

        def turns_of(buf, t):
            return [roped[:, buf, t, c * P:(c + 1) * P] for c in range(WC)]

        pe.wait_ge(inputs.sem, 16 * N_INPUTS)
        with layers(pe) as layer:
            at = (1, layer)
            gate_up(at, st1["gu1"], 0, (x_new, 0, 1))
            stage_open(at, st1["gu1"])
            down(at, st1["down1"], 0)

            pe.wait_ge(ready.sem, 16 * N_TABLES)
            for k in range(20):
                if k == 0:
                    tokens(at, st1["in"], k, 0, lambda: mean_square(at, 1, True), behind(st1["down1"]))
                elif k == 1:
                    tokens(at, st1["in"], k, None, None, behind(st1["down1"]))
                elif k < 10:
                    tokens(at, st1["in"], k)
                elif k == 11:
                    wide(at, st1["in"], k, 0, xn, KC, None, lambda: attend_turn(at, 0))
                elif k == 14:
                    wide(at, st1["in"], k, 0, xn, KC, None, lambda: attend_turn(at, 2))
                else:
                    wide(at, st1["in"], k, 0, xn, KC)
                if k == 1:
                    small_product(at, HD + NH, sm_split, sm_hi, sm_lo)
                if k == 3:
                    pe.wait_ge(idx_roped.sem, idx_roped.upto(at, 4))
                    turn(at, 0, turns_of(0, 0))
                    pe.wait_ge(small_out.sem, small_out.upto(at, 1))
                    turn(at, 1, turns_of(0, 1))
                    pe.wait_ge(idx_roped.sem, idx_roped.upto(at, 8))
                    turn(at, 2, [ki_rope[:, t].rearrange("p a d -> p (a d)") for t in range(NT)])
                if k in (4, 5, 6, 7):
                    index_scores(at, k - 4)
                if k == 7:
                    pe.wait_ge(qk_roped.sem, qk_roped.upto(at, 4))
                    turn(at, 3, turns_of(1, 0))
                    turn(at, 4, turns_of(1, 1))
                if k == 8:
                    pe.wait_ge(qk_roped.sem, qk_roped.upto(at, 8))
                    turn(at, 5, turns_of(0, 0))
                    turn(at, 6, turns_of(0, 1))
                if k == 9:
                    pe.wait_ge(relu_ok.sem, relu_ok.upto(at, 4))
                    attend_scores(at, 0, 7)
                if k == 10:
                    attend_scores(at, 1, 7)
                if k == 11:
                    attend_pv(at, 0, tok[:, V])
                    attend_turn(at, 1)
                if k == 12:
                    attend_pv(at, 1, tok[:, V])
                    attend_scores(at, 2, 7)
                if k == 13:
                    attend_out(at, 1)
                    attend_scores(at, 3, 7)
                if k == 14:
                    attend_pv(at, 2, tok[:, V])
                    attend_turn(at, 3)
                if k == 15:
                    attend_pv(at, 3, tok[:, V])
                if k == 16:
                    attend_out(at, 0)
                    gmlp_mix(at, 0)
                if k == 17:
                    gmlp_mix(at, 1)

            stage_open(at, st1["in"])
            pe.wait_ge(yb_lo.sem, yb_lo.upto(at, 2))
            for j in range(2):
                wide(at, st1["pb"], j, 0, yb, WC)
            pe.wait_ge(ya_lo.sem, ya_lo.upto(at, 2))
            for j in range(2):
                wide(at, st1["pa"], j, 0, ya, WC)
            stage_open(at, st1["pa"])
            pe.wait_ge(m_lo.sem, m_lo.upto(at, KC))
            for j in range(4):
                wide(at, st1["out"], j, 0, m, KC)
            gate_up(at, st1["gu2"], 2, behind(st1["out"]))
            stage_open(at, st1["gu2"])
            down(at, st1["down2"], FC)
        mean_square(END1, 0)
        with layers(pe) as layer:
            at = (2, layer)
            sq, ss, so = st2["qkv"], st2["side"], st2["out"]

            def turn4(bank, src, done):
                for i in range(DN_H):
                    last = pe.transpose(ps[:, bank, i * P:(i + 1) * P], src(i), ident[:])
                last.then_inc(done.sem, 1)

            def heads4(bank, lhs, rhs, done, start=True, stop=True):
                for i in range(DN_H):
                    last = pe.matmul(ps[:, bank, i * P:(i + 1) * P], lhs(i), rhs(i), start=start, stop=stop)
                if done is not None:
                    last.then_inc(done.sem, 1)

            def lane(t):
                return slice(t * P, (t + 1) * P)

            def squares_column(bank, at_col):
                for t in range(NT):
                    for i in range(DN_H):
                        col = at_col + t * DN_H + i
                        last = pe.matmul(ps[:, bank, col:col + 1], dn_sq[:, i, lane(t)], ones[:, 0:1],
                                         start=True, stop=True)
                return last

            def decay_column():
                pe.wait_ge(dn_squared.sem, dn_squared.upto(at, 1))
                squares_column(SC, NT * DN_H)
                pe.wait_ge(dec_ok.sem, dec_ok.upto(at, 2))
                for t in range(NT):
                    last = pe.matmul(ps[:, SC, t * DN_H:(t + 1) * DN_H], tri_ts[:], dec_g[:, t],
                                     start=True, stop=True)
                last.then_inc(g_col.sem, 1)

            def query_column():
                pe.wait_ge(dn_squared.sem, dn_squared.upto(at, 2))
                squares_column(SC + 1, 0).then_inc(q_col.sem, 1)

            def decay_rows_of(t):
                pe.wait_ge(gb_ok.sem, gb_ok.upto(at, 2 * t + 2))
                if t == 0:
                    pe.wait_ge(small_out.sem, small_out.upto(at, 1))
                else:
                    pe.wait_ge(k_inv_ok.sem, k_inv_ok.upto(at, 1))
                    pe.wait_ge(q2_ok.sem, q2_ok.upto(at, 1))
                bank = SC if t else AUX
                pe.matmul(ps[:, bank, :], ones[:], gb[:, 0].rearrange("p h q -> p (h q)"), start=True, stop=True)
                pe.matmul(ps[:, bank + 1, :], ones[:], gb[:, 1].rearrange("p h q -> p (h q)"),
                          start=True, stop=True).then_inc(g_rows.sem, 1)

            def turn_k():
                pe.wait_ge(gam_in.sem, gam_in.upto(at, 1))
                pe.wait_ge(beta_out.sem, beta_out.upto(at, 1))
                for t in range(NT):
                    turn4(AUX + t, lambda i, t=t: dn_k[:, i, lane(t)], dn_turned)

            def turn_v():
                pe.wait_ge(act_ok.sem, act_ok.upto(at, 6))
                for t in range(NT):
                    if t == 0:
                        pe.wait_ge(a_ok.sem, a_ok.upto(at, 1))
                    else:
                        pe.wait_ge(qk_ok.sem, qk_ok.upto(at, 1))
                    turn4(AUX + t, lambda i, t=t: dn_v[:, i, lane(t)], dn_turned)

            def gram(t):
                pe.wait_ge(act_ok.sem, act_ok.upto(at, 4))
                if t == 0:
                    pe.wait_ge(dn_scaled.sem, dn_scaled.upto(at, 2))
                else:
                    pe.wait_ge(dn_scaled.sem, dn_scaled.upto(at, 4))
                heads4(AUX, lambda i: dn_k[:, i, lane(t)], lambda i: dn_k[:, i, lane(t)], grams)
                heads4(AUX + 1, lambda i: dn_k[:, i, lane(t)], lambda i: dn_q[:, i, lane(t)], grams)

            def inverse_first():
                pe.wait_ge(a_raw.sem, a_raw.upto(at, 2))
                pe.wait_ge(qk_ok.sem, qk_ok.upto(at, 2))
                for t in range(NT):
                    pe.wait_ge(u_first.sem, u_first.upto(at, 2 * t + 2))
                    turn4(AUX + t, lambda i, t=t: u_inv[:, t, i], t_first)

            def level_p(n):
                for t in range(NT):
                    pe.wait_ge(c_ok.sem, c_ok.upto(at, 2 * (n - 1) + t + 1))
                    if n == 1:
                        pe.wait_ge(t_first_out.sem, t_first_out.upto(at, t + 1))
                    else:
                        pe.wait_ge(t_ok.sem, t_ok.upto(at, 2 * (n - 2) + t + 1))
                        pe.wait_ge(u_ok.sem, u_ok.upto(at, 2 * (n - 2) + t + 1))
                    heads4(AUX + t, lambda i: lev_c[:, t, i], lambda i: t_inv[:, t, i], lp)

            def level_t(n):
                for t in range(NT):
                    pe.wait_ge(lp_out.sem, lp_out.upto(at, 2 * (n - 1) + t + 1))
                    heads4(AUX + t, lambda i: u_inv[:, t, i], lambda i: lev_p[:, t, i], lt)

            def level_u(n):
                for t in range(NT):
                    if n < LEVELS - 1:
                        pe.wait_ge(t_ok.sem, t_ok.upto(at, 2 * (n - 1) + t + 1))
                    else:
                        pe.wait_ge(lp_out.sem, lp_out.upto(at, 2 * (n - 1) + t + 1))
                    heads4(AUX + t, lambda i: lev_p[:, t, i], lambda i: u_inv[:, t, i], lu)

            def mid(k):
                if k == 0:
                    gram(0)
                if k == 1:
                    gram(1)
                if k == 2:
                    inverse_first()
                    level_p(1)
                if k in (3, 4, 5, 6, 7):
                    level_u(k - 2)
                    level_p(k - 1)

            for k in range(6):
                def between(k=k):
                    if k == 0:
                        mean_square(at, 0, True)
                    if k == 3:
                        decay_column()
                    if k == 5:
                        decay_rows_of(1)
                wide(at, sq, k, 0, xn, KC, 0 if k == 0 else None, between)
                if k == 1:
                    small_product(at, 2 * DN_H, ba_split, ba_hi, ba_lo)
                if k == 4:
                    decay_rows_of(0)
                    query_column()
                if k == 5:
                    turn_k()
            stage_open(at, sq)
            for k in range(8):
                if k < 6:
                    tokens(at, ss, k, None, lambda: mid(k))
                else:
                    wide(at, ss, k, 0, xn, KC, None, lambda: mid(k))
                if k == 0:
                    turn_v()
                if k in (2, 3, 4, 5, 6):
                    level_t(k - 1)
                if k == 2:
                    pe.wait_ge(qk_roped.sem, qk_roped.upto(at, 4))
                    turn(at, 0, turns_of(1, 0), SC)
                    turn(at, 1, turns_of(1, 1), SC)
                if k == 4:
                    pe.wait_ge(qk_roped.sem, qk_roped.upto(at, 8))
                    turn(at, 2, turns_of(0, 0), SC)
                    turn(at, 3, turns_of(0, 1), SC)
                if k == 5:
                    attend_scores(at, 0, 4, SC)
                if k == 6:
                    attend_turn(at, 0, SC)
                if k == 7:
                    attend_pv(at, 0, tok[:, V], SC)
                    level_u(LEVELS - 1)
                    attend_scores(at, 1, 4, SC)

            pe.wait_ge(u_ok.sem, u_ok.upto(at, 11))
            heads4(AUX, lambda i: u_inv[:, 0, i], lambda i: rhs_v[:, 0, i], dn_out)
            pe.wait_ge(u_ok.sem, u_ok.upto(at, 12))
            heads4(AUX + 1, lambda i: rhs_w[:, i], lambda i: u_inv[:, 1, i], dn_out)
            attend_turn(at, 1, SC)
            pe.wait_ge(dn_copy.sem, dn_copy.upto(at, 1))
            heads4(AUX, lambda i: k_dec[:, i], lambda i: v_new[:, 0, i], dn_out)
            attend_pv(at, 1, tok[:, V], SC)
            pe.wait_ge(dn_copy.sem, dn_copy.upto(at, 3))
            for i in range(DN_H):
                out = ps[:, AUX + 1, i * P:(i + 1) * P]
                pe.matmul(out, u_inv[:, 1, i], rhs_v[:, 1, i], start=True, stop=False)
                last = pe.matmul(out, w_neg[:, i], state[:, i], start=False, stop=True)
            last.then_inc(dn_out.sem, 1)
            heads4(AUX, lambda i: v_new[:, 0, i], lambda i: qk[:, 0, i], dn_out)
            attend_out(at, 1, SC)
            pe.wait_ge(dn_copy.sem, dn_copy.upto(at, 4))
            attend_scores(at, 2, 4, SC)
            for i in range(DN_H):
                out = ps[:, AUX + 1, i * P:(i + 1) * P]
                pe.matmul(out, v_new[:, 1, i], qk[:, 1, i], start=True, stop=False)
                last = pe.matmul(out, state[:, i], qg[:, i], start=False, stop=True)
            last.then_inc(dn_out.sem, 1)
            attend_turn(at, 2, SC)
            attend_pv(at, 2, tok[:, V], SC)
            attend_scores(at, 3, 4, SC)
            pe.wait_ge(q_diag_ok.sem, q_diag_ok.upto(at, 2))
            pe.wait_ge(o_squared.sem, o_squared.upto(at, 1))
            for b in range(2):
                pe.matmul(ps[:, AUX + b, :], ones_q[:], q_diag[:, 2 * b:2 * b + 2].rearrange("p h q -> p (h q)"),
                          start=True, stop=False)
                last = pe.matmul(ps[:, AUX + b, :], ones[:],
                                 o_sq[:, 2 * b:2 * b + 2].rearrange("p h q -> p (h q)"), start=False, stop=True)
            last.then_inc(o_summed.sem, 1)
            attend_turn(at, 3, SC)
            attend_pv(at, 3, tok[:, V], SC)
            attend_out(at, 0, SC)

            stage_open(at, ss)
            pe.wait_ge(o_lo.sem, o_lo.upto(at, 1))
            pe.wait_ge(yb_lo.sem, yb_lo.upto(at, 2))
            for j in range(4):
                wide(at, so, j, 0, y2, KC)
            mean_square(at, 1)
            mean_square_direct(at)
            cycle(pe, FC, 4, lambda j, g: wide(at, st2["gu"], j, g, xn, KC, 1))
            stage_open(at, st2["gu"])
            down(at, st2["down"], 0)
            mean_square(at, 3)

    def slot_done(eng, at, st, j, g=0):
        eng.wait_ge(used.sem, used.upto(at, st.slot0 + j + 4 * g + 1))

    def tile_done(eng, at, st, j, f, g=0):
        if f < st.early:
            eng.wait_ge(full.sem, full.upto(at, st.full0 + st.early * j + f + 1 + 4 * st.early * g))
        else:
            slot_done(eng, at, st, j, g)

    def rounds(eng, at, st, nxt, count, per, split, body):
        ahead = LEAD // per
        period = RING // per

        def step(j, g):
            for s in range(per):
                split(at, st.slot0 + per * j + LEAD + s, g, st.elems)
            body(j, g)

        cycle(eng, count - ahead, period, step)
        for j in range(count - ahead, count):
            last = j == st.slots // per - 1
            for s in range(per - 1 if last else per):
                split(at, st.slot0 + per * j + LEAD + s, 0, nxt)
            body(j, 0)
            if last:
                split(at, st.slot0 + per * j + LEAD + per - 1, 0, nxt)

    @block.scalar
    def _(act):
        def copy(out, src):
            return act.activation(out, src, ACT.Copy)

        def split(at, k, g, elems):
            r = k % RING
            act.wait_ge(landed[k % RAW_RING].sem, landed[k % RAW_RING].upto(at, 16 * (k // RAW_RING + 1) + 32 * g))
            act.wait_ge(used.sem, used.upto(at, k + 1 + 4 * g - RING))
            copy(w_hi[:, r, 0:elems], raw[:, k % RAW_RING, 0:elems]).then_inc(hi.sem, 1)

        def square(at, k, c, src, first=False):
            if not first:
                act.wait_ge(x_new.sem, x_new.upto(at, KC * k + c + 1))
            if isinstance(c, int) and c == 0:
                dst = ssum[:]
            else:
                dst = sqb[:, c % 2]
                if c >= 3:
                    act.wait_ge(summed.sem, summed.upto(at, 7 * run_of(at, k) + c - 2))
            act.activation(dst, src, ACT.Square).then_inc(squared.sem, 1)

        def root(at, k, n=T):
            act.activation(warm[:, 0:1], eps[:, 0:1], ACT.Sqrt)
            act.wait_ge(mean_sq.sem, mean_sq.upto(at, k + 1))
            act.activation(rms[:, 0:n], ps[:, AUX, 0:n], ACT.Sqrt, bias=eps[:, 0:1]).then_inc(rooted.sem, 1)

        def split_xn(at, kv, c):
            act.wait_ge(v_ok.sem, v_ok.upto(at, KC * kv + c + 1))
            copy(xn[:, c, 0], v[:, c]).then_inc(xn_hi.sem, 1)

        def taps(at, st, j, f, w, bias=None, g=0):
            src = conv_in[:, j % 2, f]
            if st.name == "gu":
                tile_done(act, at, st, j, f, g)
                src = ps[:, 2 * (j % 2) + f, 0:T]
            elif f == 0:
                act.wait_ge(conv_src.sem, conv_src.upto(at, j + 1))
            else:
                act.wait_ge(drained.sem, drained.upto(at, st.free0 + j + 1))
            func = ACT.Copy if bias is None else ACT.Identity
            more = {} if bias is None else {"bias": bias}
            act.activation(conv[:, j % 2, f], src, func, scale=w, **more)\
               .then_inc(tap.sem, 1)

        def gate_silu(at, gk):
            def body(j, g):
                act.wait_ge(gate_in.sem, gate_in.upto(at, gk + j + 1 + 4 * g))
                act.activation(silu_gate[:, j % 2], silu_gate[:, j % 2], ACT.Silu).then_inc(gate_ok.sem, 1)
            return body

        def squares_of_down(at, st, k, src, nxt, kv=None):
            def body(f, odd, first=False):
                if kv is not None:
                    act.wait_ge(v_ok.sem, v_ok.upto(at, KC * kv + f + 1))
                    copy(xn[:, f, 0], v[:, f]).then_inc(xn_hi.sem, 1)
                act.wait_ge(x_new.sem, x_new.upto(at, KC * k + f + 1))
                if first:
                    act.activation(ssum[:], src[:, 0], ACT.Square).then_inc(squared.sem, 1)
                else:
                    act.wait_ge(summed.sem, summed.upto(at, 7 * run_of(at, k) + f - 2))
                    act.activation(sqb[:, odd], src[:, f], ACT.Square).then_inc(squared.sem, 1)

            def splits(j, g, elems):
                for n in range(2):
                    split(at, st.slot0 + 2 * j + LEAD + n, g, elems)

            act.activation(warm[:, 0:1], eps[:, 0:1], ACT.Sqrt)
            splits(0, 0, st.elems)
            body(0, 0, True)
            with act.Fori(0, (KC - 2) // 2) as g:
                for j in (1, 2):
                    splits(j, g, st.elems)
                    body(j + 2 * g, j % 2)
            split(at, st.slot0 + 2 * (KC - 1) + LEAD, 0, nxt)
            body(KC - 1, 1)
            split(at, st.slot0 + 2 * (KC - 1) + LEAD + 1, 0, nxt)

        def turn_copy(at, k, dst, n=WC, bank=AUX):
            act.wait_ge(turned.sem, turned.upto(at, k + 1))
            src = ps[:, bank + k % 2, 0:n * P]
            if n == WC:
                src = src.rearrange("p (c q) -> p c q", c=WC)
            copy(dst, src).then_inc(turn_out.sem, 1)

        def attend_exp(at, u):
            t, _ = UNITS[u]
            act.wait_ge(max_ok.sem, max_ok.upto(at, u + 1))
            for k in range(GROUP):
                s = soft[:, u % 2, k, 0:P * (t + 1)]
                act.activation(s, s, ACT.Exp, bias=neg_max[:, u % 2, k:k + 1],
                               accum_out=z_sum[:, u, k:k + 1]).then_inc(probs.sem, 1)

        def attend_copy(at, u, bank=AUX):
            t, _ = UNITS[u]
            if u:
                act.wait_ge(pv.sem, pv.upto(at, u))
            for b in range(t + 1):
                act.wait_ge(p_turned.sem, p_turned.upto(at, TURNS[u] - t + b))
                copy(p_t[:, b], ps[:, bank + b, :].rearrange("p (k q) -> p k q", k=GROUP)).then_inc(p_out.sem, 1)

        def attend_hi(at, t, dst, bank=AUX):
            act.wait_ge(att_turned.sem, att_turned.upto(at, 2 - t))
            copy(dst[:, :, 0, t * P:(t + 1) * P],
                 ps[:, bank, :].rearrange("p (c q) -> p c q", c=WC)).then_inc(yb_hi.sem, 1)

        act.wait_ge(inputs.sem, 16 * N_INPUTS)
        for c in range(KC):
            act.wait_ge(v_ok.sem, c + 1)
            copy(xn[:, c, 0], v[:, c]).then_inc(xn_hi.sem, 1)
        for k in range(LEAD):
            split((1, 0), k, 0, SLOT)
        for c in range(KC):
            if c == 0:
                act.activation(ssum[:], x[:, 0], ACT.Square).then_inc(squared.sem, 1)
            else:
                if c >= 3:
                    act.wait_ge(summed.sem, c - 2)
                act.activation(sqb[:, c % 2], x[:, c], ACT.Square).then_inc(squared.sem, 1)
        tables = [(ident[:], io["ident"]), (ones_q[:], io["ones_q"]),
                  (gate_bias[:], io["gate_bias"]),
                  (cos1[:], io["cos1"]), (sin1[:], io["sin1"]), (causal[:], io["causal"]),
                  (tri_ts[:], io["tri_ts"]),
                  (ones[:], io["ones"]), (gains2[:], io["gains2"]), (cos2[:], io["cos2"]),
                  (sin2[:], io["sin2"]), (reach[:], io["reach"]), (conv_w[:], io["conv_w"]),
                  (up_w[:], io["up_w"]), (up_b[:], io["up_b"]), (decay_rows[:], io["decay_rows"]),
                  (dn_gain[:], io["dn_gain"]), (mask_t[:], io["mask_t"]), (strict[:], io["strict"]),
                  (level_m[:], io["level_m"]), (ba_raw[:], io["small2"])]
        assert len(tables) == N_TABLES
        for dst, src in tables:
            act.dma_start(dst, src).then_inc(ready.sem, 16)

        with layers(act) as layer:
            at = (1, layer)

            def ffn(k, gu, dn, nxt):
                root(at, k)
                act.activation(warm[:, 1:2], eps[:, 0:1], ACT.Silu)
                rounds(act, at, gu, dn.elems, FC, 1, split, gate_silu(at, FC * (k // 2)))
                squares_of_down(at, dn, k, x, nxt, k)

            ffn(0, st1["gu1"], st1["down1"], SLOT)
            root(at, 1, T + NT)
            si = st1["in"]
            act.wait_ge(ready.sem, 16 * N_TABLES)
            act.wait_ge(params.sem, params.upto(at, 48))
            copy(sm_hi[:], sm_raw[:]).then_inc(sm_split.sem, 1)
            act.activation(warm[:, 2:3], eps[:, 0:1], ACT.Exp)
            for k in range(20):
                split(at, si.slot0 + k + LEAD, 0, SLOT)
                if k == 0:
                    act.wait_ge(rstd_ok.sem, rstd_ok.upto(at, 2))
                if k < 10:
                    for t in range(2):
                        tile_done(act, at, si, k, t)
                        part = (QI, Q, K, V, VA)[k // 2]
                        dst = tok[:, part, t, 256 * (k % 2):256 * (k % 2) + 256]
                        f = ACT.Gelu_apprx_tanh if k >= 8 else ACT.Copy
                        ins = act.activation(dst, ps[:, 2 * (k % 2) + t, 0:256], f, scale=rstd[:, T + t:T + t + 1])
                    ins.then_inc(projected.sem, 1)
                if k == 11:
                    act.wait_ge(projected.sem, projected.upto(at, 12))
                    act.activation(u_t[:], u_t[:], ACT.Gelu_apprx_tanh).then_inc(u_gelu.sem, 1)
                if k == 1:
                    act.wait_ge(small.sem, small.upto(at, 1))
                    for t in range(NT):
                        n = HD + NH
                        ins = act.activation(ki_wi[:, t], ps[:, AUX + 1, t * n:(t + 1) * n], ACT.Copy,
                                             scale=rstd[:, T + t:T + t + 1])
                    ins.then_inc(small_out.sem, 1)
                if k == 3:
                    turn_copy(at, 0, qi_t[:, :, 0:P])
                    turn_copy(at, 1, qi_t[:, :, P:T])
                    turn_copy(at, 2, ki_t[:], 2)
                if k in (4, 5, 6, 7):
                    u = k - 4
                    act.wait_ge(logits.sem, logits.upto(at, u + 1))
                    if u >= 2:
                        act.wait_ge(idx_sum.sem, idx_sum.upto(at, 4 * (u - 1)))
                    kl = P * (UNITS[u][0] + 1)
                    act.activation(soft_view(u % 2, kl), sc_view(kl), ACT.Relu).then_inc(relu_ok.sem, 1)
                if k == 7:
                    turn_copy(at, 3, q_t[:, :, 0:P])
                    turn_copy(at, 4, q_t[:, :, P:T])
                if k == 8:
                    turn_copy(at, 5, k_t[:, :, 0:P])
                    turn_copy(at, 6, k_t[:, :, P:T])
                if k == 9:
                    attend_exp(at, 0)
                if k == 10:
                    attend_copy(at, 0)
                    attend_exp(at, 1)
                if k == 11:
                    attend_copy(at, 1)
                if k == 12:
                    attend_exp(at, 2)
                if k == 13:
                    attend_hi(at, 1, yb)
                    attend_copy(at, 2)
                    attend_exp(at, 3)
                if k == 14:
                    attend_copy(at, 3)
                if k == 15:
                    act.wait_ge(ln_stats.sem, ln_stats.upto(at, 4))
                    act.activation(ln_root[:], ln_mv[:, :, 1], ACT.Sqrt, bias=eps[:, 0:1]).then_inc(ln_rooted.sem, 1)
                if k == 16:
                    attend_hi(at, 0, yb)
                if k in (17, 18):
                    n = k - 17
                    act.wait_ge(ya_ok.sem, ya_ok.upto(at, n + 1))
                    copy(ya[:, :, 0, n * P:(n + 1) * P],
                         ya_v[:, n].rearrange("p (c q) -> p c q", c=WC)).then_inc(ya_hi.sem, 1)
            def gate_sigmoid(c):
                act.activation(gates[:, c], gates[:, c], ACT.Sigmoid, bias=gate_bias[:, layer, c:c + 1])\
                   .then_inc(gate_sig.sem, 1)

            act.wait_ge(projected.sem, projected.upto(at, 20))
            for c in range(KC, KC + 4):
                gate_sigmoid(c)
            for j in range(4):
                st = st1["pb"] if j < 2 else st1["pa"]
                if j < 3:
                    split(at, st.slot0 + j % 2 + LEAD, 0, SLOT)
                    for c in range(4 * (j + 1), 4 * (j + 2)):
                        gate_sigmoid((KC + c) % (2 * KC))
                if j >= 2:
                    for c in range(4 * (j - 2), 4 * (j - 1)):
                        act.wait_ge(merge.sem, merge.upto(at, c + 1))
                        copy(m[:, c, 0], v[:, c]).then_inc(m_hi.sem, 1)
                if j == 3:
                    split(at, st.slot0 + 1 + LEAD, 0, SLOT)
            so = st1["out"]
            for j in range(4):
                if j < 3:
                    split(at, so.slot0 + j + LEAD, 0, SLOT)
                for c in (2 * j, 2 * j + 1):
                    split_xn(at, 1, c)
                    square(at, 1, c, x[:, c])
            split(at, so.slot0 + 3 + LEAD, 0, SLOT)
            ffn(2, st1["gu2"], st1["down2"], SLOT)
        root(END1, 0)
        for c in range(KC):
            square(END1, 0, c, x[:, c])
        with layers(act) as layer:
            at = (2, layer)
            sq, ss, so = st2["qkv"], st2["side"], st2["out"]

            def four(t):
                return t.rearrange("p h q -> p (h q)")

            def silu_of(k):
                act.wait_ge(conv_ok.sem, conv_ok.upto(at, 6 * (k + 1)))
                dst = (dn_k, dn_q, dn_v)[k // 2][:, 2 * (k % 2):2 * (k % 2) + 2]
                act.activation(dst, conv[:, k % 2], ACT.Silu).then_inc(act_ok.sem, 1)

            def decays():
                act.activation(beta_e[:], ba[:, :, 0:DN_H], ACT.Exp, scale=-1.0).then_inc(beta_exp.sem, 1)
                act.activation(a_exp[:], decay_rows[:, layer, 1], ACT.Exp).then_inc(dec_exp.sem, 1)
                act.wait_ge(dec_in.sem, dec_in.upto(at, 2))
                act.activation(dec_e[:], dec_n[:], ACT.Exp).then_inc(dec_exp.sem, 1)
                act.wait_ge(dec_exp.sem, dec_exp.upto(at, 2))
                act.activation(dec_n[:], dec_e[:], ACT.Ln, bias=ones[:, 0:1]).then_inc(dec_ln.sem, 1)

            def columns_out():
                act.wait_ge(g_col.sem, g_col.upto(at, 1))
                n = NT * DN_H
                act.activation(k_ln[:], ps[:, SC, n:2 * n].rearrange("p (t h) -> p t h", h=DN_H), ACT.Ln,
                               bias=eps[:, 0:1]).then_inc(k_ln_ok.sem, 1)
                act.activation(g_neg[:], ps[:, SC, 0:n].rearrange("p (t h) -> p t h", h=DN_H),
                               ACT.Copy, scale=-1.0).then_inc(g_neg_ok.sem, 1)
                act.wait_ge(k_ln_ok.sem, k_ln_ok.upto(at, 1))
                act.activation(k_inv[:], k_ln[:], ACT.Exp, scale=-0.5).then_inc(k_inv_ok.sem, 1)
                act.wait_ge(w_in.sem, w_in.upto(at, 1))
                act.activation(w_scale[:], w_scale[:], ACT.Exp).then_inc(w_exp.sem, 1)

            def decay_exps(t):
                act.wait_ge(g_rows.sem, g_rows.upto(at, t + 1))
                rows4 = ps[:, SC if t else AUX, :].rearrange("p (h q) -> p h q", h=DN_H)
                if t == 0:
                    act.activation(g_last[:], rows4[:, :, P - 1], ACT.Copy).then_inc(g_last_ok.sem, 1)
                    act.wait_ge(k_exp_in.sem, k_exp_in.upto(at, 1))
                    act.activation(k_scale[:], k_scale[:], ACT.Exp).then_inc(k_scale_ok.sem, 1)
                else:
                    act.activation(qg[:], rows4, ACT.Exp).then_inc(qg_e.sem, 1)
                act.wait_ge(gam_in.sem, gam_in.upto(at, t + 1))
                for i in range(DN_H):
                    last = act.activation(gam[:, t, i], gam[:, t, i], ACT.Exp, bias=k_bias[:, t, i:i + 1])
                last.then_inc(gam_ok.sem, 1)

            def unit_squares(i):
                src = (dn_k, dn_q)[i]
                act.wait_ge(act_ok.sem, act_ok.upto(at, 2 * i + 2))
                if i:
                    act.wait_ge(g_col.sem, g_col.upto(at, 1))
                act.activation(four(dn_sq[:]), four(src[:]), ACT.Square).then_inc(dn_squared.sem, 1)

            def first_copy():
                for t in range(NT):
                    act.wait_ge(t_first.sem, t_first.upto(at, t + 1))
                    copy(four(t_inv[:, t]), ps[:, AUX + t, :]).then_inc(t_first_out.sem, 1)

            def level_copy(n):
                for t in range(NT):
                    act.wait_ge(lp.sem, lp.upto(at, 2 * (n - 1) + t + 1))
                    copy(four(lev_p[:, t]), ps[:, AUX + t, :]).then_inc(lp_out.sem, 1)

            def out_copy(n, dst, bank, sign=1.0):
                act.wait_ge(dn_out.sem, dn_out.upto(at, n))
                src = ps[:, bank, :].rearrange("p (h q) -> p h q", h=DN_H)
                act.activation(dst, src, ACT.Copy, scale=sign).then_inc(dn_copy.sem, 1)

            for c in range(KC):
                split_xn(at, -1, c)
            root(at, 0, T + NT)
            copy(ba_hi[:], ba_raw[:, layer]).then_inc(ba_split.sem, 1)
            act.activation(warm[:, 1:2], eps[:, 0:1], ACT.Silu)
            for k in range(6):
                split(at, sq.slot0 + k + LEAD, 0, SLOT)
                if k:
                    silu_of(k - 1)
                taps(at, sq, k, 0, conv_w[:, layer, 2 * k, 3:4])
                if k == 2:
                    unit_squares(0)
                if k == 4:
                    unit_squares(1)
                taps(at, sq, k, 1, conv_w[:, layer, 2 * k + 1, 3:4])
                if k == 1:
                    act.wait_ge(small.sem, small.upto(at, 1))
                    act.wait_ge(rstd_ok.sem, rstd_ok.upto(at, 1))
                    for t in range(NT):
                        n = 2 * DN_H
                        ins = act.activation(ba[:, t], ps[:, AUX + 1, t * n:(t + 1) * n], ACT.Copy,
                                             scale=rstd[:, T + t:T + t + 1])
                    ins.then_inc(small_out.sem, 1)
                if k == 2:
                    act.wait_ge(small_out.sem, small_out.upto(at, 1))
                    decays()
                if k == 3:
                    columns_out()
                if k == 4:
                    decay_exps(0)
                    act.wait_ge(q_col.sem, q_col.upto(at, 1))
                    copy(q2[:], ps[:, SC + 1, 0:NT * DN_H].rearrange("p (t h) -> p t h", h=DN_H))\
                        .then_inc(q2_ok.sem, 1)
                if k == 5:
                    decay_exps(1)
            for k in range(8):
                split(at, ss.slot0 + k + LEAD, 0, SLOT)
                if k == 0:
                    silu_of(5)
                if k in (2, 3, 4, 5, 6, 7):
                    level_copy(k - 1)
                if k < 6:
                    for t in range(2):
                        tile_done(act, at, ss, k, t)
                        part = (Q, K, V)[k // 2]
                        ins = act.activation(tok[:, part, t, 256 * (k % 2):256 * (k % 2) + 256],
                                             ps[:, 2 * (k % 2) + t, 0:256], ACT.Copy, scale=rstd[:, T + t:T + t + 1])
                    ins.then_inc(projected.sem, 1)
                else:
                    act.wait_ge(projected.sem, projected.upto(at, k + 1))
                    z = z_t[:, 2 * (k - 6):2 * (k - 6) + 2]
                    act.activation(z, z, ACT.Silu).then_inc(z_ok.sem, 1)
                if k == 1:
                    first_copy()
                if k == 2:
                    turn_copy(at, 0, q_t[:, :, 0:P], WC, SC)
                    turn_copy(at, 1, q_t[:, :, P:T], WC, SC)
                if k == 4:
                    turn_copy(at, 2, k_t[:, :, 0:P], WC, SC)
                    turn_copy(at, 3, k_t[:, :, P:T], WC, SC)
                if k == 5:
                    attend_exp(at, 0)
                if k == 6:
                    attend_copy(at, 0, SC)
            attend_exp(at, 1)
            out_copy(1, v_new[:, 0], AUX)
            out_copy(2, w_neg[:], AUX + 1, -1.0)
            attend_copy(at, 1, SC)
            out_copy(3, state[:], AUX)
            out_copy(4, v_new[:, 1], AUX + 1)
            out_copy(5, o_t[:, :, 0:P], AUX)
            attend_hi(at, 1, y2[:, 0:WC], SC)
            attend_exp(at, 2)
            out_copy(6, o_t[:, :, P:T], AUX + 1)
            act.wait_ge(dn_copy.sem, dn_copy.upto(at, 6))
            act.activation(four(o_sq[:]), four(o_t[:]), ACT.Square).then_inc(o_squared.sem, 1)
            attend_copy(at, 2, SC)
            attend_exp(at, 3)
            act.wait_ge(o_summed.sem, o_summed.upto(at, 1))
            act.activation(o_rn[:].rearrange("p (b h) q -> p b (h q)", b=2), ps[:, AUX:AUX + 2, :], ACT.Ln,
                           bias=eps[:, 1:2], scale=1.0 / P).then_inc(o_rooted.sem, 1)
            act.wait_ge(o_rooted.sem, o_rooted.upto(at, 1))
            act.activation(four(o_rn[:]), four(o_rn[:]), ACT.Exp, scale=-0.5).then_inc(o_inv.sem, 1)
            attend_copy(at, 3, SC)
            act.wait_ge(o_gated.sem, o_gated.upto(at, 1))
            copy(y2[:, WC:KC, 0], o_t[:]).then_inc(o_hi.sem, 1)
            attend_hi(at, 0, y2[:, 0:WC], SC)
            for j in range(4):
                if j < 3:
                    split(at, so.slot0 + j + LEAD, 0, SLOT)
                square(at, 0, 2 * j, hm[:, 2 * j])
                square(at, 0, 2 * j + 1, hm[:, 2 * j + 1])
            root(at, 1)
            split(at, so.slot0 + 3 + LEAD, 0, SLOT)
            for c in range(KC):
                act.wait_ge(x_new.sem, x_new.upto(at, KC + c + 1))
                act.activation(sq8[:, c], x[:, c], ACT.Square).then_inc(squared.sem, 1)
            root(at, 2)
            for c in range(KC):
                split_xn(at, 0, c)

            def gate_gelu(j, g):
                st = st2["gu"]
                i = j + 4 * g
                act.wait_ge(hv_ok.sem, hv_ok.upto(at, i - 1))
                taps(at, st, j, 0, up_w[:, layer, i, 2:3], up_b[:, layer, bass.ds(i, 1)], g)
                taps(at, st, j, 1, up_w[:, layer, i + FC, 2:3], up_b[:, layer, bass.ds(i + FC, 1)], g)
                act.wait_ge(conv_ok.sem, conv_ok.upto(at, 36 + 3 * j + 3 + 12 * g))
                act.activation(silu_gate[:, j % 2], conv[:, j % 2, 0], ACT.Gelu_apprx_tanh).then_inc(gate_ok.sem, 1)

            act.activation(warm[:, 3:4], eps[:, 0:1], ACT.Gelu_apprx_tanh)
            rounds(act, at, st2["gu"], SLOT_DOWN, FC, 1, split, gate_gelu)
            squares_of_down(at, st2["down"], 2, hm, SLOT)
            root(at, 3)
            for c in range(KC):
                square(at, 3, c, x[:, c])

    @block.vector
    def _(dve):
        dve.sem_inc(lo.sem, RAW_RING)
        dve.sem_inc(drained.sem, 2)
        dve.sem_inc(x_new.sem, 2)

        def split(at, k, g, elems):
            r = k % RING
            dve.wait_ge(hi.sem, hi.upto(at, k + 1 + 4 * g))
            dve.tensor_tensor(w_lo[:, r, 0:elems], raw[:, k % RAW_RING, 0:elems], w_hi[:, r, 0:elems],
                              ALU.subtract).then_inc(lo.sem, 1)

        def inverse(at, k):
            dve.wait_ge(rooted.sem, rooted.upto(at, k + 1))
            n = T + NT if (at[0], k) in ((1, 1), (2, 0)) else T
            dve.reciprocal(rstd[:, 0:n], rms[:, 0:n]).then_inc(rstd_ok.sem, 1)
            dve.wait_ge(rstd_ok.sem, rstd_ok.upto(at, k + 1))
            dve.sem_inc(held.sem, 1)

        def scale(at, n, f, gain):
            dve.wait_ge(x_new.sem, x_new.upto(at, KC * n + f + 1))
            dve.tensor_scalar(v[:, f], x[:, f], gain, None, ALU.mult).then_inc(v_ok.sem, 1)

        def scale_low(at, n, f):
            dve.wait_ge(xn_hi.sem, xn_hi.upto(at, KC * n + f + 1))
            dve.tensor_tensor(xn[:, f, 1], v[:, f], xn[:, f, 0], ALU.subtract).then_inc(xn_lo_even.sem, 1)

        def low_even(at, n, c):
            dve.wait_ge(xn_hi.sem, xn_hi.upto(at, KC * n + c + 1))
            dve.tensor_tensor(xn[:, c, 1], v[:, c], xn[:, c, 0], ALU.subtract).then_inc(xn_lo_even.sem, 1)

        def gated(at, st, gk, hk):
            def body(j, g):
                tile_done(dve, at, st, j, 0, g)
                dve.tensor_tensor(silu_gate[:, j % 2], ps[:, 2 * (j % 2), 0:T], rstd[:, 0:T], ALU.mult)\
                   .then_inc(gate_in.sem, 1)
                dve.wait_ge(gate_ok.sem, gate_ok.upto(at, gk + j + 1 + 4 * g))
                slot_done(dve, at, st, j, g)
                dve.wait_ge(h_lo.sem, h_lo.upto(at, hk + j - 1 + 4 * g))
                dve.tensor_tensor(hv[:, j % 2], silu_gate[:, j % 2], ps[:, 2 * (j % 2) + 1, 0:T], ALU.mult)\
                   .then_inc(drained.sem, 1)
            return body

        def residual(at, st, n):
            def body(j, g):
                slot_done(dve, at, st, 2 * j + 1, g)
                f = j + 2 * g
                dve.scalar_tensor_tensor(x[:, f], ps[:, 2 * (j % 2), 0:T], 0.5, x[:, f], ALU.mult, ALU.add)\
                   .then_inc(x_new.sem, 1)
                scale(at, n, f, gains1[:, 3 * at[1] + n + 1, bass.ds(f, 1)])
                if j % 2 == 0:
                    scale_low(at, n, f)
            return body

        def rope(eng, signal, at, done, raw_v, out, tmp, cos, sin, n_heads, half):
            shape = [P, NT, n_heads, HD]
            part = [P, NT, n_heads, half]
            c = cos[:].unsqueeze(2).broadcast_to(shape)
            eng.tensor_tensor(out, raw_v, c, ALU.mult).then_inc(signal.sem, 1)
            for i in range(2):
                s = sin[:, :, i * half:(i + 1) * half].unsqueeze(2).broadcast_to(part)
                o = (1 - i) * half
                eng.tensor_tensor(tmp[:, :, :, i * half:(i + 1) * half], raw_v[:, :, :, o:o + half], s,
                                  ALU.mult).then_inc(signal.sem, 1)
            eng.wait_ge(signal.sem, signal.upto(at, done + 3))
            eng.tensor_tensor(out[:, :, :, 0:2 * half], out[:, :, :, 0:2 * half], tmp[:, :, :, 0:2 * half],
                              ALU.add).then_inc(signal.sem, 1)

        def attend_mask(at, u, bias):
            t, _ = UNITS[u]
            kl = P * (t + 1)
            dve.wait_ge(scores.sem, scores.upto(at, u + 1))
            if u >= 2:
                dve.wait_ge(p_turned.sem, p_turned.upto(at, TURNS[u - 2]))
            b = bias.unsqueeze(1).broadcast_to([P, 2, kl])
            for a in range(2):
                dve.scalar_tensor_tensor(soft_view(u % 2, kl)[:, a], sc_view(kl)[:, a], float(HD) ** -0.5, b,
                                         ALU.mult, ALU.add).then_inc(masked.sem, 1)
            dve.wait_ge(masked.sem, masked.upto(at, 2 * u + 2))
            dve.tensor_reduce(neg_max[:, u % 2], soft[:, u % 2, :, 0:kl], AX.X, ALU.max, negate=True)\
               .then_inc(max_ok.sem, 1)

        def attend_norm(at, u, bank=AUX):
            t, g = UNITS[u]
            dve.wait_ge(probs.sem, probs.upto(at, GROUP * (u + 1)))
            dve.reciprocal(z_inv[:, u], z_sum[:, u]).then_inc(zi.sem, 1)
            dve.wait_ge(zi.sem, zi.upto(at, u + 1))
            dve.wait_ge(pv.sem, pv.upto(at, u + 1))
            z = z_inv[:, u].rearrange("p (a b) -> p b a", a=2).unsqueeze(3).broadcast_to([P, 2, 2, HD])
            view = "p (b a d) -> p b a d"
            dve.tensor_tensor(att[:, t, g * 256:(g + 1) * 256].rearrange(view, a=2, d=HD),
                              ps[:, bank + 1, 0:256].rearrange(view, a=2, d=HD), z, ALU.mult)\
               .then_inc(att_ok.sem, 1)

        def attend_lo(at, t, dst, bank=AUX):
            dve.wait_ge(yb_hi.sem, yb_hi.upto(at, 2 - t))
            lane = slice(t * P, (t + 1) * P)
            dve.tensor_tensor(dst[:, :, 1, lane], ps[:, bank, :].rearrange("p (c q) -> p c q", c=WC),
                              dst[:, :, 0, lane], ALU.subtract).then_inc(yb_lo.sem, 1)

        def index_sum(at, u):
            t, g = UNITS[u]
            kl = P * (t + 1)
            dve.wait_ge(relu_ok.sem, relu_ok.upto(at, u + 1))
            w_t = work[:, t, 0:kl]
            for k in range(GROUP):
                hh = 2 * (k % 2) + k // 2
                n = GROUP * u + k
                if n:
                    dve.wait_ge(idx_sum.sem, idx_sum.upto(at, n))
                acc = causal[:, T - kl:T] if g == 0 and k == 0 else w_t
                dve.scalar_tensor_tensor(w_t, soft[:, u % 2, k, 0:kl], w_idx[:, t, GROUP * g + hh:GROUP * g + hh + 1],
                                         acc, ALU.mult, ALU.add).then_inc(idx_sum.sem, 1)

        def top_k(at, i):
            t = UNITS[2 * i][0]
            kl = P * (t + 1)
            w_t = work[:, t, 0:kl]
            dve.wait_ge(idx_sum.sem, idx_sum.upto(at, 8 * (i + 1)))
            dve.sem_inc(held.sem, 1)
            for r in range(TOPK // 8):
                n = 2 * (TOPK // 8 * i + r)
                if n:
                    dve.wait_ge(top8.sem, top8.upto(at, n))
                    dve.sem_inc(held.sem, 1)
                dve.max(best8[:], w_t).then_inc(top8.sem, 1)
                dve.wait_ge(top8.sem, top8.upto(at, n + 1))
                dve.sem_inc(held.sem, 1)
                dve.match_replace(w_t, best8[:], w_t, TAKEN).then_inc(top8.sem, 1)
            dve.wait_ge(top8.sem, top8.upto(at, 16 * (i + 1)))
            dve.tensor_scalar(w_t, w_t, TAKEN / 2, NEG, ALU.is_gt, ALU.mult).then_inc(bias_ok.sem, 1)
            dve.wait_ge(bias_ok.sem, bias_ok.upto(at, 2 * i + 1))
            dve.tensor_tensor(w_t, w_t, causal[:, T - kl:T], ALU.add).then_inc(bias_ok.sem, 1)
            dve.wait_ge(bias_ok.sem, bias_ok.upto(at, 2 * i + 2))

        dve.wait_ge(inputs.sem, 16 * N_INPUTS)
        for c in range(KC):
            dve.tensor_scalar(v[:, c], x[:, c], gains1[:, 0, c:c + 1], None, ALU.mult).then_inc(v_ok.sem, 1)
        for c in range(0, KC, 2):
            dve.wait_ge(xn_hi.sem, c + 1)
            dve.tensor_tensor(xn[:, c, 1], v[:, c], xn[:, c, 0], ALU.subtract).then_inc(xn_lo_even.sem, 1)
        for k in range(LEAD):
            split((1, 0), k, 0, SLOT)
        with layers(dve) as layer:
            at = (1, layer)

            def ffn(k, gu, dn, hk):
                inverse(at, k)
                rounds(dve, at, gu, dn.elems, FC, 1, split, gated(at, gu, hk, hk))
                rounds(dve, at, dn, SLOT, KC, 2, split, residual(at, dn, k))

            ffn(0, st1["gu1"], st1["down1"], 0)
            inverse(at, 1)
            dve.wait_ge(ready.sem, 16 * N_TABLES)
            si = st1["in"]
            for k in range(20):
                split(at, si.slot0 + k + LEAD, 0, SLOT)
                if k == 0:
                    dve.wait_ge(sm_split.sem, sm_split.upto(at, 1))
                    dve.tensor_tensor(sm_lo[:], sm_raw[:], sm_hi[:], ALU.subtract).then_inc(sm_split.sem, 1)
                if k == 1:
                    dve.wait_ge(projected.sem, projected.upto(at, 2))
                    rope(dve, idx_roped, at, 0, heads(tok[:, QI]), heads(roped[:, 0]),
                         heads(soft[:, 0].rearrange("p a k -> p (a k)").rearrange("p (t n) -> p t n", t=NT)),
                         cos1, sin1, NH, HD // 2)
                if k == 2:
                    dve.wait_ge(small_out.sem, small_out.upto(at, 1))
                    kis = ki_wi[:, :, 0:HD].unsqueeze(2).broadcast_to([P, NT, 2, HD])
                    tmp = soft[:, 1, 0, 0:2 * NT * HD].rearrange("p (t a d) -> p t a d", t=NT, a=2)
                    rope(dve, idx_roped, at, 4, kis, ki_rope[:], tmp, cos1, sin1, 2, HD // 2)
                    dve.tensor_scalar(w_idx[:], ki_wi[:, :, HD:HD + NH], float(HD) ** -0.5 * float(NH) ** -0.5,
                                      None, ALU.mult).then_inc(w_idx_ok.sem, 1)
                    dve.wait_ge(w_idx_ok.sem, w_idx_ok.upto(at, 1))
                if k == 4:
                    index_sum(at, 0)
                if k == 5:
                    index_sum(at, 1)
                    top_k(at, 0)
                if k == 6:
                    index_sum(at, 2)
                if k == 7:
                    index_sum(at, 3)
                    top_k(at, 1)
                if k == 9:
                    attend_mask(at, 0, work[:, 1, 0:T])
                if k == 10:
                    attend_mask(at, 1, work[:, 1, 0:T])
                if k == 11:
                    attend_norm(at, 0)
                if k == 12:
                    attend_norm(at, 1)
                    attend_mask(at, 2, work[:, 0, 0:P])
                if k == 13:
                    attend_lo(at, 1, yb)
                    attend_mask(at, 3, work[:, 0, 0:P])
                if k == 14:
                    attend_norm(at, 2)
                    dve.wait_ge(projected.sem, projected.upto(at, 10))
                    for t in range(NT):
                        dve.bn_stats(ln_raw[:, t], tok[:, VA, t]).then_inc(ln_stats.sem, 1)
                    dve.wait_ge(ln_stats.sem, ln_stats.upto(at, 2))
                    dve.sem_inc(held.sem, 1)
                    for t in range(NT):
                        dve.bn_aggr(ln_mv[:, t], ln_raw[:, t]).then_inc(ln_stats.sem, 1)
                if k == 15:
                    attend_norm(at, 3)
                    dve.wait_ge(ln_rooted.sem, ln_rooted.upto(at, 1))
                    dve.reciprocal(ln_rstd[:], ln_root[:]).then_inc(ln_inv.sem, 1)
                    dve.wait_ge(ln_inv.sem, ln_inv.upto(at, 1))
                    for t in range(NT):
                        dve.tensor_scalar(tok[:, VA, t], tok[:, VA, t], ln_mv[:, t, 0:1], ln_rstd[:, t:t + 1],
                                          ALU.subtract, ALU.mult).then_inc(ln_norm.sem, 1)
                if k == 16:
                    attend_lo(at, 0, yb)
                if k >= 10:
                    if k == 10:
                        dve.wait_ge(projected.sem, projected.upto(at, 10))
                    if k == 12:
                        dve.wait_ge(idx_roped.sem, idx_roped.upto(at, 8))
                        dve.wait_ge(qk_roped.sem, qk_roped.upto(at, 8))
                    for t in range(2):
                        tile_done(dve, at, si, k, t)
                        f = 2 * (k - 10) + t
                        dst = u_t[:, f] if k < 12 else gates[:, f - WC]
                        ins = dve.tensor_tensor(dst, ps[:, 2 * (k % 2) + t, 0:T], rstd[:, 0:T], ALU.mult)
                    ins.then_inc(projected.sem, 1)
                if k in (17, 18):
                    n = k - 17
                    lane = slice(n * P, (n + 1) * P)
                    dve.wait_ge(mixed.sem, mixed.upto(at, n + 1))
                    dve.tensor_tensor(mix_b[:, n], ps[:, AUX + 1, :], rows[:, 2], ALU.add).then_inc(mix_ok.sem, 1)
                    dve.wait_ge(u_gelu.sem, u_gelu.upto(at, 1))
                    dve.wait_ge(mix_ok.sem, mix_ok.upto(at, n + 1))
                    dve.tensor_tensor(ya_v[:, n].rearrange("p (c q) -> p c q", c=WC),
                                      mix_b[:, n].rearrange("p (c q) -> p c q", c=WC), u_t[:, :, lane],
                                      ALU.mult).then_inc(ya_ok.sem, 1)
            for name in ("pb", "pa"):
                st = st1[name]
                for j in range(2):
                    last = name == "pa" and j == 1
                    for f in range(4):
                        if f == 2 and not last:
                            split(at, st.slot0 + j + LEAD, 0, SLOT)
                        c = 4 * j + f
                        tile_done(dve, at, st, j, f)
                        src = ps[:, 2 * ((c // 2) % 2) + f % 2, 0:T]
                        gate = gates[:, c + (KC if name == "pb" else 0)]
                        dve.wait_ge(gate_sig.sem, gate_sig.upto(at, c + 1 + (0 if name == "pb" else KC)))
                        dst = gate if name == "pb" else v[:, c]
                        ins = dve.tensor_tensor(dst, src, gate, ALU.mult)
                        if f % 2:
                            ins.then_inc(drained.sem, 1)
                        else:
                            ins.then_inc(merge_even.sem, 1)
                        if name == "pa":
                            if f % 2:
                                dve.wait_ge(drained.sem, drained.upto(at, st.free0 + c // 2 + 1))
                            else:
                                dve.wait_ge(merge_even.sem, merge_even.upto(at, 4 + c // 2 + 1))
                            dve.tensor_tensor(v[:, c], v[:, c], gates[:, KC + c], ALU.add).then_inc(merge.sem, 1)
                    if last:
                        split(at, st.slot0 + j + LEAD, 0, SLOT)
            so = st1["out"]
            for j in range(4):
                for f in range(2):
                    if f == 1 and j < 3:
                        split(at, so.slot0 + j + LEAD, 0, SLOT)
                    c = 2 * j + f
                    tile_done(dve, at, so, j, f)
                    dve.tensor_tensor(x[:, c], x[:, c], ps[:, 2 * (j % 2) + f, 0:T], ALU.add)\
                       .then_inc(x_new.sem, 1)
                    scale(at, 1, c, gains1[:, 3 * layer + 2, c:c + 1])
                    if f == 0:
                        scale_low(at, 1, c)
            split(at, so.slot0 + 3 + LEAD, 0, SLOT)
            ffn(2, st1["gu2"], st1["down2"], FC)
        inverse(END1, 0)
        for c in range(KC):
            dve.tensor_tensor(x[:, c], v[:, c], rstd[:, 0:T], ALU.mult)\
               .then_inc(x_new.sem, 1)
            dve.wait_ge(x_new.sem, x_new.upto(END1, c + 1))
            dve.tensor_scalar(v[:, c], x[:, c], gains2[:, 0, c:c + 1], None, ALU.mult).then_inc(v_ok.sem, 1)
        with layers(dve) as layer:
            at = (2, layer)
            sq, ss, so = st2["qkv"], st2["side"], st2["out"]

            def four(t):
                return t.rearrange("p h q -> p (h q)")

            def bank4(b):
                return ps[:, b, :].rearrange("p (h q) -> p h q", h=DN_H)

            def over_heads(m):
                return m.unsqueeze(1).broadcast_to([P, DN_H, P])

            def over_cols(m):
                return m.unsqueeze(2).broadcast_to([P, DN_H, P])

            def taps(st, j, g, w, slots0, conv0, last_tap):
                whole = st.name == "gu"
                if not whole:
                    for f in range(2):
                        tile_done(dve, at, st, j, f, g)
                        dve.tensor_tensor(conv_in[:, j % 2, f], ps[:, 2 * (j % 2) + f, 0:T], rstd[:, 0:T], ALU.mult)\
                           .then_inc((conv_src, drained)[f].sem, 1)
                    dve.wait_ge(drained.sem, drained.upto(at, st.free0 + j + 1))
                per = 2 * last_tap - (1 if whole else 0)
                for s in range(1, last_tap + 1):
                    for f in range(2):
                        k = 2 * (s - 1) + f
                        if k < 2:
                            dve.wait_ge(tap.sem, tap.upto(at, 2 * (slots0 + j) + f + 1 + 8 * g))
                        else:
                            dve.wait_ge(conv_ok.sem, conv_ok.upto(at, conv0 + per * j + k - 1 + 4 * per * g))
                        c = conv[:, j % 2, f, s:T]
                        src = ps[:, 2 * (j % 2) + f, 0:T - s] if whole else conv_in[:, j % 2, f, 0:T - s]
                        ins = dve.scalar_tensor_tensor(c, src, w(f, last_tap - s), c, ALU.mult, ALU.add)
                        if k < per:
                            ins.then_inc(conv_ok.sem, 1)
                        else:
                            ins.then_inc(drained.sem, 1)

            def decays():
                a = ba[:, :, DN_H:2 * DN_H]
                rows_b = decay_rows[:, layer, 0].unsqueeze(1).broadcast_to([P, NT, DN_H])
                dve.wait_ge(small_out.sem, small_out.upto(at, 1))
                dve.tensor_tensor(dec_t[:], a, rows_b, ALU.add).then_inc(dec_in.sem, 1)
                dve.wait_ge(dec_in.sem, dec_in.upto(at, 1))
                dve.scalar_tensor_tensor(dec_n[:], dec_t[:], -1.0, dec_t[:], ALU.mult, ALU.min)\
                   .then_inc(dec_in.sem, 1)
                dve.wait_ge(beta_exp.sem, beta_exp.upto(at, 1))
                dve.tensor_scalar(beta_e[:], beta_e[:], 1.0, None, ALU.add).then_inc(beta_ok.sem, 1)
                dve.wait_ge(beta_ok.sem, beta_ok.upto(at, 1))
                dve.reciprocal(beta[:], beta_e[:]).then_inc(beta_ok.sem, 1)
                dve.wait_ge(dec_ln.sem, dec_ln.upto(at, 1))
                dve.scalar_tensor_tensor(dec_g[:], dec_t[:], 0.0, dec_n[:], ALU.max, ALU.add)\
                   .then_inc(dec_ok.sem, 1)
                dve.wait_ge(dec_ok.sem, dec_ok.upto(at, 1))
                dve.scalar_tensor_tensor(dec_g[:], dec_g[:], -1.0, a_exp[:].unsqueeze(1).broadcast_to([P, NT, DN_H]),
                                         ALU.mult, ALU.mult).then_inc(dec_ok.sem, 1)

            def decay_in(t):
                dve.wait_ge(g_rows.sem, g_rows.upto(at, t + 1))
                bank = SC if t else AUX
                dve.tensor_tensor(beta_s[:, t], bank4(bank + 1), over_heads(strict[:]), ALU.mult)\
                   .then_inc(beta_out.sem, 1)
                if t == 0:
                    dve.wait_ge(g_last_ok.sem, g_last_ok.upto(at, 1))
                else:
                    dve.wait_ge(qg_e.sem, qg_e.upto(at, 1))
                dve.tensor_tensor(gam[:, t], bank4(bank), over_heads(mask_t[:]), ALU.add).then_inc(gam_in.sem, 1)
                if t == 0:
                    dve.tensor_tensor(k_scale[:], g_last[:], k_bias[:, 0], ALU.add).then_inc(k_exp_in.sem, 1)
                else:
                    dve.wait_ge(w_exp.sem, w_exp.upto(at, 1))
                    dve.tensor_tensor(w_scale[:], w_scale[:], beta[:, 1], ALU.mult).then_inc(w_scale_ok.sem, 1)

            def columns_in():
                dve.wait_ge(k_ln_ok.sem, k_ln_ok.upto(at, 1))
                dve.wait_ge(g_neg_ok.sem, g_neg_ok.upto(at, 1))
                dve.scalar_tensor_tensor(w_scale[:], k_ln[:, 1], -0.5, g_neg[:, 1], ALU.mult, ALU.subtract)\
                   .then_inc(w_in.sem, 1)
                dve.scalar_tensor_tensor(k_bias[:], k_ln[:], -0.5, g_neg[:], ALU.mult, ALU.add)\
                   .then_inc(k_bias_ok.sem, 1)
                dve.wait_ge(k_inv_ok.sem, k_inv_ok.upto(at, 1))
                dve.tensor_tensor(beta_k[:], beta[:], k_inv[:], ALU.mult).then_inc(beta_k_ok.sem, 1)

            def scaled(n, dst, scale, bank):
                dve.wait_ge(dn_turned.sem, dn_turned.upto(at, n))
                dve.tensor_tensor(dst, bank4(bank), over_cols(scale), ALU.mult).then_inc(dn_scaled.sem, 1)

            def grams_in(t):
                dve.wait_ge(gam_ok.sem, gam_ok.upto(at, t + 1))
                dve.wait_ge(grams.sem, grams.upto(at, 2 * t + 1))
                dve.tensor_tensor(a_t[:, t], bank4(AUX), gam[:, t], ALU.mult).then_inc(a_raw.sem, 1)
                dve.wait_ge(grams.sem, grams.upto(at, 2 * t + 2))
                dve.tensor_tensor(qk[:, t], bank4(AUX + 1), gam[:, t], ALU.mult).then_inc(qk_ok.sem, 1)
                dve.wait_ge(a_raw.sem, a_raw.upto(at, t + 1))
                dve.tensor_tensor(a_t[:, t], a_t[:, t], beta_s[:, t], ALU.mult).then_inc(a_ok.sem, 1)

            def level_t(n):
                for t in range(NT):
                    dve.wait_ge(lt.sem, lt.upto(at, 2 * (n - 1) + t + 1))
                    dve.tensor_tensor(four(t_inv[:, t]), four(t_inv[:, t]), ps[:, AUX + t, :], ALU.subtract)\
                       .then_inc(t_ok.sem, 1)

            def level_u(n):
                for t in range(NT):
                    dve.wait_ge(lu.sem, lu.upto(at, 2 * (n - 1) + t + 1))
                    dve.tensor_tensor(four(u_inv[:, t]), four(u_inv[:, t]), ps[:, AUX + t, :], ALU.subtract)\
                       .then_inc(u_ok.sem, 1)

            def reach_of(kl):
                return reach[:, T - kl:T]

            for c in range(0, KC, 2):
                low_even(at, 0, c)
            inverse(at, 0)
            for k in range(6):
                split(at, sq.slot0 + k + LEAD, 0, SLOT)
                if k == 0:
                    dve.wait_ge(ba_split.sem, ba_split.upto(at, 1))
                    dve.tensor_tensor(ba_lo[:], ba_raw[:, layer], ba_hi[:], ALU.subtract).then_inc(ba_split.sem, 1)
                taps(sq, k, 0, lambda f, n: conv_w[:, layer, 2 * k + f, n:n + 1], 0, 0, N_CONV - 1)
                if k == 2:
                    decays()
                if k == 3:
                    columns_in()
                if k == 4:
                    decay_in(0)
                if k == 5:
                    decay_in(1)
                    dve.wait_ge(k_scale_ok.sem, k_scale_ok.upto(at, 1))
                    scaled(1, k_dec[:], k_scale[:], AUX)
                    dve.wait_ge(w_scale_ok.sem, w_scale_ok.upto(at, 1))
                    scaled(2, rhs_w[:], w_scale[:], AUX + 1)
            for k in range(8):
                if k in (3, 4, 5, 6, 7):
                    level_u(k - 2)
                split(at, ss.slot0 + k + LEAD, 0, SLOT)
                if k == 0:
                    grams_in(0)
                    dve.wait_ge(qg_e.sem, qg_e.upto(at, 1))
                    dve.tensor_tensor(qg[:], qg[:], dn_q[:, :, P:T], ALU.mult).then_inc(qg_ok.sem, 1)
                if k == 1:
                    grams_in(1)
                if k == 0:
                    scaled(3, rhs_v[:, 0], beta[:, 0], AUX)
                    scaled(4, rhs_v[:, 1], beta[:, 1], AUX + 1)
                if k in (2, 3, 4, 5, 6):
                    level_t(k - 1)
                if k >= 6:
                    if k == 6:
                        dve.wait_ge(dn_scaled.sem, dn_scaled.upto(at, 4))
                        dve.wait_ge(projected.sem, projected.upto(at, 6))
                    for t in range(2):
                        tile_done(dve, at, ss, k, t)
                        ins = dve.tensor_tensor(z_t[:, 2 * (k - 6) + t], ps[:, 2 * (k % 2) + t, 0:T], rstd[:, 0:T],
                                                ALU.mult)
                    ins.then_inc(projected.sem, 1)
                if k == 5:
                    attend_mask(at, 0, reach_of(T))
                if k == 7:
                    attend_norm(at, 0, SC)
                    level_u(LEVELS - 1)
            attend_mask(at, 1, reach_of(T))
            attend_norm(at, 1, SC)
            attend_lo(at, 1, y2[:, 0:WC], SC)
            attend_mask(at, 2, reach_of(P))
            attend_norm(at, 2, SC)
            attend_mask(at, 3, reach_of(P))
            dve.wait_ge(o_inv.sem, o_inv.upto(at, 1))
            dve.scalar_tensor_tensor(four(o_t[:]), four(o_t[:]), dn_gain[:, layer], four(o_rn[:]), ALU.mult,
                                     ALU.mult).then_inc(o_norm.sem, 1)
            dve.wait_ge(o_norm.sem, o_norm.upto(at, 1))
            dve.wait_ge(z_ok.sem, z_ok.upto(at, 2))
            dve.tensor_tensor(four(o_t[:]), four(o_t[:]), four(z_t[:]), ALU.mult).then_inc(o_gated.sem, 1)
            attend_norm(at, 3, SC)
            attend_lo(at, 0, y2[:, 0:WC], SC)
            for j in range(4):
                for f in range(2):
                    if f == 1 and j < 3:
                        split(at, so.slot0 + j + LEAD, 0, SLOT)
                    tile_done(dve, at, so, j, f)
                    dve.tensor_copy(hm[:, 2 * j + f], ps[:, 2 * (j % 2) + f, 0:T]).then_inc(x_new.sem, 1)

            def post(k):
                inverse(at, k)

                def add(c):
                    dve.wait_ge(post_v.sem, post_v.upto(at, KC * (k // 2) + c + 1))
                    dve.tensor_tensor(x[:, c], x[:, c], v[:, c], ALU.add).then_inc(x_new.sem, 1)

                def scale_next(c):
                    if k == 3:
                        dve.wait_ge(x_new.sem, x_new.upto(at, 3 * KC + c + 1))
                        dve.tensor_scalar(v[:, c], x[:, c], gains2[:, 4 * layer + 4, c:c + 1], None, ALU.mult)\
                           .then_inc(v_ok.sem, 1)

                for c in range(KC):
                    dve.scalar_tensor_tensor(v[:, c], hm[:, c], gains2[:, 4 * layer + k, c:c + 1], rstd[:, 0:T],
                                             ALU.mult, ALU.mult).then_inc(post_v.sem, 1)
                    if c >= 1:
                        add(c - 1)
                    if c >= 2:
                        scale_next(c - 2)
                add(KC - 1)
                scale_next(KC - 2)
                scale_next(KC - 1)

            post(1)
            split(at, so.slot0 + 3 + LEAD, 0, SLOT)
            inverse(at, 2)
            for c in range(KC):
                dve.scalar_tensor_tensor(v[:, c], x[:, c], gains2[:, 4 * layer + 2, c:c + 1], rstd[:, 0:T],
                                         ALU.mult, ALU.mult).then_inc(v_ok.sem, 1)
                if c >= 2 and c % 2 == 0:
                    low_even(at, 1, c - 2)
            low_even(at, 1, KC - 2)

            def gated2(j, g):
                i = j + 4 * g
                taps(st2["gu"], j, g, lambda f, n: up_w[:, layer, i + FC * f, n:n + 1], 6, 36, 2)

            rounds(dve, at, st2["gu"], SLOT_DOWN, FC, 1, split, gated2)

            def out_of_down(j, g):
                f = j + 2 * g
                slot_done(dve, at, st2["down"], 2 * j + 1, g)
                dve.tensor_copy(hm[:, f], ps[:, 2 * (j % 2), 0:T]).then_inc(x_new.sem, 1)

            rounds(dve, at, st2["down"], SLOT, KC, 2, split, out_of_down)
            post(3)

    @block.gpsimd
    def _(pool):
        pool.sem_inc(h_lo.sem, 2)
        pool.sem_inc(hv_ok.sem, 2)

        def add_square(at, k, c):
            pool.wait_ge(squared.sem, squared.upto(at, KC * k + c + 1))
            if c > 1:
                pool.wait_ge(summed.sem, summed.upto(at, 7 * run_of(at, k) + c - 1))
            pool.tensor_tensor(ssum[:], ssum[:], sqb[:, c % 2], ALU.add).then_inc(summed.sem, 1)

        def low(at, n, c):
            pool.wait_ge(xn_hi.sem, xn_hi.upto(at, KC * n + c + 1))
            pool.tensor_tensor(xn[:, c, 1], v[:, c], xn[:, c, 0], ALU.subtract).then_inc(xn_lo_odd.sem, 1)

        def add_squares(at, k, n=None):
            for c in range(1, KC):
                if n is not None and c % 2:
                    low(at, n, c)
                add_square(at, k, c)

        def low_odd(at, k):
            for c in range(1, KC, 2):
                low(at, k, c)

        def split_h(at, st, hk):
            def body(j, g):
                i = j + 4 * g
                if st is st2["gu"]:
                    pool.wait_ge(gate_ok.sem, gate_ok.upto(at, i + 1))
                    pool.wait_ge(drained.sem, drained.upto(at, st.free0 + i + 1))
                    pool.tensor_tensor(hv[:, j % 2], silu_gate[:, j % 2], conv[:, j % 2, 1], ALU.mult)\
                        .then_inc(hv_ok.sem, 1)
                    pool.wait_ge(hv_ok.sem, hv_ok.upto(at, i + 1))
                else:
                    pool.wait_ge(drained.sem, drained.upto(at, st.free0 + i + 1))
                    pool.tensor_tensor(hv[:, j % 2], hv[:, j % 2], rstd[:, 0:T], ALU.mult).then_inc(h_scaled.sem, 1)
                    pool.wait_ge(h_scaled.sem, h_scaled.upto(at, hk + i + 1))
                pool.sem_inc(held.sem, 1)
                pool.tensor_copy(h[:, i, 0], hv[:, j % 2]).then_inc(h_hi.sem, 1)
                pool.wait_ge(h_hi.sem, h_hi.upto(at, hk + i + 1))
                pool.tensor_tensor(h[:, i, 1], hv[:, j % 2], h[:, i, 0], ALU.subtract).then_inc(h_lo.sem, 1)
            cycle(pool, FC, 4, body)

        def rope(signal, at, done, raw_v, out, tmp, cos, sin, half):
            shape = [P, NT, NH, HD]
            part = [P, NT, NH, half]
            pool.tensor_tensor(out, raw_v, cos[:].unsqueeze(2).broadcast_to(shape), ALU.mult).then_inc(signal.sem, 1)
            for i in range(2):
                s = sin[:, :, i * half:(i + 1) * half].unsqueeze(2).broadcast_to(part)
                o = (1 - i) * half
                pool.tensor_tensor(tmp[:, :, :, i * half:(i + 1) * half], raw_v[:, :, :, o:o + half], s,
                                   ALU.mult).then_inc(signal.sem, 1)
            pool.wait_ge(signal.sem, signal.upto(at, done + 3))
            pool.tensor_tensor(out[:, :, :, 0:2 * half], out[:, :, :, 0:2 * half], tmp[:, :, :, 0:2 * half],
                               ALU.add).then_inc(signal.sem, 1)

        pool.wait_ge(inputs.sem, 16 * N_INPUTS)
        low_odd((1, 0), -1)
        add_squares((1, 0), -1)
        with layers(pool) as layer:
            at = (1, layer)
            split_h(at, st1["gu1"], 0)
            add_squares(at, 0, 0)
            pool.wait_ge(ready.sem, 16 * N_TABLES)
            pool.wait_ge(params.sem, params.upto(at, 48))
            pool.tensor_tensor(ws_m[:], ws_raw[:], tri_ts[:].unsqueeze(1).broadcast_to([P, WC, P]), ALU.mult)\
                .then_inc(ws_ok.sem, 1)
            pool.wait_ge(projected.sem, projected.upto(at, 4))
            rope(qk_roped, at, 0, heads(tok[:, Q]), heads(roped[:, 1]), heads(rope_tmp[:]), cos1, sin1, HD // 2)
            pool.wait_ge(projected.sem, projected.upto(at, 6))
            pool.wait_ge(turned.sem, turned.upto(at, 2))
            pool.wait_ge(qk_roped.sem, qk_roped.upto(at, 4))
            rope(qk_roped, at, 4, heads(tok[:, K]), heads(roped[:, 0]), heads(rope_tmp[:]), cos1, sin1, HD // 2)
            for t in range(NT):
                pool.wait_ge(ln_norm.sem, ln_norm.upto(at, t + 1))
                pool.tensor_tensor(tok[:, VA, t], tok[:, VA, t], rows[:, 0], ALU.mult).then_inc(ln_ok.sem, 1)
                pool.wait_ge(ln_ok.sem, ln_ok.upto(at, 2 * t + 1))
                pool.tensor_tensor(tok[:, VA, t], tok[:, VA, t], rows[:, 1], ALU.add).then_inc(ln_ok.sem, 1)
            for n in range(NT):
                lane = slice(n * P, (n + 1) * P)
                pool.wait_ge(ya_hi.sem, ya_hi.upto(at, n + 1))
                pool.tensor_tensor(ya[:, :, 1, lane], ya_v[:, n].rearrange("p (c q) -> p c q", c=WC),
                                   ya[:, :, 0, lane], ALU.subtract).then_inc(ya_lo.sem, 1)
            for c in range(KC):
                pool.wait_ge(m_hi.sem, m_hi.upto(at, c + 1))
                pool.tensor_tensor(m[:, c, 1], v[:, c], m[:, c, 0], ALU.subtract).then_inc(m_lo.sem, 1)
            add_squares(at, 1, 1)
            split_h(at, st1["gu2"], FC)
            add_squares(at, 2, 2)
        add_squares(END1, 0)
        with layers(pool) as layer:
            at = (2, layer)

            def over_heads(m):
                return m.unsqueeze(1).broadcast_to([P, DN_H, P])

            def over_cols(m):
                return m.unsqueeze(2).broadcast_to([P, DN_H, P])

            def level_c(n):
                for t in range(NT):
                    if n > 1:
                        pool.wait_ge(lp.sem, lp.upto(at, 2 * (n - 2) + t + 1))
                    pool.tensor_tensor(lev_c[:, t], a_t[:, t], over_heads(level_m[:, n]), ALU.mult)\
                        .then_inc(c_ok.sem, 1)

            low_odd(at, 0)
            pool.wait_ge(dec_ok.sem, dec_ok.upto(at, 2))
            for t in range(NT):
                if t:
                    pool.wait_ge(g_rows.sem, g_rows.upto(at, 1))
                pool.tensor_tensor(gb[:, 0], over_heads(tri_ts[:]), over_cols(dec_g[:, t]), ALU.mult)\
                    .then_inc(gb_ok.sem, 1)
                if t == 0:
                    pool.wait_ge(beta_k_ok.sem, beta_k_ok.upto(at, 1))
                pool.tensor_tensor(gb[:, 1], over_heads(ident[:]), over_cols(beta_k[:, t]), ALU.mult)\
                    .then_inc(gb_ok.sem, 1)
            for t in range(NT):
                pool.wait_ge(a_ok.sem, a_ok.upto(at, t + 1))
                if t == 0:
                    pool.wait_ge(grams.sem, grams.upto(at, 4))
                pool.tensor_tensor(lev_c[:, t], a_t[:, t], over_heads(level_m[:, 0]), ALU.mult)\
                    .then_inc(u_first.sem, 1)
                pool.wait_ge(u_first.sem, u_first.upto(at, 2 * t + 1))
                pool.tensor_tensor(u_inv[:, t], over_heads(ident[:]), lev_c[:, t], ALU.subtract)\
                    .then_inc(u_first.sem, 1)
            pool.wait_ge(u_first.sem, u_first.upto(at, 4))
            level_c(1)
            pool.wait_ge(projected.sem, projected.upto(at, 2))
            rope(qk_roped, at, 0, heads(tok[:, Q]), heads(roped[:, 1]), heads(rope_tmp[:]), cos2, sin2, ROPE2 // 2)
            level_c(2)
            level_c(3)
            pool.wait_ge(projected.sem, projected.upto(at, 4))
            pool.wait_ge(qk_roped.sem, qk_roped.upto(at, 4))
            rope(qk_roped, at, 4, heads(tok[:, K]), heads(roped[:, 0]), heads(rope_tmp[:]), cos2, sin2, ROPE2 // 2)
            for n in range(4, LEVELS):
                level_c(n)
            pool.wait_ge(q2_ok.sem, q2_ok.upto(at, 1))
            for t in range(NT):
                pool.tensor_tensor(q_diag[:, :, t * P:(t + 1) * P], over_heads(ident[:]), over_cols(q2[:, t]),
                                   ALU.mult).then_inc(q_diag_ok.sem, 1)
            pool.wait_ge(o_hi.sem, o_hi.upto(at, 1))
            pool.tensor_tensor(y2[:, WC:KC, 1], o_t[:], y2[:, WC:KC, 0], ALU.subtract).then_inc(o_lo.sem, 1)
            add_squares(at, 0)
            low_odd(at, 1)
            split_h(at, st2["gu"], 0)
            add_squares(at, 2)
            add_squares(at, 3)


def lay_out(inp):
    f = lambda a: np.ascontiguousarray(a)

    def slots(w, chunks, cols):
        l, _, n = w.shape
        return f(w.reshape(l, chunks, P, n // cols, cols).transpose(0, 3, 2, 1, 4)
                 .reshape(l, n // cols, P, chunks * cols))

    def gate_up(w):
        return f(w.reshape(DEPTH, KC, P, 2, FC, P).transpose(0, 4, 2, 1, 3, 5).reshape(DEPTH, FC, P, SLOT))

    def down(w):
        return f(w.reshape(DEPTH, 2, FC // 2, P, KC, P).transpose(0, 4, 1, 3, 2, 5)
                 .reshape(DEPTH, 2 * KC, P, SLOT_DOWN))

    def columns(g):
        g = g.reshape(*g.shape[:-1], -1, P)
        return f(np.moveaxis(g, -1, 0))

    w = inp["w_in"]
    cut = np.cumsum([W, W, W, W, W, W, HD, NH, D, D])
    u, va, q, k, vv, qi, ki, wi, ga, gb = np.split(w, cut[:-1], axis=-1)
    main = np.concatenate([qi, q, k, vv, va, u, ga, gb], axis=-1)
    side = np.concatenate([ki, wi], axis=-1)
    out = {
        "x": f(inp["x"][0].T.reshape(KC, P, T).transpose(1, 0, 2)),
        "gu1": gate_up(inp["ffn1_w_gu"]), "down1": down(inp["ffn1_w_down"]),
        "gu2": gate_up(inp["ffn2_w_gu"]), "down2": down(inp["ffn2_w_down"]),
        "in1": slots(main, KC, 256),
        "small1": f(side.reshape(DEPTH, KC, P, HD + NH).transpose(0, 2, 1, 3)),
        "pb1": slots(inp["w_pb"], WC, 512), "pa1": slots(inp["w_pa"], WC, 512),
        "out1": slots(inp["w_out"], KC, 256),
        "gains1": columns(np.concatenate([np.stack([inp["ffn1_norm"], inp["mix_norm"], inp["ffn2_norm"]], 1)
                                          .reshape(3 * DEPTH, D), inp["final_norm"][None]])),
        "gate_bias": columns(inp["b_gate"]),
        "ws1": f(inp["gmlp_w_s"].transpose(0, 3, 1, 2)),
        "rows1": f(np.broadcast_to(np.stack([inp["gmlp_ln_g"], inp["gmlp_ln_b"],
                                             inp["gmlp_b_s"].reshape(DEPTH, W)], 1)[:, None],
                                   (DEPTH, P, 3, W))),
    }
    w = inp["w_in_2"]
    cut = np.cumsum([W, W, W, W, DN_H, DN_H, W, W, W])
    dq, dk, dv, z, b, a, bq, bk, bv = np.split(w, cut[:-1], axis=-1)
    taps_of = lambda c: f(np.moveaxis(c.reshape(DEPTH, c.shape[1], -1, P), (3, 0, 2, 1), (0, 1, 2, 3)))
    cq, ck, cv = np.split(inp["dn_conv_2"], 3, axis=-1)
    out.update({
        "in2": slots(np.concatenate([dk, dq, dv, bq, bk, bv, z], axis=-1), KC, 256),
        "small2": f(np.concatenate([b, a], axis=-1).reshape(DEPTH, KC, P, 2 * DN_H).transpose(2, 0, 1, 3)),
        "out2": slots(np.concatenate([inp["w_out_2"][:, W:], inp["w_out_2"][:, :W]], axis=1), KC, 256),
        "gu3": gate_up(inp["ffn_up_2"]), "down3": down(inp["ffn_down_2"]),
        "gains2": columns(np.concatenate([np.stack([inp["pre_mix_norm_2"], inp["post_mix_norm_2"],
                                                    inp["pre_ffn_norm_2"], inp["post_ffn_norm_2"]], 1)
                                          .reshape(4 * DEPTH, D), inp["post_ffn_norm_2"][-1:]])),
        "conv_w": taps_of(np.concatenate([ck, cq, cv], axis=-1)),
        "up_w": taps_of(inp["ffn_conv_2"]),
        "up_b": columns(inp["ffn_conv_bias_2"]),
        "decay_rows": f(np.broadcast_to(np.stack([inp["dn_dt_bias_2"], inp["dn_a_log_2"]], 1)[None],
                                        (P, DEPTH, 2, DN_H))),
        "dn_gain": columns(inp["dn_out_norm_2"]),
    })
    out.update(tables())
    return out


def tables():
    f = lambda a: np.ascontiguousarray(np.asarray(a, np.float32))

    def angles(theta, dim):
        inv = np.float32(theta) ** (-np.arange(0, dim, 2, dtype=np.float32) / np.float32(dim))
        ang = np.arange(T, dtype=np.float32)[:, None] * inv[None, :]
        return np.cos(ang), np.sin(ang)

    by_tile = lambda a: f(a.reshape(NT, P, -1).transpose(1, 0, 2))
    c, s = angles(10000.0, HD)
    p = np.arange(P)
    q = P + p[:, None]
    dist = q - np.arange(T)[None, :]
    c2, s2 = angles(500000.0, ROPE2)
    count = sum((dist >= 0) & (dist % dil == 0) & (dist <= window) for window, dil in DILATIONS)
    return {
        "ones_d": f(np.full((P, P), 1.0 / D)), "ident": f(np.eye(P)), "eps": f(np.full((P, 2), [EPS, P * EPS ** 2])),
        "ones_q": f(np.full((P, P), EPS * P ** 2)),
        "cos1": by_tile(np.concatenate([c, c], 1)), "sin1": by_tile(np.concatenate([-s, s], 1)),
        "causal": f(np.where(dist >= 0, 0.0, NEG)),
        "ones": f(np.ones((P, P))),
        "cos2": by_tile(np.concatenate([c2, c2, np.ones((T, HD - ROPE2), np.float32)], 1)),
        "sin2": by_tile(np.concatenate([-s2, s2], 1)),
        "reach": f(np.where(count > 0, np.log(np.maximum(count, 1)), NEG)),
        "mask_t": f(np.where(p[:, None] <= p[None, :], 0.0, NEG)),
        "strict": f(p[:, None] < p[None, :]),
        "level_m": f(np.stack([(p[None, :] // b % 2 == 1) & (p[:, None] // b == p[None, :] // b - 1)
                               for b in 2 ** np.arange(LEVELS)], 1)),
        "tri_ts": f(p[:, None] <= p[None, :]),
    }


def kernel(**inputs):
    import concourse.bacc as _bacc
    from concourse.bass_utils import run_bass_kernel_spmd as _run

    nc = _bacc.Bacc("TRN2", target_bir_lowering=False, num_devices=1)
    arrays, io = {}, {}
    for name, a in lay_out({name: np.asarray(a) for name, a in inputs.items()}).items():
        arrays[f"in_{name}_dram"] = a
        io[name] = nc.dram_tensor(f"in_{name}_dram", a.shape, mybir.dt.from_np(a.dtype), kind="ExternalInput").ap()
    io["out"] = nc.dram_tensor("out_dram", (P, KC, T), F32, kind="ExternalOutput").ap()
    with ExitStack() as ctx:
        program(nc, io, ctx)
    r = _run(nc, [arrays], core_ids=[0])
    return np.ascontiguousarray(r.results[0]["out_dram"].transpose(1, 0, 2).reshape(D, T).T)[None]
```
